# Optimizing a Trainium2 kernel written in Bass

```python
import jax, jax.numpy as jnp
from jax import lax
import numpy as np
import jax
import jax.numpy as jnp

D_MODEL = 1024
BATCH = 1
SEQ = 512
DEPTH = 2

D_MIX = D_MODEL
ATT_HEADS = 8
ATT_HEAD_DIM = 64
ATT_WIDTH = ATT_HEADS * ATT_HEAD_DIM
MLSTM_HEADS = 4
MLSTM_HEAD_DIM = 128
MLSTM_WIDTH = MLSTM_HEADS * MLSTM_HEAD_DIM
Q_RANK = 256
N_IDX_HEADS = 8
IDX_DIM = 64
INDEX_TOPK = 256
Q_BLOCK = 128
MLSTM_CHUNK = 64
CONV_WIDTH = 4
FFN_HIDDEN = -(-8 * D_MODEL // (3 * 256)) * 256
ROPE_THETA = 10000.0
EPS = 1e-6
IN_SPLITS = (Q_RANK, ATT_WIDTH, ATT_WIDTH, IDX_DIM, N_IDX_HEADS,
             MLSTM_WIDTH, MLSTM_WIDTH, MLSTM_WIDTH, MLSTM_WIDTH, MLSTM_HEADS, MLSTM_HEADS)
IN_COLS = sum(IN_SPLITS)


def rms_norm(x, w):
    x32 = x.astype(jnp.float32)
    y = x32 * lax.rsqrt(jnp.mean(x32 * x32, axis=-1, keepdims=True) + EPS)
    return (y * w.astype(jnp.float32)).astype(x.dtype)

def rope(x, positions):
    d = x.shape[-1]
    inv_freq = ROPE_THETA ** (-jnp.arange(0, d, 2, dtype=jnp.float32) / d)
    ang = positions.astype(jnp.float32)[..., None] * inv_freq
    cos = jnp.cos(ang)[:, :, None, :]
    sin = jnp.sin(ang)[:, :, None, :]
    x1, x2 = jnp.split(x.astype(jnp.float32), 2, axis=-1)
    return jnp.concatenate([x1 * cos - x2 * sin, x2 * cos + x1 * sin], axis=-1).astype(x.dtype)

def causal_dwconv(x, w, b):
    ch = x.shape[-1]
    y = lax.conv_general_dilated(x, w[:, None, :].astype(x.dtype), window_strides=(1,),
                                 padding=[(CONV_WIDTH - 1, 0)],
                                 dimension_numbers=('NWC', 'WIO', 'NWC'),
                                 feature_group_count=ch)
    return y + b.astype(x.dtype)

def dsa_attention(q, k, v, q_idx, k_idx, w_idx):
    def one_seq(args):
        q_, k_, v_, qi_, ki_, wi_ = args
        seq = q_.shape[0]
        n_sel = min(INDEX_TOPK, seq // 4)
        key_pos = jnp.arange(seq)
        ki32 = ki_.astype(jnp.float32)
        scale = ATT_HEAD_DIM ** -0.5

        def block(i):
            start = i * Q_BLOCK
            t = start + jnp.arange(Q_BLOCK)
            qb = lax.dynamic_slice_in_dim(q_, start, Q_BLOCK, 0)
            qib = lax.dynamic_slice_in_dim(qi_, start, Q_BLOCK, 0).astype(jnp.float32)
            wib = lax.dynamic_slice_in_dim(wi_, start, Q_BLOCK, 0).astype(jnp.float32)
            idx_logits = jnp.einsum('thd,sd->ths', qib, ki32)
            idx_score = jnp.einsum('ths,th->ts', jax.nn.relu(idx_logits), wib)
            idx_score = jnp.where(key_pos[None, :] <= t[:, None], idx_score, -jnp.inf)
            _, sel = lax.top_k(idx_score, n_sel)
            valid = sel <= t[:, None]
            k_sel = k_[sel]
            v_sel = v_[sel]
            logits = jnp.einsum('thd,tkhd->thk', qb, k_sel).astype(jnp.float32) * scale
            logits = jnp.where(valid[:, None, :], logits, -jnp.inf)
            p = jax.nn.softmax(logits, axis=-1)
            return jnp.einsum('thk,tkhd->thd', p.astype(v_.dtype), v_sel)

        out = lax.map(block, jnp.arange(seq // Q_BLOCK))
        return out.reshape((seq,) + q_.shape[1:])

    return lax.map(one_seq, (q, k, v, q_idx, k_idx, w_idx))

def mlstm_chunkwise(q, k, v, ig, lf):
    b_, nh, seq, dk = q.shape
    dv = v.shape[-1]
    nc = seq // MLSTM_CHUNK

    def chunks(a):
        return jnp.moveaxis(a.reshape(a.shape[:2] + (nc, MLSTM_CHUNK) + a.shape[3:]), 2, 0)

    qc, kc, vc, igc, lfc = chunks(q), chunks(k), chunks(v), chunks(ig), chunks(lf)
    bc = jnp.cumsum(lfc, axis=-1)
    causal = jnp.tril(jnp.ones((MLSTM_CHUNK, MLSTM_CHUNK), dtype=bool))

    def step(carry, inp):
        c_s, n_s, m_s = carry
        q_, k_, v_, ig_, b_c = inp
        d_mat = b_c[..., :, None] - b_c[..., None, :] + ig_[..., None, :]
        d_mat = jnp.where(causal, d_mat, -jnp.inf)
        inter = b_c + m_s[..., None]
        m_row = jnp.maximum(inter, jnp.max(d_mat, axis=-1))
        w_intra = jnp.exp(d_mat - m_row[..., None])
        w_inter = jnp.exp(inter - m_row)
        s_mat = jnp.einsum('bhtd,bhsd->bhts', q_, k_) * w_intra
        num = (jnp.einsum('bhts,bhsv->bhtv', s_mat, v_)
               + w_inter[..., None] * jnp.einsum('bhtd,bhdv->bhtv', q_, c_s))
        den = jnp.sum(s_mat, axis=-1) + w_inter * jnp.einsum('bhtd,bhd->bht', q_, n_s)
        h = num / jnp.maximum(jnp.abs(den), jnp.exp(-m_row))[..., None]
        total = b_c[..., -1]
        w_log = total[..., None] - b_c + ig_
        m_new = jnp.maximum(total + m_s, jnp.max(w_log, axis=-1))
        decay = jnp.exp(total + m_s - m_new)
        w_state = jnp.exp(w_log - m_new[..., None])
        c_new = decay[..., None, None] * c_s + jnp.einsum('bhs,bhsd,bhsv->bhdv', w_state, k_, v_)
        n_new = decay[..., None] * n_s + jnp.einsum('bhs,bhsd->bhd', w_state, k_)
        return (c_new, n_new, m_new), h

    init = (jnp.zeros((b_, nh, dk, dv), jnp.float32), jnp.zeros((b_, nh, dk), jnp.float32),
            jnp.zeros((b_, nh), jnp.float32))
    _, hs = lax.scan(step, init, (qc, kc, vc, igc, bc))
    return jnp.moveaxis(hs, 0, 2).reshape(b_, nh, seq, dv)

def hybrid_mixer(h, positions, w_in, q_latent_norm, w_q_up, w_qidx_up, conv_w, conv_b,
                 b_igate, b_fgate, attn_out_norm, mlstm_out_norm, w_out):
    b_, seq, _ = h.shape
    split_pts = [int(s) for s in np.cumsum(IN_SPLITS)[:-1]]
    (cq, k_att, v_att, k_idx, w_idx,
     q_m, k_m, v_m, o_m, i_m, f_m) = jnp.split(h @ w_in, split_pts, axis=-1)

    cq = rms_norm(cq, q_latent_norm)
    q = rope((cq @ w_q_up).reshape(b_, seq, ATT_HEADS, ATT_HEAD_DIM), positions)
    q_idx = rope((cq @ w_qidx_up).reshape(b_, seq, N_IDX_HEADS, IDX_DIM), positions)
    k = rope(k_att.reshape(b_, seq, ATT_HEADS, ATT_HEAD_DIM), positions)
    v = v_att.reshape(b_, seq, ATT_HEADS, ATT_HEAD_DIM)
    k_idx = rope(k_idx[:, :, None, :], positions)[:, :, 0, :]
    w_idx = w_idx * (N_IDX_HEADS * IDX_DIM) ** -0.5
    att = dsa_attention(q, k, v, q_idx, k_idx, w_idx)
    att = rms_norm(att, attn_out_norm.reshape(ATT_HEADS, ATT_HEAD_DIM)).reshape(b_, seq, ATT_WIDTH)

    qk = jax.nn.silu(causal_dwconv(jnp.concatenate([q_m, k_m], axis=-1), conv_w, conv_b))
    q_m, k_m = jnp.split(qk, 2, axis=-1)

    def heads(a):
        return a.reshape(b_, seq, MLSTM_HEADS, MLSTM_HEAD_DIM).transpose(0, 2, 1, 3).astype(jnp.float32)

    ig = (i_m + b_igate).astype(jnp.float32).transpose(0, 2, 1)
    lf = jax.nn.log_sigmoid((f_m + b_fgate).astype(jnp.float32)).transpose(0, 2, 1)
    hm = mlstm_chunkwise(heads(q_m) * MLSTM_HEAD_DIM ** -0.5, heads(k_m), heads(v_m), ig, lf)
    hm = hm.transpose(0, 2, 1, 3).astype(h.dtype)
    hm = rms_norm(hm, mlstm_out_norm.reshape(MLSTM_HEADS, MLSTM_HEAD_DIM))
    hm = (jax.nn.sigmoid(o_m).reshape(b_, seq, MLSTM_HEADS, MLSTM_HEAD_DIM) * hm).reshape(b_, seq, MLSTM_WIDTH)

    return jnp.concatenate([att, hm], axis=-1) @ w_out

def swiglu(h, w_gate_up, w_down):
    g, u = jnp.split(h @ w_gate_up, 2, axis=-1)
    return (jax.nn.silu(g) * u) @ w_down

def first_inputs(seed: int = 0) -> dict:
    key = jax.random.key(seed)
    ks = jax.random.split(key, 24)
    L = DEPTH

    def nrm(k, shape, scale):
        return jax.random.normal(k, shape, jnp.float32) * scale

    def gain(k, shape):
        return 1.0 + 0.05 * jax.random.normal(k, shape, jnp.float32)

    x = nrm(ks[0], (BATCH, SEQ, D_MODEL), 1.0)
    c = nrm(ks[1], (BATCH, D_MODEL), 1.0)
    offsets = jax.random.randint(ks[2], (BATCH, 1), 0, 1024, dtype=jnp.int32)
    positions = (offsets + jnp.arange(SEQ, dtype=jnp.int32)[None, :]).astype(jnp.int32)
    b_fgate = (jnp.linspace(3.0, 6.0, MLSTM_HEADS, dtype=jnp.float32)[None, :]
               + nrm(ks[14], (L, MLSTM_HEADS), 0.1))
    return {
        "x": x,
        "c": c,
        "positions": positions,
        "w_mod": nrm(ks[3], (L, D_MODEL, 6 * D_MODEL), 0.5 * D_MODEL ** -0.5),
        "b_mod": nrm(ks[4], (L, 6 * D_MODEL), 0.01),
        "mix_norm_pre": gain(ks[5], (L, D_MODEL)),
        "mix_norm_post": gain(ks[6], (L, D_MODEL)),
        "w_in": nrm(ks[7], (L, D_MODEL, IN_COLS), D_MODEL ** -0.5),
        "q_latent_norm": gain(ks[8], (L, Q_RANK)),
        "w_q_up": nrm(ks[9], (L, Q_RANK, ATT_WIDTH), Q_RANK ** -0.5),
        "w_qidx_up": nrm(ks[10], (L, Q_RANK, N_IDX_HEADS * IDX_DIM), Q_RANK ** -0.5),
        "conv_w": nrm(ks[11], (L, CONV_WIDTH, 2 * MLSTM_WIDTH), CONV_WIDTH ** -0.5),
        "conv_b": nrm(ks[12], (L, 2 * MLSTM_WIDTH), 0.01),
        "b_igate": nrm(ks[13], (L, MLSTM_HEADS), 0.1),
        "b_fgate": b_fgate,
        "attn_out_norm": gain(ks[15], (L, ATT_WIDTH)),
        "mlstm_out_norm": gain(ks[16], (L, MLSTM_WIDTH)),
        "w_out": nrm(ks[17], (L, D_MIX, D_MODEL), D_MIX ** -0.5),
        "ffn_norm_pre": gain(ks[18], (L, D_MODEL)),
        "ffn_norm_post": gain(ks[19], (L, D_MODEL)),
        "w_gate_up": nrm(ks[20], (L, D_MODEL, 2 * FFN_HIDDEN), D_MODEL ** -0.5),
        "w_down": nrm(ks[21], (L, FFN_HIDDEN, D_MODEL), FFN_HIDDEN ** -0.5),
    }

def first_block(x, c, positions, w_mod, b_mod, mix_norm_pre, mix_norm_post, w_in, q_latent_norm,
              w_q_up, w_qidx_up, conv_w, conv_b, b_igate, b_fgate, attn_out_norm, mlstm_out_norm,
              w_out, ffn_norm_pre, ffn_norm_post, w_gate_up, w_down):
    c_act = jax.nn.silu(c)
    for l in range(DEPTH):
        mod = c_act @ w_mod[l] + b_mod[l]
        sh_m, sc_m, g_m, sh_f, sc_f, g_f = jnp.split(mod, 6, axis=-1)
        h = rms_norm(x, mix_norm_pre[l]) * (1.0 + sc_m[:, None, :]) + sh_m[:, None, :]
        y = hybrid_mixer(h, positions, w_in[l], q_latent_norm[l], w_q_up[l], w_qidx_up[l],
                         conv_w[l], conv_b[l], b_igate[l], b_fgate[l], attn_out_norm[l],
                         mlstm_out_norm[l], w_out[l])
        x = x + g_m[:, None, :] * rms_norm(y, mix_norm_post[l])
        h = rms_norm(x, ffn_norm_pre[l]) * (1.0 + sc_f[:, None, :]) + sh_f[:, None, :]
        y = swiglu(h, w_gate_up[l], w_down[l])
        x = x + g_f[:, None, :] * rms_norm(y, ffn_norm_post[l])
    return x


HEAD_DIM = 64
NSA_HEADS = 8
NSA_KV_HEADS = 2
NSA_GROUP = NSA_HEADS // NSA_KV_HEADS
SB_HEADS = 8
CMP_BLOCK = 32
CMP_STRIDE = 16
SLC_BLOCK = 64
SLC_TOPK = 16
WINDOW = 512
WIN_QBLOCK = 128
SLC_QCHUNK = 64
SB_QBLOCK = 128
D_FF = 2816
CONV_WIDTH_2 = 3
RMS_EPS = 1e-6
NEG_INF = -1e30
FORCE_BONUS = 1e4

NSA_WIDTH = NSA_HEADS * HEAD_DIM
KV_WIDTH = NSA_KV_HEADS * HEAD_DIM
SB_WIDTH = SB_HEADS * HEAD_DIM
IN_SPLITS_2 = (NSA_WIDTH, 6 * KV_WIDTH, 3 * NSA_HEADS, 3 * SB_WIDTH, 2 * D_MODEL)
IN_WIDTH = sum(IN_SPLITS_2)


def rms_norm_2(x, gain):
    xf = x.astype(jnp.float32)
    y = xf * lax.rsqrt(jnp.mean(xf * xf, axis=-1, keepdims=True) + RMS_EPS)
    return y.astype(x.dtype) * gain

def rope_2(x, positions):
    half = x.shape[-1] // 2
    inv_freq = ROPE_THETA ** (-jnp.arange(half, dtype=jnp.float32) / half)
    ang = positions.astype(jnp.float32)[:, :, None] * inv_freq
    cos = jnp.cos(ang)[:, :, None, :]
    sin = jnp.sin(ang)[:, :, None, :]
    xf = x.astype(jnp.float32)
    x1, x2 = xf[..., :half], xf[..., half:]
    return jnp.concatenate([x1 * cos - x2 * sin, x2 * cos + x1 * sin], axis=-1).astype(x.dtype)

def compress_blocks(k, pe, w1, b1, w2):
    B, T, Hkv, hd = k.shape
    n_cmp = (T - CMP_BLOCK) // CMP_STRIDE + 1
    idx = np.arange(n_cmp)[:, None] * CMP_STRIDE + np.arange(CMP_BLOCK)[None, :]
    blocks = k[:, idx] + pe[None, None, :, None, :]
    flat = jnp.transpose(blocks, (0, 1, 3, 2, 4)).reshape(B, n_cmp, Hkv, CMP_BLOCK * hd)
    return jax.nn.gelu(flat @ w1 + b1, approximate=True) @ w2

def nsa_attention(q, k_cmp, v_cmp, k_slc, v_slc, k_win, v_win, gate_logits,
                  ck_pe, ck_w1, ck_b1, ck_w2, cv_pe, cv_w1, cv_b1, cv_w2):
    B, T, H, hd = q.shape
    scale = hd ** -0.5
    qg = q.reshape(B, T, NSA_KV_HEADS, NSA_GROUP, hd)
    t_idx = jnp.arange(T)

    kc = compress_blocks(k_cmp, ck_pe, ck_w1, ck_b1, ck_w2)
    vc = compress_blocks(v_cmp, cv_pe, cv_w1, cv_b1, cv_w2)
    n_cmp = kc.shape[1]
    cmp_end = jnp.arange(n_cmp) * CMP_STRIDE + CMP_BLOCK - 1
    cmp_mask = cmp_end[None, :] <= t_idx[:, None]
    s = jnp.einsum('bthgd,bnhd->bhgtn', qg, kc).astype(jnp.float32) * scale
    p_cmp = jax.nn.softmax(jnp.where(cmp_mask, s, NEG_INF), axis=-1) * cmp_mask
    o_cmp = jnp.einsum('bhgtn,bnhd->bthgd', p_cmp.astype(vc.dtype), vc)

    n_slc = T // SLC_BLOCK
    top_n = min(SLC_TOPK, n_slc)
    ci = np.arange(n_cmp)[:, None] * CMP_STRIDE
    sj = np.arange(n_slc)[None, :] * SLC_BLOCK
    overlap = ((ci < sj + SLC_BLOCK) & (sj < ci + CMP_BLOCK)).astype(np.float32)
    p_slc = jnp.einsum('bhtn,nj->bhtj', p_cmp.sum(axis=2), jnp.asarray(overlap))
    blk = jnp.arange(n_slc)
    cur = t_idx // SLC_BLOCK
    blk_valid = blk[None, :] * SLC_BLOCK <= t_idx[:, None]
    forced = (blk[None, :] == 0) | (blk[None, :] == cur[:, None]) | (blk[None, :] == cur[:, None] - 1)
    score = jnp.where(blk_valid, p_slc + jnp.where(forced, FORCE_BONUS, 0.0), -1.0)
    top_score, top_idx = lax.top_k(score, top_n)
    top_valid = top_score >= 0.0

    ks_blk = jnp.transpose(k_slc.reshape(B, n_slc, SLC_BLOCK, NSA_KV_HEADS, hd), (0, 3, 1, 2, 4))
    vs_blk = jnp.transpose(v_slc.reshape(B, n_slc, SLC_BLOCK, NSA_KV_HEADS, hd), (0, 3, 1, 2, 4))
    b_ix = jnp.arange(B)[:, None, None, None]
    h_ix = jnp.arange(NSA_KV_HEADS)[None, :, None, None]
    n_chunk = T // SLC_QCHUNK

    def slc_chunk(args):
        qc, idx_c, ok_c, t_c = args
        kg = ks_blk[b_ix, h_ix, idx_c]
        vg = vs_blk[b_ix, h_ix, idx_c]
        tok = idx_c[..., None] * SLC_BLOCK + jnp.arange(SLC_BLOCK)
        mask = ok_c[..., None] & (tok <= t_c[None, None, :, None, None])
        sc = jnp.einsum('bqhgd,bhqnld->bhgqnl', qc, kg).astype(jnp.float32) * scale
        sc = jnp.where(mask[:, :, None], sc, NEG_INF)
        p = jax.nn.softmax(sc.reshape(*sc.shape[:4], -1), axis=-1).reshape(sc.shape)
        return jnp.einsum('bhgqnl,bhqnld->bqhgd', p.astype(vg.dtype), vg)

    xs = (jnp.swapaxes(qg.reshape(B, n_chunk, SLC_QCHUNK, NSA_KV_HEADS, NSA_GROUP, hd), 0, 1),
          jnp.moveaxis(top_idx.reshape(B, NSA_KV_HEADS, n_chunk, SLC_QCHUNK, top_n), 2, 0),
          jnp.moveaxis(top_valid.reshape(B, NSA_KV_HEADS, n_chunk, SLC_QCHUNK, top_n), 2, 0),
          t_idx.reshape(n_chunk, SLC_QCHUNK))
    o_slc = jnp.swapaxes(lax.map(slc_chunk, xs), 0, 1).reshape(B, T, NSA_KV_HEADS, NSA_GROUP, hd)

    n_wblk = T // WIN_QBLOCK
    span = WINDOW + WIN_QBLOCK
    kw_pad = jnp.pad(k_win, ((0, 0), (WINDOW, 0), (0, 0), (0, 0)))
    vw_pad = jnp.pad(v_win, ((0, 0), (WINDOW, 0), (0, 0), (0, 0)))

    def win_block(i):
        start = i * WIN_QBLOCK
        qb = lax.dynamic_slice_in_dim(qg, start, WIN_QBLOCK, axis=1)
        kb = lax.dynamic_slice_in_dim(kw_pad, start, span, axis=1)
        vb = lax.dynamic_slice_in_dim(vw_pad, start, span, axis=1)
        q_pos = start + jnp.arange(WIN_QBLOCK)
        k_pos = start - WINDOW + jnp.arange(span)
        diff = q_pos[:, None] - k_pos[None, :]
        mask = (diff >= 0) & (diff < WINDOW) & (k_pos[None, :] >= 0)
        sc = jnp.einsum('bqhgd,bkhd->bhgqk', qb, kb).astype(jnp.float32) * scale
        p = jax.nn.softmax(jnp.where(mask, sc, NEG_INF), axis=-1)
        return jnp.einsum('bhgqk,bkhd->bqhgd', p.astype(vb.dtype), vb)

    o_win = jnp.swapaxes(lax.map(win_block, jnp.arange(n_wblk)), 0, 1).reshape(B, T, NSA_KV_HEADS, NSA_GROUP, hd)

    g = jax.nn.sigmoid(gate_logits.reshape(B, T, NSA_KV_HEADS, NSA_GROUP, 3))
    o = g[..., 0:1] * o_cmp + g[..., 1:2] * o_slc + g[..., 2:3] * o_win
    return o.reshape(B, T, H * hd)

def stick_breaking_attention(q, k, v):
    B, T, H, hd = q.shape
    scale = hd ** -0.5
    outs = []
    for i in range(T // SB_QBLOCK):
        q0, q1 = i * SB_QBLOCK, (i + 1) * SB_QBLOCK
        z = jnp.einsum('bqhd,bkhd->bhqk', q[:, q0:q1], k[:, :q1]).astype(jnp.float32) * scale
        q_pos = jnp.arange(q0, q1)
        k_pos = jnp.arange(q1)
        strict = k_pos[None, :] < q_pos[:, None]
        log_1m = jnp.where(strict, -jax.nn.softplus(z), 0.0)
        later = lax.cumsum(log_1m, axis=3, reverse=True) - log_1m
        w = jnp.where(strict, jnp.exp(jax.nn.log_sigmoid(z) + later), 0.0)
        outs.append(jnp.einsum('bhqk,bkhd->bqhd', w.astype(v.dtype), v[:, :q1]))
    return jnp.concatenate(outs, axis=1)

def hybrid_mixer_2(h, positions, w_in, ck_pe, ck_w1, ck_b1, ck_w2, cv_pe, cv_w1, cv_b1, cv_w2,
                 w_proj_nsa, w_proj_sb, w_out):
    B, T, _ = h.shape
    cuts = np.cumsum(IN_SPLITS_2)[:-1].tolist()
    q_nsa, kv_nsa, g_nsa, qkv_sb, g_merge = jnp.split(h @ w_in, cuts, axis=-1)
    q_nsa = rope_2(q_nsa.reshape(B, T, NSA_HEADS, HEAD_DIM), positions)
    kv = kv_nsa.reshape(B, T, 6, NSA_KV_HEADS, HEAD_DIM)
    k_cmp = rope_2(kv[:, :, 0], positions)
    v_cmp = kv[:, :, 1]
    k_slc = rope_2(kv[:, :, 2], positions)
    v_slc = kv[:, :, 3]
    k_win = rope_2(kv[:, :, 4], positions)
    v_win = kv[:, :, 5]
    o_nsa = nsa_attention(q_nsa, k_cmp, v_cmp, k_slc, v_slc, k_win, v_win, g_nsa,
                          ck_pe, ck_w1, ck_b1, ck_w2, cv_pe, cv_w1, cv_b1, cv_w2)
    qkv = qkv_sb.reshape(B, T, 3, SB_HEADS, HEAD_DIM)
    o_sb = stick_breaking_attention(qkv[:, :, 0], qkv[:, :, 1], qkv[:, :, 2]).reshape(B, T, SB_WIDTH)
    g_a, g_b = jnp.split(jax.nn.sigmoid(g_merge), 2, axis=-1)
    y = g_a * (o_nsa @ w_proj_nsa) + g_b * (o_sb @ w_proj_sb)
    return y @ w_out

def conv_ffn(h, w_up, conv_w, conv_b, w_down):
    u = h @ w_up
    c = u.shape[-1]
    u = lax.conv_general_dilated(u, conv_w[:, None, :], window_strides=(1,),
                                 padding=[(CONV_WIDTH_2 - 1, 0)],
                                 dimension_numbers=('NWC', 'WIO', 'NWC'),
                                 feature_group_count=c) + conv_b
    gate, up = jnp.split(u, 2, axis=-1)
    return (jax.nn.gelu(gate, approximate=True) * up) @ w_down

def second_inputs(seed: int = 0) -> dict:
    key = jax.random.key(seed)
    ks = jax.random.split(key, 24)
    f32 = jnp.float32

    def nrm(k, shape, scale):
        return jax.random.normal(k, shape, f32) * scale

    def gain(k):
        return 1.0 + 0.02 * jax.random.normal(k, (DEPTH, D_MODEL), f32)

    cmp_in = CMP_BLOCK * HEAD_DIM
    return {
        'x': nrm(ks[0], (BATCH, SEQ, D_MODEL), 1.0),
        'positions': jnp.broadcast_to(jnp.arange(SEQ, dtype=jnp.int32), (BATCH, SEQ)),
        'g_pre_mix': gain(ks[1]),
        'w_in': nrm(ks[2], (DEPTH, D_MODEL, IN_WIDTH), D_MODEL ** -0.5),
        'ck_pe': nrm(ks[3], (DEPTH, CMP_BLOCK, HEAD_DIM), 0.02),
        'ck_w1': nrm(ks[4], (DEPTH, cmp_in, HEAD_DIM), cmp_in ** -0.5),
        'ck_b1': nrm(ks[5], (DEPTH, HEAD_DIM), 0.01),
        'ck_w2': nrm(ks[6], (DEPTH, HEAD_DIM, HEAD_DIM), HEAD_DIM ** -0.5),
        'cv_pe': nrm(ks[7], (DEPTH, CMP_BLOCK, HEAD_DIM), 0.02),
        'cv_w1': nrm(ks[8], (DEPTH, cmp_in, HEAD_DIM), cmp_in ** -0.5),
        'cv_b1': nrm(ks[9], (DEPTH, HEAD_DIM), 0.01),
        'cv_w2': nrm(ks[10], (DEPTH, HEAD_DIM, HEAD_DIM), HEAD_DIM ** -0.5),
        'w_proj_nsa': nrm(ks[11], (DEPTH, NSA_WIDTH, D_MODEL), NSA_WIDTH ** -0.5),
        'w_proj_sb': nrm(ks[12], (DEPTH, SB_WIDTH, D_MODEL), SB_WIDTH ** -0.5),
        'w_out': nrm(ks[13], (DEPTH, D_MODEL, D_MODEL), D_MODEL ** -0.5),
        'g_post_mix': gain(ks[14]),
        'g_pre_ffn': gain(ks[15]),
        'w_up': nrm(ks[16], (DEPTH, D_MODEL, 2 * D_FF), D_MODEL ** -0.5),
        'conv_w': nrm(ks[17], (DEPTH, CONV_WIDTH_2, 2 * D_FF), CONV_WIDTH_2 ** -0.5),
        'conv_b': nrm(ks[18], (DEPTH, 2 * D_FF), 0.01),
        'w_down': nrm(ks[19], (DEPTH, D_FF, D_MODEL), D_FF ** -0.5),
        'g_post_ffn': gain(ks[20]),
    }

def second_block(x, positions, g_pre_mix, w_in, ck_pe, ck_w1, ck_b1, ck_w2, cv_pe, cv_w1, cv_b1, cv_w2,
              w_proj_nsa, w_proj_sb, w_out, g_post_mix, g_pre_ffn, w_up, conv_w, conv_b, w_down, g_post_ffn):
    for l in range(DEPTH):
        h = rms_norm_2(x, g_pre_mix[l])
        m = hybrid_mixer_2(h, positions, w_in[l], ck_pe[l], ck_w1[l], ck_b1[l], ck_w2[l],
                         cv_pe[l], cv_w1[l], cv_b1[l], cv_w2[l], w_proj_nsa[l], w_proj_sb[l], w_out[l])
        x = x + rms_norm_2(m, g_post_mix[l])
        h = rms_norm_2(x, g_pre_ffn[l])
        f = conv_ffn(h, w_up[l], conv_w[l], conv_b[l], w_down[l])
        x = x + rms_norm_2(f, g_post_ffn[l])
    return x


def setup_inputs(seed=0):
    out = dict(first_inputs(seed))
    for name, value in second_inputs(seed + 1).items():
        if name != "x":
            out[name + "_2"] = value
    return out


def reference(
    x, c, positions, w_mod, b_mod, mix_norm_pre, mix_norm_post, w_in, q_latent_norm, w_q_up,
    w_qidx_up, conv_w, conv_b, b_igate, b_fgate, attn_out_norm, mlstm_out_norm, w_out,
    ffn_norm_pre, ffn_norm_post, w_gate_up, w_down, positions_2, g_pre_mix_2, w_in_2, ck_pe_2,
    ck_w1_2, ck_b1_2, ck_w2_2, cv_pe_2, cv_w1_2, cv_b1_2, cv_w2_2, w_proj_nsa_2, w_proj_sb_2,
    w_out_2, g_post_mix_2, g_pre_ffn_2, w_up_2, conv_w_2, conv_b_2, w_down_2, g_post_ffn_2,
):
    x = first_block(
        x, c, positions, w_mod, b_mod, mix_norm_pre, mix_norm_post, w_in, q_latent_norm, w_q_up,
        w_qidx_up, conv_w, conv_b, b_igate, b_fgate, attn_out_norm, mlstm_out_norm, w_out,
        ffn_norm_pre, ffn_norm_post, w_gate_up, w_down,
    )
    return second_block(
        x, positions_2, g_pre_mix_2, w_in_2, ck_pe_2, ck_w1_2, ck_b1_2, ck_w2_2, cv_pe_2,
        cv_w1_2, cv_b1_2, cv_w2_2, w_proj_nsa_2, w_proj_sb_2, w_out_2, g_post_mix_2,
        g_pre_ffn_2, w_up_2, conv_w_2, conv_b_2, w_down_2, g_post_ffn_2,
    )


_drawn_inputs = setup_inputs


def setup_inputs(seed=0):
    import zlib

    import numpy as np

    out = dict(_drawn_inputs(seed))
    spreads = {}
    factors = {'conv_b': 8.0,
     'b_igate': 64.0,
     'mlstm_out_norm': 2.816,
     'ck_pe_2': 34.662,
     'ck_b1_2': 64.0,
     'cv_pe_2': 8.0,
     'cv_b1_2': 8.0,
     'g_post_mix_2': 2.807,
     'g_pre_ffn_2': 2.709,
     'conv_b_2': 5.125,
     'g_post_ffn_2': 3.806}
    for name, (base, spread) in spreads.items():
        noise = np.random.default_rng([zlib.crc32(name.encode()), seed]).standard_normal(out[name].shape)
        drawn = base * np.exp(spread * noise) if base else spread * noise
        out[name] = jnp.asarray(drawn.astype(out[name].dtype))
    for name, factor in factors.items():
        out[name] = (out[name] * factor).astype(out[name].dtype)
    return out
```

```python
from contextlib import ExitStack, contextmanager

import concourse.bass as bass
import numpy as np
from concourse import mybir

F32 = mybir.dt.float32
F32R = mybir.dt.float32r
I32 = mybir.dt.int32
ALU = mybir.AluOpType
ACT = mybir.ActivationFunctionType
AX_X = mybir.AxisListType.X

P = 128
T = 512
D = 1024
KD = D // P
NT = T // P
LAYERS = 2
STREAM_SEM, FIRST_SEM = 193, 200
FF = 2816
KF = FF // P
SLOT = 1024
RING = 4
EPS = 1e-6
HEADS = 8
HD = 64
MH = 4
MD = 128
QR = 256
TOPK = T // 4
NCMP = (T - 32) // 16 + 1
CB = 32
NEG = -1e30
TAKEN = -3e38

IN1, GU, DN, OUT = 30, 2 * KF, 3 * KD, KD
IN2, PROJ = 48, 8
SL1 = IN1 + OUT + GU + DN
SL2 = IN2 + PROJ + OUT + GU + DN

C_ID, C_ROT, C_CAUSAL, C_ONES, C_SEL, C_FREQ, C_CMP = 0, 128, 256, 768, 896, 1408, 1409
C_COLS = 1409 + NT * 32

A_PRE, A_POST, A_FPRE, A_FPOST, A_BMOD, A_QN, A_CW, A_CB, A_AN, A_MN, A_BI, A_BF = (
    0, 8, 16, 24, 32, 80, 82, 114, 122, 126, 130, 131)
A_COLS = 132
B_PRE, B_POST, B_FPRE, B_FPOST, B_CW, B_CB, B_B1K, B_B1V, B_PEK, B_PEV, B_W2K, B_W2V = (
    0, 8, 16, 24, 32, 164, 208, 209, 210, 242, 274, 402)
B_COLS = 530


@contextmanager
def phase(nc, *names, run_ends=False):
    with ExitStack() as ctx:
        sems = [ctx.enter_context(nc.semaphore(n, num=FIRST_SEM + k)) for k, n in enumerate(names)]
        with nc.Block() as block:
            yield (block, *sems)
        first = STREAM_SEM if run_ends else FIRST_SEM
        nc.all_engine_barrier(sems_to_clear=range(first, FIRST_SEM + len(names)))


class Arena:

    def __init__(self, nc, base, size):
        self.nc, self.at, self.end = nc, base, base + size

    def __call__(self, name, shape, dt=F32):
        size = 4 * int(np.prod(shape[1:]))
        t = self.nc.alloc_sbuf_tensor_at(name, shape, dt, offset=self.at)
        self.at += -(-size // 32) * 32
        assert self.at <= self.end, (name, self.at, self.end)
        return t


class Signal:

    def __init__(self, eng, sem):
        self.eng, self.sem, self.n = eng, sem, 0

    def __call__(self, ins):
        self.n += 1
        ins.then_inc(self.sem, 1)
        self.eng.wait_ge(self.sem, self.n)


class Mem:
    pass


STREAM = ("w_in0", "w_in1", "w_in2", "w_in3", "head_ready", "rest_ready", "slot_done")


class Stream:

    def __init__(self, mem, w, base, total, sems, width=lambda t: SLOT):
        self.m, self.w, self.base, self.total, self.width = mem, w, base, total, width
        self.w_in, (self.head_ready, self.rest_ready, self.slot_done) = sems[:4], sems[4:7]

    def load(self, sp, i, j, width=SLOT):
        n = i * RING + j + self.base
        src = self.w[n if isinstance(n, int) else sp.snap(n)]
        if not (isinstance(i, int) and i == 0):
            sp.wait_ge(self.rest_ready, RING * i + j + 1 - RING)
        sp.dma_start(self.m.raw[:, j, 0:width], src[:, 0:width]).then_inc(self.w_in[j], 16)

    def head(self, act, i, j, width=SLOT):
        act.wait_ge(self.w_in[j], i * 16 + 16)
        if not (isinstance(i, int) and RING * i + j < 2):
            act.wait_ge(self.slot_done, RING * i + j - 1)
        act.activation(self.m.wh[:, j % 2, 0:width], self.m.raw[:, j, 0:width], ACT.Copy)\
           .then_inc(self.head_ready, 1)

    def rest(self, pool, i, j, width=SLOT):
        pool.wait_ge(self.head_ready, RING * i + j + 1)
        pool.tensor_tensor(self.m.wl[:, j % 2, 0:width], self.m.raw[:, j, 0:width],
                           self.m.wh[:, j % 2, 0:width].bitcast(F32), ALU.subtract)\
            .then_inc(self.rest_ready, 1)

    def ready(self, pe, i, j):
        pe.wait_ge(self.rest_ready, RING * i + j + 1)

    def loads(self, sp, t0, t1):
        for t in range(t0, min(t1, self.total)):
            self.load(sp, t // RING, t % RING, self.width(t))

    def heads(self, act, t0, t1):
        for t in range(t0, min(t1, self.total)):
            self.head(act, t // RING, t % RING, self.width(t))

    def rests(self, pool, t0, t1):
        for t in range(t0, min(t1, self.total)):
            self.rest(pool, t // RING, t % RING, self.width(t))


def three_pass(pe, out, wh, wl, xh, xl, start, stop):
    pe.matmul(out, wh, xh, start=start, stop=False)
    pe.matmul(out, wh, xl, start=False, stop=False)
    return pe.matmul(out, wl, xh, start=False, stop=stop)


def build(nc, a, out):
    m = Mem()
    base0 = -(-nc.sbuf_base // 32) * 32
    total = nc.sbuf_usable_end // 32 * 32 - base0
    MIX = KF * T * 4 * 2
    fixed = Arena(nc, base0, total - MIX)
    mix0 = base0 + total - MIX
    m.x = fixed("x", [P, KD, T])
    m.hh = fixed("hh", [P, KD, T], F32R)
    m.hl = fixed("hl", [P, KD, T], F32R)
    y_at = fixed.at
    m.y = fixed("y", [P, KD, T])
    ring_at = fixed.at
    m.raw = fixed("raw", [P, RING, SLOT])
    m.wh = fixed("wh", [P, 2, SLOT], F32R)
    m.wl = fixed("wl", [P, 2, SLOT], F32R)
    RING_BYTES = fixed.at - ring_at
    m.cst = fixed("cst", [P, C_COLS])
    m.pc = fixed("pc", [P, B_COLS])
    m.mod = fixed("mod", [P, 48])
    m.col = fixed("col", [P, 32])
    m.eps = fixed("eps", [P, 2])
    m.cos = fixed("cos", [P, T])
    m.sin = fixed("sin", [P, T])
    m.sq = fixed("sq", [P, 2, T])
    m.acc = fixed("acc", [P, T])
    m.tmp = fixed("tmp", [P, 2, T])

    ident = m.cst[:, C_ID:C_ID + P]
    rot = m.cst[:, C_ROT:C_ROT + P]
    ones = m.cst[:, C_ONES:C_ONES + P]
    freq = m.cst[:, C_FREQ:C_FREQ + 1]

    ps = [nc.alloc_psum_tensor(f"bank{i}", [P, T], F32) for i in range(8)]

    def causal(tb):
        return m.cst[:, C_CAUSAL + (NT - 1 - tb) * P:C_CAUSAL + T]

    with phase(nc, "loaded", "eps_set") as (block, loaded, eps_set):
        @block.sync
        def _(sp):
            sp.dma_start(m.x[:], a["x"]).then_inc(loaded, 16)
            sp.dma_start(m.cst[:], a["cst"]).then_inc(loaded, 16)
            sp.wait_ge(loaded, 32)

        @block.vector
        def _(dve):
            dve.memset(m.eps[:, 0:1], EPS).then_inc(eps_set, 1)
            dve.memset(m.eps[:, 1:2], 0.0).then_inc(eps_set, 1)

    def rope_tables(pos):
        TWO_PI = 2 * np.pi
        c1 = float(np.float32(np.round(TWO_PI * 512) / 512))
        c2 = float(np.float32(np.round((TWO_PI - c1) * 2 ** 22) / 2 ** 22))
        c3 = float(np.float32(TWO_PI - c1 - c2))
        MAGIC = 1.5 * 2.0 ** 23
        ar = Arena(nc, y_at, KD * T * 4)
        posi, ang = ar("posi" + pos, [P, T], I32), ar("ang" + pos, [P, T])
        k, r = ar("turns" + pos, [P, T]), ar("rest" + pos, [P, T])
        with phase(nc, "loaded", "reduced", "order") as (block, loaded, reduced, order):
            @block.sync
            def _(sp):
                sp.dma_start(posi[:], a[pos].partition_broadcast(P)).then_inc(loaded, 16)

            @block.vector
            def _(dve):
                step, done = Signal(dve, order), Signal(dve, reduced)
                dve.wait_ge(loaded, 16)
                step(dve.tensor_copy(ang[:], posi[:]))
                step(dve.tensor_scalar(ang[:], ang[:], freq, None, ALU.mult))
                for quarter, dst in ((0.0, m.sin), (0.25, m.cos)):
                    step(dve.tensor_scalar(k[:], ang[:], 1 / TWO_PI, quarter, ALU.mult, ALU.add))
                    step(dve.tensor_scalar(k[:], k[:], MAGIC, None, ALU.add))
                    step(dve.tensor_scalar(k[:], k[:], -MAGIC, None, ALU.add))
                    step(dve.scalar_tensor_tensor(r[:], k[:], -c1, ang[:], ALU.mult, ALU.add))
                    step(dve.scalar_tensor_tensor(r[:], k[:], -c2, r[:], ALU.mult, ALU.add))
                    step(dve.scalar_tensor_tensor(r[:], k[:], -c3, r[:], ALU.mult, ALU.add))
                    step(dve.tensor_scalar(r[:], r[:], quarter * TWO_PI, 3.1415925, ALU.add, ALU.min))
                    done(dve.tensor_scalar(dst[:], r[:], -3.1415925, None, ALU.max))

            @block.scalar
            def _(act):
                act.wait_ge(reduced, 2)
                act.activation(m.sin[:], m.sin[:], ACT.Sin)
                act.activation(m.cos[:], m.cos[:], ACT.Sin)

    def junction(tag, post=None, pre=None, ahead=None):
        names = ("sum_ready", "root_ready", "x_ready", "square_ready", "square_used", "xsum_ready",
                 "xroot_ready", "scaled_ready", "h_head_ready", "order", "act_order")
        with phase(nc, *names) as (block, sum_ready, root_ready, x_ready, square_ready, square_used,
                                   xsum_ready, xroot_ready, scaled_ready, head_ready, order, act_order):
            A = m.col[:, 0:8]
            G = m.col[:, 8:16]

            @block.sync
            def _(sp):
                if ahead:
                    ahead.loads(sp, 0, RING)

            @block.gpsimd
            def _(pool):
                if ahead:
                    ahead.rests(pool, 0, 2)

            @block.tensor
            def _(pe):
                if post:
                    pe.matmul(ps[0][:], ones, m.acc[:], start=True, stop=True).then_inc(sum_ready, 1)
                if pre:
                    for k in range(KD):
                        pe.wait_ge(square_ready, k + 1)
                        pe.matmul(ps[1][:], ones, m.sq[:, k % 2, :], start=(k == 0), stop=(k == KD - 1))\
                          .then_inc(square_used, 1)

            @block.scalar
            def _(act):
                if ahead:
                    ahead.heads(act, 0, 2)
                if post:
                    act.wait_ge(sum_ready, 1)
                    act.activation(m.acc[:], ps[0][:], ACT.Sqrt, bias=m.eps[:, 0:1], scale=1.0 / D)\
                       .then_inc(root_ready, 1)
                if pre:
                    for k in range(KD):
                        if post:
                            act.wait_ge(x_ready, k + 1)
                        if k >= 2:
                            act.wait_ge(square_used, k - 1)
                        act.activation(m.sq[:, k % 2, :], m.x[:, k, :], ACT.Square).then_inc(square_ready, 1)
                    act.wait_ge(square_used, KD)
                    act.activation(m.acc[:], ps[1][:], ACT.Sqrt, bias=m.eps[:, 0:1], scale=1.0 / D)\
                       .then_inc(xroot_ready, 1)
                    for k in range(KD):
                        act.wait_ge(scaled_ready, k + 1)
                        shift = pre[2][:, k:k + 1] if pre[2] is not None else 0.0
                        act.activation(m.hh[:, k, :], m.tmp[:, k % 2, :], ACT.Identity, bias=shift)\
                           .then_inc(head_ready, 1)

            @block.vector
            def _(dve):
                step, x_done, scaled = Signal(dve, order), Signal(dve, x_ready), Signal(dve, scaled_ready)
                if post:
                    if post[1] is not None:
                        step(dve.tensor_tensor(G, post[0], post[1], ALU.mult))
                        gain = G
                    else:
                        gain = post[0]
                if pre:
                    if pre[1] is not None:
                        step(dve.scalar_tensor_tensor(A, pre[1], 1.0, pre[0], ALU.add, ALU.mult))
                        scale = A
                    else:
                        scale = pre[0]
                if post:
                    dve.wait_ge(root_ready, 1)
                    step(dve.reciprocal(m.acc[:], m.acc[:]))
                    for k in range(KD):
                        step(dve.scalar_tensor_tensor(m.tmp[:, k % 2, :], m.y[:, k, :], gain[:, k:k + 1],
                                                      m.acc[:], ALU.mult, ALU.mult))
                        x_done(dve.tensor_tensor(m.x[:, k, :], m.x[:, k, :], m.tmp[:, k % 2, :], ALU.add))
                if pre:
                    dve.wait_ge(xroot_ready, 1)
                    step(dve.reciprocal(m.acc[:], m.acc[:]))
                    for k in range(KD + 1):
                        if k < KD:
                            if k >= 2:
                                dve.wait_ge(head_ready, k - 1)
                            scaled(dve.scalar_tensor_tensor(m.tmp[:, k % 2, :], m.x[:, k, :], scale[:, k:k + 1],
                                                            m.acc[:], ALU.mult, ALU.mult))
                        if k >= 1:
                            dve.wait_ge(head_ready, k)
                            shift = pre[2][:, k - 1:k] if pre[2] is not None else 0.0
                            step(dve.scalar_tensor_tensor(m.hl[:, k - 1, :], m.tmp[:, (k - 1) % 2, :], shift,
                                                          m.hh[:, k - 1, :].bitcast(F32), ALU.add, ALU.subtract))

    def product_out(s, t0, per, chunks, xh, xl, started=True):
        n = t0 + KD * per
        with phase(nc, "square_ready", "square_used", "y_order", run_ends=(n == s.total)) as \
                (block, square_ready, square_used, y_order):
            @block.sync
            def _(sp):
                s.loads(sp, t0 + RING if started else t0, n + RING)

            @block.gpsimd
            def _(pool):
                s.rests(pool, t0 + 2 if started else t0, n + 2)

            @block.tensor
            def _(pe):
                for t in range(t0, n):
                    nb, part = (t - t0) // per, (t - t0) % per
                    s.ready(pe, t // RING, t % RING)
                    if part == 0 and nb >= 2:
                        pe.wait_ge(square_ready, nb - 1)
                    c0 = 8 * part
                    for c in range(s.width(t) // P):
                        wc = slice(c * P, (c + 1) * P)
                        last = three_pass(pe, ps[nb % 2][:], m.wh[:, t % 2, wc], m.wl[:, t % 2, wc],
                                          xh[:, c0 + c, :], xl[:, c0 + c, :],
                                          start=(c0 + c == 0), stop=(c0 + c == chunks - 1))
                    last.then_inc(s.slot_done, 1)

            @block.scalar
            def _(act):
                if not started:
                    s.heads(act, t0, t0 + 2)
                for t in range(t0, n):
                    s.heads(act, t + 2, t + 3)
                    nb = (t - t0) // per
                    if (t - t0) % per == per - 1:
                        act.wait_ge(s.slot_done, t + 1)
                        act.activation(m.y[:, nb, :], ps[nb % 2][:], ACT.Copy).then_inc(y_order, 1)
                        if nb >= 2:
                            act.wait_ge(square_used, nb - 1)
                        act.activation(m.sq[:, nb % 2, :], ps[nb % 2][:], ACT.Square).then_inc(square_ready, 1)

            @block.vector
            def _(dve):
                for nb in range(KD):
                    dve.wait_ge(square_ready, nb + 1)
                    if nb == 0:
                        dve.tensor_copy(m.acc[:], m.sq[:, 0, :]).then_inc(square_used, 1)
                    else:
                        dve.wait_ge(square_used, nb)
                        dve.tensor_tensor(m.acc[:], m.acc[:], m.sq[:, nb % 2, :], ALU.add)\
                           .then_inc(square_used, 1)

    hid = Arena(nc, mix0, MIX)
    hidh, hidl = hid("hidh", [P, KF, T], F32R), hid("hidl", [P, KF, T], F32R)

    hidh2 = hidh[:].rearrange("p k t -> p (k t)")
    hidl2 = hidl[:].rearrange("p k t -> p (k t)")

    def gate_up(tag, s, conv):
        n = KF // 2
        ar = Arena(nc, y_at, KD * T * 4)
        gs, us = ar("gate" + tag, [P, 2, T]), ar("up" + tag, [P, 2, T])
        hs = ar("hidden" + tag, [P, 2, T])
        with phase(nc, "gate_base", "up_base", "gate_conv", "gate_act", "hid_ready", "pair_free",
                   "order") as (block, *sems):
            gate_base, up_base, gate_conv, gate_act, hid_ready, pair_free, order = sems

            @block.sync
            def _(sp):
                with sp.Fori(1, n) as i:
                    for j in range(RING):
                        s.load(sp, i, j)
                s.loads(sp, GU, GU + RING)

            @block.gpsimd
            def _(pool):
                s.rests(pool, 2, RING)
                with pool.Fori(1, n) as i:
                    for j in range(RING):
                        s.rest(pool, i, j)
                s.rests(pool, GU, GU + 2)

            @block.tensor
            def _(pe):
                def body(i, first=False):
                    for j in range(RING):
                        s.ready(pe, i, j)
                        if not first and j % 2 == 0:
                            pe.wait_ge(pair_free, i * 2 + (j // 2 - 1))
                        for c in range(KD):
                            wc = slice(c * P, (c + 1) * P)
                            last = three_pass(pe, ps[j][:], m.wh[:, j % 2, wc], m.wl[:, j % 2, wc],
                                              m.hh[:, c, :], m.hl[:, c, :], start=(c == 0), stop=(c == KD - 1))
                        last.then_inc(s.slot_done, 1)
                body(0, True)
                with pe.Fori(1, n) as i:
                    body(i)

            @block.scalar
            def _(act):
                def body(i, first=False):
                    for j in range(RING):
                        s.head(act, i + j // 2, (j + 2) % RING)
                        pair = j // 2
                        if conv:
                            act.wait_ge(s.slot_done, i * RING + (j + 1))
                            if not first:
                                act.wait_ge(pair_free, i * 2 + (pair - 1))
                            dst, cb, ready = (gs, 0, gate_base) if j % 2 == 0 else (us, KF, up_base)
                            act.activation(dst[:, pair, :], ps[j][:], ACT.Identity,
                                           bias=m.pc[:, bass.ds(i * 2 + (B_CB + cb + pair), 1)],
                                           scale=m.pc[:, bass.ds(i * 2 + (B_CW + 88 + cb + pair), 1)])\
                               .then_inc(ready, 1)
                            if j % 2 == 1:
                                act.wait_ge(gate_conv, i * 2 + (pair + 1))
                                act.activation(gs[:, pair, :], gs[:, pair, :], ACT.Gelu_apprx_tanh)\
                                   .then_inc(gate_act, 1)
                        elif j % 2 == 0:
                            act.wait_ge(s.slot_done, i * RING + (j + 1))
                            if not first:
                                act.wait_ge(pair_free, i * 2 + (pair - 1))
                            act.activation(gs[:, pair, :], ps[j][:], ACT.Silu).then_inc(gate_act, 1)
                body(0, first=True)
                with act.Fori(1, n) as i:
                    body(i)

            @block.vector
            def _(dve):
                STEPS = 5 if conv else 2

                def body(i):
                    for pair in range(2):
                        cnt = [0]

                        def step(ins):
                            cnt[0] += 1
                            ins.then_inc(order, 1)
                            dve.wait_ge(order, i * (2 * STEPS) + (pair * STEPS + cnt[0]))

                        def tap(buf, bank, block, shift, ready):
                            w_col = B_CW + 44 * (2 - shift) + block
                            return dve.scalar_tensor_tensor(
                                buf[:, pair, shift:T], bank[:, 0:T - shift],
                                m.pc[:, bass.ds(i * 2 + (w_col + pair), 1)], buf[:, pair, shift:T],
                                ALU.mult, ALU.add)
                        if conv:
                            dve.wait_ge(gate_base, i * 2 + (pair + 1))
                            step(tap(gs, ps[2 * pair], 0, 1, gate_base))
                            tap(gs, ps[2 * pair], 0, 2, None).then_inc(gate_conv, 1)
                            dve.wait_ge(up_base, i * 2 + (pair + 1))
                            step(tap(us, ps[2 * pair + 1], KF, 1, up_base))
                            step(tap(us, ps[2 * pair + 1], KF, 2, None))
                            up = us[:, pair, :]
                        else:
                            dve.wait_ge(s.slot_done, i * RING + (2 * pair + 2))
                            up = ps[2 * pair + 1][:]
                        dve.wait_ge(gate_act, i * 2 + (pair + 1))
                        dve.tensor_tensor(hs[:, pair, :], gs[:, pair, :], up, ALU.mult).then_inc(pair_free, 1)
                        dve.wait_ge(pair_free, i * 2 + (pair + 1))
                        step(dve.tensor_copy(hidh2[:, bass.ds(i * (2 * T) + pair * T, T)], hs[:, pair, :]))
                        step(dve.tensor_tensor(hidl2[:, bass.ds(i * (2 * T) + pair * T, T)], hs[:, pair, :],
                                               hidh2[:, bass.ds(i * (2 * T) + pair * T, T)].bitcast(F32), ALU.subtract))
                with dve.Fori(0, n) as i:
                    body(i)

    def feed_forward(tag, s, conv):
        gate_up(tag, s, conv)
        product_out(s, GU, 3, KF, hidh, hidl)

    stream_sems = [nc.semaphore(n, num=STREAM_SEM + k).__enter__() for k, n in enumerate(STREAM)]

    def run(w, base, total, width=lambda t: SLOT):
        return Stream(m, w, base, total, stream_sems, width)

    def ff_run(w, base):
        return run(w, base, GU + DN, lambda t: SLOT if t < GU or (t - GU) % 3 < 2 else (KF - 16) * P)

    cbc_ar = Arena(nc, mix0, MIX)
    cbc, junk, cst4 = cbc_ar("cbc", [P, D]), cbc_ar("junk", [P, D]), cbc_ar("mod4", [P, 4])

    def modulation(w, base, pcols):
        n = 48 // RING
        with phase(nc, "cols_in0", "cols_in1", "cols_in2", "cols_in3", "c_in", "c_act", "used", "moved", "p_in") as \
                (block, w0, w1, w2, w3, c_in, c_act, used, moved, p_in):
            w_in = (w0, w1, w2, w3)

            @block.sync
            def _(sp):
                sp.dma_start(cbc[:], a["c"].partition_broadcast(P)).then_inc(c_in, 16)
                sp.dma_start(m.pc[:, 0:A_COLS], pcols).then_inc(p_in, 16)
                for j in range(RING):
                    sp.dma_start(m.raw[:, j, :], w[sp.snap(base + j)]).then_inc(w_in[j], 16)
                with sp.Fori(1, n) as i:
                    for j in range(RING):
                        src = w[sp.snap(base + i * RING + j)]
                        sp.wait_ge(used, i * RING + (j + 1 - RING))
                        sp.dma_start(m.raw[:, j, :], src).then_inc(w_in[j], 16)

            @block.scalar
            def _(act):
                act.wait_ge(c_in, 16)
                act.activation(cbc[:], cbc[:], ACT.Silu).then_inc(c_act, 1)

            @block.vector
            def _(dve):
                dve.wait_ge(c_act, 1)

                def body(i, first=False):
                    for j in range(RING):
                        dve.wait_ge(w_in[j], i * 16 + 16)
                        if j == 0 and not first:
                            dve.wait_ge(moved, i)
                        if not (first and j == 0):
                            dve.wait_ge(used, i * RING + j)
                        dve.tensor_tensor_reduce(junk[:], m.raw[:, j, :], cbc[:], 1.0, 0.0, ALU.mult, ALU.add,
                                                 cst4[:, j:j + 1]).then_inc(used, 1)
                    dve.wait_ge(used, i * RING + RING)
                    dve.tensor_copy(m.mod[:, bass.ds(i * RING, RING)], cst4[:]).then_inc(moved, 1)
                body(0, True)
                with dve.Fori(1, n) as i:
                    body(i)
                dve.wait_ge(moved, n)
                dve.wait_ge(p_in, 16)
                dve.tensor_tensor(m.mod[:], m.mod[:], m.pc[:, A_BMOD:A_BMOD + 48], ALU.add)


    mx = Arena(nc, mix0, MIX)
    qT, kT, qi = mx("qT", [P, 4, T]), mx("kT", [P, 4, T]), mx("qi", [P, 4, T])
    ki, va = mx("ki", [P, T]), mx("va", [P, NT, T])
    qk = mx("qk", [P, 8, T])
    og = mx("og", [P, MH, T])
    vm = mx("vm", [P, NT, MH, MD + 1])
    wi, ir, fr = mx("wi", [8, T]), mx("ir", [MH, T]), mx("fr", [MH, T])
    work1 = mx.at
    rawb = mx("rawb", [P, 2, T])
    yar = Arena(nc, y_at, KD * T * 4)
    cqf, cqh, cql = yar("cqf", [P, 2, T]), yar("cqh", [P, 2, T], F32R), yar("cql", [P, 2, T], F32R)

    def in_products1(s):
        kinds = ([("latent", c) for c in range(2)] + [("key", c) for c in range(4)] + [("ikey", 0), ("rows", 0)]
                 + [("conv", c) for c in range(8)] + [("ogate", c) for c in range(4)]
                 + [("value", c) for c in range(4)] + [("mvalue", c) for c in range(4)]
                 + [("query", 0), ("iquery", 0)])
        assert len(kinds) == IN1
        ropes = []
        for t, (kind, c) in enumerate(kinds):
            if kind == "key":
                ropes.append((t, t % 4, kT[:, c, :]))
            if kind == "ikey":
                ropes.append((t, t % 4, ki[:]))
            if kind in ("query", "iquery"):
                dst = qT if kind == "query" else qi
                ropes += [(t, (4 if kind == "query" else 0) + b, dst[:, b, :]) for b in range(4)]
        rope_of = {}
        for r, (t, _, _) in enumerate(ropes):
            rope_of.setdefault(t, []).append(r)
        uses = [0] * 8
        before = {}
        for t, (kind, c) in enumerate(kinds):
            if t < 20:
                before[t] = {t % 4: uses[t % 4]}
                uses[t % 4] += 1
            elif kind in ("value", "mvalue", "query", "iquery") and c == 0:
                banks = range(4, 8) if kind in ("value", "query") else range(4)
                before[t] = {b: uses[b] for b in banks}
                for b in banks:
                    uses[b] += 1
            if t == 1:
                uses[4] += 1
        free_names = [f"bank_free{b}" for b in range(8)]
        with phase(nc, *free_names, "latent_sq", "latent_sum", "latent_root", "latent_ready",
                   "unrotated_ready", "rotated_ready", "rope_done", "conv_base", "conv_done", "order",
                   "act_order", "ones_set", run_ends=True) as (block, *sems):
            bank_free = sems[0:8]
            (latent_sq, latent_sum, latent_root, latent_ready, unrotated_ready, rotated_ready, rope_done,
             conv_base, conv_done, order, act_order, ones_set) = sems[8:]

            @block.sync
            def _(sp):
                s.loads(sp, RING, IN1)

            @block.gpsimd
            def _(pool):
                pool.memset(vm[:, :, :, MD:MD + 1], 1.0).then_inc(ones_set, 1)
                s.rests(pool, 2, IN1)

            @block.tensor
            def _(pe):
                def rotate(t):
                    for r in rope_of.get(t, ()):
                        pe.wait_ge(unrotated_ready, r + 1)
                        pe.matmul(ps[ropes[r][1]][:], rot, rawb[:, r % 2, :], start=True, stop=True)\
                          .then_inc(rotated_ready, 1)

                for t, (kind, c) in enumerate(kinds):
                    s.ready(pe, t // RING, t % RING)
                    for b, n in before.get(t, {}).items():
                        if n:
                            pe.wait_ge(bank_free[b], n)
                    if kind in ("value", "mvalue"):
                        b0 = 4 if kind == "value" else 0
                        for kk in range(2):
                            k = 2 * c + kk
                            wc = slice(kk * T, (kk + 1) * T)
                            for tb in range(NT):
                                tc = slice(tb * P, (tb + 1) * P)
                                o = ps[b0 + tb][:]
                                pe.matmul(o, m.hh[:, k, tc], m.wh[:, t % 2, wc], start=(k == 0), stop=False)
                                pe.matmul(o, m.hh[:, k, tc], m.wl[:, t % 2, wc], start=False, stop=False)
                                last = pe.matmul(o, m.hl[:, k, tc], m.wh[:, t % 2, wc], start=False,
                                                 stop=(k == KD - 1))
                    elif kind in ("query", "iquery"):
                        if kind == "query":
                            pe.wait_ge(latent_ready, 1)
                        b0 = 4 if kind == "query" else 0
                        for nb in range(4):
                            for k in range(2):
                                wc = slice(k * T + nb * P, k * T + (nb + 1) * P)
                                last = three_pass(pe, ps[b0 + nb][:], m.wh[:, t % 2, wc], m.wl[:, t % 2, wc],
                                                  cqh[:, k, :], cql[:, k, :], start=(k == 0), stop=(k == 1))
                    else:
                        for k in range(KD):
                            wc = slice(k * P, (k + 1) * P)
                            last = three_pass(pe, ps[t % 4][:], m.wh[:, t % 2, wc], m.wl[:, t % 2, wc],
                                              m.hh[:, k, :], m.hl[:, k, :], start=(k == 0), stop=(k == KD - 1))
                    last.then_inc(s.slot_done, 1)
                    if t == 3:
                        pe.wait_ge(latent_sq, 2)
                        pe.matmul(ps[4][:], ones, m.sq[:, 0, :], start=True, stop=False)
                        pe.matmul(ps[4][:], ones, m.sq[:, 1, :], start=False, stop=True).then_inc(latent_sum, 1)
                    if t >= 1:
                        rotate(t - 1)
                rotate(IN1 - 1)

            @block.scalar
            def _(act):
                step = Signal(act, act_order)

                def silu(c):
                    act.wait_ge(conv_done, c + 1)
                    step(act.activation(qk[:, c, :], qk[:, c, :], ACT.Silu))

                for t, (kind, c) in enumerate(kinds):
                    s.heads(act, t + 2, t + 3)
                    act.wait_ge(s.slot_done, t + 1)
                    bank = ps[t % 4]
                    if kind == "latent":
                        step(act.activation(cqf[:, c, :], bank[:], ACT.Copy))
                        act.activation(m.sq[:, c, :], bank[:], ACT.Square).then_inc(bank_free[t % 4], 1)
                        act.wait_ge(bank_free[t % 4], 1)
                        act.sem_inc(latent_sq, 1)
                    if t == 4:
                        act.wait_ge(latent_sum, 1)
                        act.activation(m.acc[:], ps[4][:], ACT.Sqrt, bias=m.eps[:, 0:1], scale=1.0 / QR)\
                           .then_inc(latent_root, 1)
                    for r in rope_of.get(t, ()):
                        if r >= 2:
                            act.wait_ge(rope_done, r - 1)
                        act.activation(rawb[:, r % 2, :], ps[ropes[r][1]][:], ACT.Copy).then_inc(unrotated_ready, 1)
                    if kind == "rows":
                        step(act.activation(wi[:], bank[0:8, :], ACT.Copy, scale=float((8 * 64) ** -0.5)))
                        step(act.activation(ir[:], bank[32:32 + MH, :], ACT.Identity, bias=m.pc[0:MH, A_BI:A_BI + 1]))
                        act.activation(fr[:], bank[64:64 + MH, :], ACT.Identity, bias=m.pc[0:MH, A_BF:A_BF + 1])\
                           .then_inc(bank_free[t % 4], 1)
                    if kind == "conv":
                        act.activation(qk[:, c, :], bank[:], ACT.Identity, bias=m.pc[:, A_CB + c:A_CB + c + 1],
                                       scale=m.pc[:, A_CW + 24 + c:A_CW + 25 + c]).then_inc(conv_base, 1)
                        if c:
                            silu(c - 1)
                    if kind == "ogate":
                        if c == 0:
                            silu(7)
                        act.activation(og[:, c, :], bank[:], ACT.Sigmoid).then_inc(bank_free[t % 4], 1)
                    if kind == "mvalue" and c == 3:
                        act.wait_ge(ones_set, 1)
                        for tb in range(NT):
                            act.activation(vm[:, tb, :, 0:MD], ps[tb][:].rearrange("p (h d) -> p h d", h=MH),
                                           ACT.Copy).then_inc(bank_free[tb], 1)

            @block.vector
            def _(dve):
                step = Signal(dve, order)

                def rope(r):
                    _, bank, dst = ropes[r]
                    dve.wait_ge(unrotated_ready, r + 1)
                    step(dve.tensor_tensor(m.tmp[:, 0, :], rawb[:, r % 2, :], m.cos[:], ALU.mult))
                    dve.wait_ge(rotated_ready, r + 1)
                    dve.tensor_tensor(m.tmp[:, 1, :], ps[bank][:], m.sin[:], ALU.mult).then_inc(bank_free[bank], 1)
                    freed[bank] += 1
                    dve.wait_ge(bank_free[bank], freed[bank])
                    dve.tensor_tensor(dst, m.tmp[:, 0, :], m.tmp[:, 1, :], ALU.add).then_inc(rope_done, 1)
                    dve.wait_ge(rope_done, r + 1)

                freed = [0] * 8
                for t, (kind, c) in enumerate(kinds):
                    if t == 5:
                        dve.wait_ge(latent_root, 1)
                        dve.reciprocal(m.acc[:], m.acc[:]).then_inc(bank_free[4], 1)
                        freed[4] += 1
                        dve.wait_ge(bank_free[4], 1)
                        for k in range(2):
                            step(dve.scalar_tensor_tensor(cqf[:, k, :], cqf[:, k, :],
                                                          m.pc[:, A_QN + k:A_QN + k + 1], m.acc[:],
                                                          ALU.mult, ALU.mult))
                            step(dve.tensor_copy(cqh[:, k, :], cqf[:, k, :]))
                            step(dve.tensor_tensor(cql[:, k, :], cqf[:, k, :], cqh[:, k, :].bitcast(F32),
                                                   ALU.subtract))
                        dve.sem_inc(latent_ready, 1)
                    for r in rope_of.get(t, ()):
                        rope(r)
                    bank = ps[t % 4]
                    if kind == "conv":
                        dve.wait_ge(conv_base, c + 1)
                        for shift in (1, 2, 3):
                            w_col = A_CW + 8 * (3 - shift) + c
                            ins = dve.scalar_tensor_tensor(qk[:, c, shift:T], bank[:, 0:T - shift],
                                                           m.pc[:, w_col:w_col + 1], qk[:, c, shift:T],
                                                           ALU.mult, ALU.add)
                            if shift < 3:
                                step(ins)
                        ins.then_inc(conv_done, 1)
                        dve.wait_ge(conv_done, c + 1)
                        dve.sem_inc(bank_free[t % 4], 1)
                    if kind == "value" and c == 3:
                        dve.wait_ge(s.slot_done, t + 1)
                        for tb in range(NT):
                            dve.tensor_copy(va[:, tb, :], ps[4 + tb][:]).then_inc(bank_free[4 + tb], 1)
                            freed[4 + tb] += 1

                    for b, n in before.get(t, {}).items():
                        if t < 20:
                            freed[b] = n + 1
                        elif kind == "mvalue":
                            freed[b] = n + 1



    wk = Arena(nc, ring_at, RING_BYTES)
    sc, pr, pt = wk("sc", [P, 2, T]), wk("pr", [P, 3, T]), wk("pt", [P, 2, T])
    sel_at = wk.at
    sel = wk("sel", [P, NT, T])
    on = wk("on", [P, T])
    small = wk("small", [P, 256])
    yk = Arena(nc, y_at, KD * T * 4)
    wt = yk("wt", [P, 2, 1280])
    arg = yk("arg", [P, 2, T])
    att_n = Arena(nc, y_at, NT * T * 4)("att_n", [P, NT, T])
    wk2 = Arena(nc, work1, mix0 + MIX - work1)
    num = wk2("num", [P, NT, MH, MD + 1])
    b_row = wk2("b_row", [MH, T])
    rw = Arena(nc, sel_at, NT * T * 4)
    f_row, lf_row, m_row, one_row = (rw(n, [MH, T]) for n in ("f_row", "lf_row", "m_row", "one_row"))
    WT_AT = [0, 512, 896, 1152]

    def mixer1():
        names = ("gate_abs", "gate_log", "gate_sums", "m_exp", "rows_turned", "cols_ready",
                 "peak_row", "peak_used", "mscore", "arg_ready", "decay", "weight_ready", "masked",
                 "mout", "mout_copied", "iscore", "irelu", "irelu_used", "sel_ready",
                 "score", "soft_in", "weights", "turned", "turned_copied", "pv", "out_copied",
                 "root_in", "root", "norm_ready", "feat_turned", "feat_used", "order", "aorder", "porder")
        with phase(nc, *names) as (block, *sems):
            (gate_abs, gate_log, gate_sums, m_exp, rows_turned, cols_ready, peak_row, peak_used, mscore,
             arg_ready, decay, weight_ready, masked, mout, mout_copied, iscore, irelu, irelu_used, sel_ready,
             score, soft_in, weights, turned, turned_copied, pv, out_copied, root_in, root, norm_ready,
             feat_turned, feat_used, order, aorder, porder) = sems
            wi_col = small[:, 0:32]
            bm_col = small[:, 32:64]
            mxs, nmx = small[:, 64:96], small[:, 96:128]
            den, root_c = small[:, 128:160], small[:, 160:192]
            peak = small[:, 192:200]
            mden = small[:, 200:216]
            mitems = [(h, sb) for h in range(MH) for sb in range(NT)]
            iitems = [(tb, h) for tb in range(1, NT) for h in range(HEADS)]
            items = [(tb, h) for tb in range(NT) for h in range(HEADS)]

            def attend(pe):
                def scores(i):
                    tb, h = items[i]
                    if i >= 3:
                        pe.wait_ge(soft_in, i - 2)
                    r = slice(64 * (h % 2), 64 * (h % 2) + 64)
                    w_ = (tb + 1) * P
                    pe.matmul(ps[i % 3][:, 0:w_], qT[r, h // 2, tb * P:(tb + 1) * P], kT[r, h // 2, 0:w_],
                              start=True, stop=True).then_inc(score, 1)

                def turn(i):
                    tb, h = items[i]
                    pe.wait_ge(weights, i + 1)
                    if i >= 2:
                        pe.wait_ge(turned_copied, i - 1)
                    for kb in range(tb + 1):
                        ins = pe.transpose(ps[3 + i % 2][:, kb * P:(kb + 1) * P],
                                           pr[:, i % 3, kb * P:(kb + 1) * P], ident)
                    ins.then_inc(turned, 1)

                def values(i):
                    tb, h = items[i]
                    pe.wait_ge(turned_copied, i + 1)
                    if h == 0 and tb >= 2:
                        pe.wait_ge(out_copied, tb - 1)
                    for kb in range(tb + 1):
                        ins = pe.matmul(ps[5 + tb % 2][:, h * HD:(h + 1) * HD], pt[:, i % 2, kb * P:(kb + 1) * P],
                                        va[:, kb, h * HD:(h + 1) * HD], start=(kb == 0), stop=(kb == tb))
                    ins.then_inc(pv, 1)
                N = len(items)
                for i in range(N + 3):
                    if i < N:
                        scores(i)
                    if 0 <= i - 2 < N:
                        turn(i - 2)
                    if 0 <= i - 3 < N:
                        values(i - 3)

            def square_root(act, g):
                act.wait_ge(root_in, g + 1)
                n_ = MH if g < NT else HEADS
                act.activation(root_c[:, 0:n_], root_c[:, 0:n_], ACT.Sqrt, bias=m.eps[:, 0:1],
                               scale=1.0 / (MD if g < NT else HD)).then_inc(root, 1)

            def mcopy(act, h):
                act.wait_ge(mout, h + 1)
                for half in range(2):
                    act.activation(num[:, 2 * half:2 * half + 2, h, :],
                                   ps[4 + half][:, 0:258].rearrange("p (b d) -> p b d", b=2), ACT.Copy)\
                       .then_inc(mout_copied, 1)

            def mweight(dve, n, wready):
                h, sb = mitems[n]
                w_ = T - sb * P
                dve.wait_ge(mscore, n + 1)
                dve.wait_ge(decay, n + 1)
                if h >= 2 and sb == 0:
                    dve.wait_ge(mout, h - 1)
                wready(dve.scalar_tensor_tensor(wt[:, h % 2, WT_AT[sb]:WT_AT[sb] + w_], ps[n % 2][:, 0:w_],
                                                MD ** -0.5, arg[:, n % 2, 0:w_], ALU.mult, ALU.mult))

            def rescale(dve, step, rin, nready, g, src, dst, col, n_, d_, r2):
                bc = lambda c: c.unsqueeze(2).to_broadcast([P, n_, d_])
                step(dve.tensor_tensor(dst, src, bc(col), ALU.mult))
                sq_ = m.sq[:, 0, :].rearrange("p (h d) -> p h d", h=n_)
                step(dve.tensor_tensor(sq_, dst, dst, ALU.mult))
                rin(dve.tensor_reduce(root_c[:, 0:n_], sq_, AX_X, ALU.add))
                dve.wait_ge(root, g + 1)
                step(dve.reciprocal(r2, root_c[:, 0:n_]))
                nready(dve.tensor_tensor(dst, dst, bc(r2), ALU.mult))

            def finish(dve, step, ocop, rin, nready, tb):
                dve.wait_ge(pv, HEADS * (tb + 1))
                r_ = small[:, 216:224]
                step(dve.reciprocal(r_, den[:, HEADS * tb:HEADS * (tb + 1)]))
                src = ps[5 + tb % 2][:].rearrange("p (h d) -> p h d", h=HEADS)
                dst = att_n[:, tb, :].rearrange("p (h d) -> p h d", h=HEADS)
                ocop(dve.tensor_tensor(dst, src, r_.unsqueeze(2).to_broadcast([P, HEADS, HD]), ALU.mult))
                sq_ = m.sq[:, 0, :].rearrange("p (h d) -> p h d", h=HEADS)
                step(dve.tensor_tensor(sq_, dst, dst, ALU.mult))
                rin(dve.tensor_reduce(root_c[:, 0:HEADS], sq_, AX_X, ALU.add))
                dve.wait_ge(root, NT + tb + 1)
                step(dve.reciprocal(small[:, 224:232], root_c[:, 0:HEADS]))
                nready(dve.tensor_tensor(dst, dst, small[:, 224:232].unsqueeze(2).to_broadcast([P, HEADS, HD]),
                                         ALU.mult))

            @block.tensor
            def _(pe):
                for tb in range(NT):
                    ins = pe.transpose(ps[7][:, 8 * tb:8 * tb + 8], wi[0:8, tb * P:(tb + 1) * P], ident[0:8, 0:8])
                ins.then_inc(rows_turned, 1)
                def index(n):
                    tb, h = iitems[n]
                    if n >= 3:
                        pe.wait_ge(irelu, n - 2)
                    r = slice(64 * (h % 2), 64 * (h % 2) + 64)
                    w_ = (tb + 1) * P
                    pe.matmul(ps[n % 3][:, 0:w_], qi[r, h // 2, tb * P:(tb + 1) * P], ki[r, 0:w_],
                              start=True, stop=True).then_inc(iscore, 1)
                pe.wait_ge(m_exp, 1)
                pe.wait_ge(gate_sums, 2)
                for tb in range(NT):
                    pe.transpose(ps[7][:, 32 + 8 * tb:36 + 8 * tb], b_row[:, tb * P:(tb + 1) * P], ident[0:4, 0:4])
                    ins = pe.transpose(ps[7][:, 36 + 8 * tb:40 + 8 * tb], f_row[:, tb * P:(tb + 1) * P],
                                       ident[0:4, 0:4])
                ins.then_inc(rows_turned, 1)
                for h in range(MH):
                    if h:
                        pe.wait_ge(arg_ready, NT * h)
                    pe.matmul(ps[6][:], m.cst[0:MH, C_SEL + h * P:C_SEL + (h + 1) * P], m_row[:],
                              start=True, stop=True).then_inc(peak_row, 1)
                    for sb in range(NT):
                        n = NT * h + sb
                        if n >= 2:
                            pe.wait_ge(weight_ready, n - 1)
                        pe.matmul(ps[n % 2][:, 0:T - sb * P], qk[:, 4 + h, sb * P:(sb + 1) * P],
                                  qk[:, h, sb * P:T], start=True, stop=True).then_inc(mscore, 1)
                    if h:
                        pe.wait_ge(mout_copied, 2 * h)
                    pe.wait_ge(masked, NT * (h + 1))
                    for tb in range(NT):
                        for sb in range(tb + 1):
                            c0 = WT_AT[sb] + (tb - sb) * P
                            ins = pe.matmul(ps[4 + tb // 2][:, (tb % 2) * 129:(tb % 2) * 129 + 129],
                                            wt[:, h % 2, c0:c0 + P], vm[:, sb, h, :],
                                            start=(sb == 0), stop=(sb == tb))
                    ins.then_inc(mout, 1)
                for n in range(len(iitems)):
                    if n == 0:
                        pe.wait_ge(weight_ready, 16)
                    index(n)
                pe.wait_ge(irelu, len(iitems))
                pe.wait_ge(mout_copied, 8)
                attend(pe)
                for g in range(2 * NT):
                    pe.wait_ge(norm_ready, g + 1)
                    if g:
                        pe.wait_ge(feat_used, g)
                    for c in range(4):
                        s_ = num[:, g, c, 0:MD] if g < NT else att_n[:, g - NT, c * P:(c + 1) * P]
                        ins = pe.transpose(ps[7][:, c * P:(c + 1) * P], s_, ident)
                    ins.then_inc(feat_turned, 1)

            @block.scalar
            def _(act):
                step = Signal(act, aorder)
                step(act.activation(lf_row[:], fr[:], ACT.Abs))
                step(act.activation(lf_row[:], lf_row[:], ACT.Exp, scale=-1.0))
                act.activation(lf_row[:], lf_row[:], ACT.Ln, bias=1.0).then_inc(gate_log, 1)
                act.wait_ge(gate_sums, 1)
                act.activation(f_row[:], f_row[:], ACT.Exp, scale=-1.0).then_inc(m_exp, 1)
                for n, (h, sb) in enumerate(mitems):
                    act.wait_ge(arg_ready, n + 1)
                    act.activation(arg[:, n % 2, 0:T - sb * P], arg[:, n % 2, 0:T - sb * P], ACT.Exp)\
                       .then_inc(decay, 1)
                    if sb == NT - 1 and h >= 1:
                        mcopy(act, h - 1)
                mcopy(act, MH - 1)
                for n, (tb, h) in enumerate(iitems):
                    act.wait_ge(iscore, n + 1)
                    if n >= 2:
                        act.wait_ge(irelu_used, n - 1)
                    act.activation(sc[:, n % 2, 0:(tb + 1) * P], ps[n % 3][:, 0:(tb + 1) * P], ACT.Relu)\
                       .then_inc(irelu, 1)

                def soften(i):
                    tb, h = items[i]
                    act.wait_ge(soft_in, i + 1)
                    if i >= 3:
                        act.wait_ge(turned, i - 2)
                    w_ = (tb + 1) * P
                    act.activation(pr[:, i % 3, 0:w_], sc[:, i % 2, 0:w_], ACT.Exp, bias=nmx[:, i:i + 1],
                                   scale=HD ** -0.5, accum_out=den[:, i:i + 1]).then_inc(weights, 1)

                def copy_turned(i):
                    tb, h = items[i]
                    act.wait_ge(turned, i + 1)
                    if i >= 2:
                        act.wait_ge(pv, i - 1)
                    w_ = (tb + 1) * P
                    act.activation(pt[:, i % 2, 0:w_], ps[3 + i % 2][:, 0:w_], ACT.Copy).then_inc(turned_copied, 1)
                N = len(items)
                for g in range(NT):
                    square_root(act, g)
                for i in range(N + 1):
                    if i < N:
                        soften(i)
                    if i >= 1:
                        copy_turned(i - 1)
                    if i > HEADS and i % HEADS == 3:
                        square_root(act, NT + i // HEADS - 1)
                square_root(act, 2 * NT - 1)

            @block.gpsimd
            def _(pool):
                for n, (h, sb) in enumerate(mitems):
                    pool.wait_ge(weight_ready, n + 1)
                    w_ = wt[:, h % 2, WT_AT[sb]:WT_AT[sb] + P]
                    pool.affine_select(out=w_, in_=w_, compare_op=ALU.is_ge, fill=0.0, base=0,
                                       pattern=[[1, P]], channel_multiplier=-1).then_inc(masked, 1)

            @block.vector
            def _(dve):
                step = Signal(dve, order)
                S = lambda sem: Signal(dve, sem)
                sums, cols, args, wready, iused, sready = (S(x) for x in (
                    gate_sums, cols_ready, arg_ready, weight_ready, irelu_used, sel_ready))
                sin_, ocop, rin, nready, fused = (S(x) for x in (soft_in, out_copied, root_in, norm_ready,
                                                                 feat_used))
                step(dve.memset(one_row[:], 1.0))
                dve.wait_ge(rows_turned, 1)
                step(dve.tensor_copy(wi_col, ps[7][:, 0:32]))
                dve.wait_ge(gate_log, 1)
                step(dve.scalar_tensor_tensor(lf_row[:], fr[:], 0.0, lf_row[:], ALU.min, ALU.subtract))
                step(dve.tensor_tensor_scan(f_row[:], one_row[:], lf_row[:], 0.0, ALU.mult, ALU.add))
                step(dve.tensor_tensor(b_row[:], ir[:], f_row[:], ALU.subtract))
                step(dve.tensor_tensor_scan(m_row[:], b_row[:], b_row[:], 0.0, ALU.max, ALU.max))
                sums(dve.tensor_tensor(f_row[:], f_row[:], m_row[:], ALU.add))
                sums(dve.tensor_scalar(m_row[:], m_row[:], -1.0, None, ALU.mult))
                dve.wait_ge(rows_turned, 2)
                cols(dve.tensor_copy(bm_col, ps[7][:, 32:64]))
                for n, (h, sb) in enumerate(mitems):
                    w_ = T - sb * P
                    if sb == 0 and n:
                        mweight(dve, n - 1, wready)
                    dve.wait_ge(peak_row, h + 1)
                    if n >= 2:
                        dve.wait_ge(weight_ready, n - 1)
                    args(dve.tensor_scalar(arg[:, n % 2, 0:w_], ps[6][:, sb * P:T],
                                           bm_col[:, 8 * sb + h:8 * sb + h + 1], 0.0, ALU.add, ALU.min))
                    if sb:
                        mweight(dve, n - 1, wready)
                mweight(dve, 15, wready)
                for n, (tb, h) in enumerate(iitems):
                    w_ = (tb + 1) * P
                    acc_ = sel[:, tb, 0:w_]
                    dve.wait_ge(irelu, n + 1)
                    wcol = wi_col[:, 8 * tb + h:8 * tb + h + 1]
                    if h == 0:
                        iused(dve.scalar_tensor_tensor(acc_, sc[:, n % 2, 0:w_], wcol, causal(tb),
                                                       ALU.mult, ALU.add))
                    else:
                        iused(dve.scalar_tensor_tensor(acc_, sc[:, n % 2, 0:w_], wcol, acc_, ALU.mult, ALU.add))
                    if h == HEADS - 1:
                        for _ in range(TOPK // 8):
                            step(dve.max(peak, acc_))
                            step(dve.match_replace(acc_, peak, acc_, TAKEN))
                        sready(dve.tensor_scalar(acc_, acc_, TAKEN, NEG, ALU.not_equal, ALU.mult))
                dve.wait_ge(mout_copied, 8)
                for tb in range(NT):
                    step(dve.scalar_tensor_tensor(mden[:, 0:4], num[:, tb, :, MD], -1.0, num[:, tb, :, MD],
                                                  ALU.mult, ALU.max))
                    step(dve.tensor_tensor(mden[:, 0:4], mden[:, 0:4], bm_col[:, 8 * tb + 4:8 * tb + 8], ALU.max))
                    step(dve.reciprocal(mden[:, 0:4], mden[:, 0:4]))
                    rescale(dve, step, rin, nready, tb, num[:, tb, :, 0:MD], num[:, tb, :, 0:MD],
                            mden[:, 0:4], MH, MD, mden[:, 4:8])
                for i, (tb, h) in enumerate(items):
                    w_ = (tb + 1) * P
                    dve.wait_ge(score, i + 1)
                    if i >= 2:
                        dve.wait_ge(weights, i - 1)
                    mask = causal(tb) if tb == 0 else sel[:, tb, 0:w_]
                    step(dve.tensor_tensor_reduce(sc[:, i % 2, 0:w_], ps[i % 3][:, 0:w_], mask, 1.0, TAKEN,
                                                  ALU.add, ALU.max, mxs[:, i:i + 1]))
                    sin_(dve.tensor_scalar(nmx[:, i:i + 1], mxs[:, i:i + 1], -(HD ** -0.5), None, ALU.mult))
                    if h == 3 and tb:
                        finish(dve, step, ocop, rin, nready, tb - 1)
                finish(dve, step, ocop, rin, nready, NT - 1)
                for g in range(2 * NT):
                    tb = g % NT
                    dve.wait_ge(feat_turned, g + 1)
                    c0 = 4 if g < NT else 0
                    for c in range(4):
                        ts_ = slice(tb * P, (tb + 1) * P)
                        dst = on[:, c * P:(c + 1) * P]
                        if g < NT:
                            ins = dve.scalar_tensor_tensor(dst, ps[7][:, c * P:(c + 1) * P],
                                                           m.pc[:, A_MN + c:A_MN + c + 1], og[:, c, ts_],
                                                           ALU.mult, ALU.mult)
                        else:
                            ins = dve.tensor_scalar(dst, ps[7][:, c * P:(c + 1) * P],
                                                    m.pc[:, A_AN + c:A_AN + c + 1], None, ALU.mult)
                        if c < 3:
                            step(ins)
                        else:
                            fused(ins)
                    o3 = on[:].rearrange("p (c t) -> p c t", c=4)
                    step(dve.tensor_copy(m.hh[:, c0:c0 + 4, tb * P:(tb + 1) * P], o3))
                    step(dve.tensor_tensor(m.hl[:, c0:c0 + 4, tb * P:(tb + 1) * P], o3,
                                           m.hh[:, c0:c0 + 4, tb * P:(tb + 1) * P].bitcast(F32), ALU.subtract))


    mz = Arena(nc, mix0, MIX)
    q2 = mz("q2", [P, 4, T])
    kc, vc, ksl, kwn = (mz(n, [P, T]) for n in ("kc", "vc", "ksl", "kwn"))
    VSW = 280
    vsw = mz("vsw", [P, NT, VSW])
    sq2, sk2, sv2 = mz("sq2", [P, 4, T]), mz("sk2", [P, 4, T]), mz("sv2", [P, NT, T])
    gm = mz("gm", [P, 2 * KD, T])
    kct, vct = mz("kct", [P, 32]), mz("vct", [P, P])
    rawb2 = mz("rawb2", [P, T])
    y2 = Arena(nc, y_at, KD * T * 4)
    peh = [y2(f"peh{i}", [P, CB, 32], F32R) for i in range(2)]
    pel = [y2(f"pel{i}", [P, CB, 32], F32R) for i in range(2)]

    def params2(pcols):
        with phase(nc, "loaded") as (block, loaded):
            @block.sync
            def _(sp):
                sp.dma_start(m.pc[:], pcols).then_inc(loaded, 16)
                sp.wait_ge(loaded, 16)

    def in_products2(s):
        kinds = ([("rope", q2[:, c, :]) for c in range(4)] + [("rope", kc[:]), ("plain", vc[:]), ("rope", ksl[:]),
                 ("rope", kwn[:])] + [("value", c) for c in range(4)]
                 + [("plain", sq2[:, c, :]) for c in range(4)] + [("plain", sk2[:, c, :]) for c in range(4)]
                 + [("svalue", c) for c in range(4)] + [("compress", c) for c in range(8)]
                 + [("merge", c) for c in range(16)])
        assert len(kinds) == IN2
        ropes = [(t, t % 4, dst) for t, (kind, dst) in enumerate(kinds) if kind == "rope"]
        rope_of = {t: r for r, (t, _, _) in enumerate(ropes)}
        uses, before = [0] * 8, {}
        for t, (kind, c) in enumerate(kinds):
            if kind in ("value", "svalue"):
                banks = range(4, 8) if c == 0 else ()
            elif kind == "compress":
                banks = (4 + c // 4,) if c % 4 == 0 else ()
            else:
                banks = (t % 4,)
            before[t] = {b: uses[b] for b in banks}
            for b in banks:
                uses[b] += 1
        free_names = [f"bank_free{b}" for b in range(8)]
        with phase(nc, *free_names, "unrotated_ready", "rotated_ready", "rope_done", "plain_done",
                   "windows_ready", "hidden_ready", "second_done", "order", "aorder", run_ends=True) as (block, *sems):
            bank_free = sems[0:8]
            (unrotated_ready, rotated_ready, rope_done, plain_done, windows_ready, hidden_ready, second_done,
             order, aorder) = sems[8:]
            hc = [m.sq[:, 0, 0:32], m.sq[:, 0, 32:64]]

            @block.sync
            def _(sp):
                s.loads(sp, RING, IN2)

            @block.gpsimd
            def _(pool):
                s.rests(pool, 2, IN2)

            @block.tensor
            def _(pe):
                def rotate(t):
                    if t in rope_of:
                        r = rope_of[t]
                        pe.wait_ge(unrotated_ready, r + 1)
                        pe.matmul(ps[t % 4][:], rot, rawb2[:], start=True, stop=True).then_inc(rotated_ready, 1)

                for t, (kind, c) in enumerate(kinds):
                    s.ready(pe, t // RING, t % RING)
                    for b, n in before[t].items():
                        if n:
                            pe.wait_ge(bank_free[b], n)
                    if kind in ("value", "svalue"):
                        nw = VSW if kind == "value" else T
                        for kk in range(2):
                            k = 2 * c + kk
                            wc = slice(kk * T, kk * T + nw)
                            for tb in range(NT):
                                tc = slice(tb * P, (tb + 1) * P)
                                o = ps[4 + tb][:, 0:nw]
                                pe.matmul(o, m.hh[:, k, tc], m.wh[:, t % 2, wc], start=(k == 0), stop=False)
                                pe.matmul(o, m.hh[:, k, tc], m.wl[:, t % 2, wc], start=False, stop=False)
                                last = pe.matmul(o, m.hl[:, k, tc], m.wh[:, t % 2, wc], start=False,
                                                 stop=(k == KD - 1))
                    elif kind == "compress":
                        kv, q_ = c // 4, c % 4
                        pe.wait_ge(windows_ready, kv + 1)
                        for j in range(8):
                            wc = slice(j * P, (j + 1) * P)
                            jj = 8 * q_ + j
                            last = three_pass(pe, ps[4 + kv][:, 0:32], m.wh[:, t % 2, wc], m.wl[:, t % 2, wc],
                                              peh[kv][:, jj, :], pel[kv][:, jj, :], start=(jj == 0),
                                              stop=(jj == CB - 1))
                    else:
                        for k in range(KD):
                            wc = slice(k * P, (k + 1) * P)
                            last = three_pass(pe, ps[t % 4][:], m.wh[:, t % 2, wc], m.wl[:, t % 2, wc],
                                              m.hh[:, k, :], m.hl[:, k, :], start=(k == 0), stop=(k == KD - 1))
                    last.then_inc(s.slot_done, 1)
                    if t >= 1:
                        rotate(t - 1)
                    if kind == "merge" and c == 1:
                        pe.wait_ge(hidden_ready, 2)
                        pe.wait_ge(bank_free[6], uses[6])
                        pe.wait_ge(bank_free[7], uses[7])
                        pe.matmul(ps[6][:, 0:NCMP], m.pc[:, B_W2K:B_W2K + P], hc[0][:, 0:NCMP],
                                  start=True, stop=True)
                        pe.matmul(ps[7][0:NCMP, 0:P], hc[1][:, 0:NCMP], m.pc[:, B_W2V:B_W2V + P],
                                  start=True, stop=True).then_inc(second_done, 1)

            @block.scalar
            def _(act):
                for t, (kind, c) in enumerate(kinds):
                    s.heads(act, t + 2, t + 3)
                    act.wait_ge(s.slot_done, t + 1)
                    bank = ps[t % 4]
                    if kind == "rope":
                        r = rope_of[t]
                        if r:
                            act.wait_ge(rope_done, r)
                        act.activation(rawb2[:], bank[:], ACT.Copy).then_inc(unrotated_ready, 1)
                    if kind == "plain":
                        act.activation(c, bank[:], ACT.Copy).then_inc(bank_free[t % 4], 1)
                    if kind == "merge":
                        act.activation(gm[:, c, :], bank[:], ACT.Sigmoid).then_inc(bank_free[t % 4], 1)
                    if kind == "compress" and c % 4 == 3:
                        kv = c // 4
                        act.activation(hc[kv], ps[4 + kv][:, 0:32], ACT.Gelu_apprx_tanh,
                                       bias=m.pc[:, B_B1K + kv:B_B1K + kv + 1]).then_inc(hidden_ready, 1)

            @block.vector
            def _(dve):
                step = Signal(dve, order)
                for t, (kind, c) in enumerate(kinds):
                    if kind == "rope":
                        r = rope_of[t]
                        dve.wait_ge(unrotated_ready, r + 1)
                        step(dve.tensor_tensor(m.tmp[:, 0, :], rawb2[:], m.cos[:], ALU.mult))
                        dve.wait_ge(rotated_ready, r + 1)
                        step(dve.tensor_tensor(m.tmp[:, 1, :], ps[t % 4][:], m.sin[:], ALU.mult))
                        dve.sem_inc(bank_free[t % 4], 1)
                        dve.tensor_tensor(c, m.tmp[:, 0, :], m.tmp[:, 1, :], ALU.add).then_inc(rope_done, 1)
                        dve.wait_ge(rope_done, r + 1)
                    if kind in ("value", "svalue") and c == 3:
                        dve.wait_ge(s.slot_done, t + 1)
                        for tb in range(NT):
                            dst = vsw[:, tb, :] if kind == "value" else sv2[:, tb, :]
                            nw = VSW if kind == "value" else T
                            dve.tensor_copy(dst, ps[4 + tb][:, 0:nw]).then_inc(bank_free[4 + tb], 1)
                        dve.wait_ge(bank_free[4 + NT - 1], 1 if kind == "value" else 2)
                    if t == 9:
                        dve.wait_ge(bank_free[1], 2)
                        win = m.tmp[:].rearrange("p a (j n) -> p (a j) n", n=32)
                        for kv, src in enumerate((kc, vc)):
                            pe_col = m.pc[:, B_PEK + CB * kv:B_PEK + CB * (kv + 1)]
                            step(dve.memset(m.tmp[:], 0.0))
                            for half in range(2):
                                j0 = 16 * half
                                view = src[:, j0:j0 + 16 * NCMP].rearrange("p (n j) -> p j n", j=16)
                                step(dve.tensor_tensor(
                                    win[:, j0:j0 + 16, 0:NCMP], view,
                                    pe_col[:, j0:j0 + 16].unsqueeze(2).to_broadcast([P, 16, NCMP]), ALU.add))
                            step(dve.tensor_copy(peh[kv][:], win))
                            step(dve.tensor_tensor(pel[kv][:], win, peh[kv][:].bitcast(F32), ALU.subtract))
                            dve.sem_inc(windows_ready, 1)
                dve.wait_ge(second_done, 1)
                dve.tensor_copy(kct[:, 0:NCMP], ps[6][:, 0:NCMP])
                dve.tensor_copy(vct[0:NCMP, :], ps[7][0:NCMP, 0:P])

    w3 = Arena(nc, ring_at, RING_BYTES)
    sc3, pr3, pt3 = w3("sc3", [P, 3, T]), w3("pr3", [P, 3, T]), w3("pt3", [P, 2, T])
    lg, ng = w3("lg", [P, T]), w3("ng", [P, T])
    sm3 = w3("sm3", [P, 512])
    y3 = Arena(nc, y_at, KD * T * 4)
    o_nsa, o_sb = y3("o_nsa", [P, NT, T]), y3("o_sb", [P, NT, T])
    SCALE = HD ** -0.5

    def mixer2():
        items = [(kind, tb, h) for tb in range(NT) for h in range(HEADS) for kind in ("slc", "win", "sb")]
        N, PER_TB = len(items), 3 * HEADS
        soft_no = {}
        for i, (kind, tb, h) in enumerate(items):
            if kind != "sb":
                soft_no[i] = (0 if kind == "slc" else 32) + HEADS * tb + h
        sb_no = {i: n for n, i in enumerate(i for i, it in enumerate(items) if it[0] == "sb")}
        soft_rank = {i: n for n, i in enumerate(i for i, it in enumerate(items) if it[0] != "sb")}
        mxs, nmx, den = sm3[:, 0:64], sm3[:, 64:128], sm3[:, 128:192]
        gts = sm3[:, 192:288].rearrange("p (b h c) -> p b h c", b=NT, c=3)
        cneg = sm3[:, 288:288 + 32 * NT].rearrange("p (b n) -> p b n", b=NT)
        t8 = sm3[:, 416:448]
        o_bank = {"slc": 5, "win": 6, "sb": 7}
        names = ("gates", "cscore", "cshift", "cexp", "cweights", "cturned", "cturned_copied", "cpv", "cout",
                 "score", "sfree0", "sfree1", "sfree2", "soft_in", "logs", "neg_ready", "neg_masked", "raw_weights",
                 "weights_masked", "turned", "turned_copied", "pv", "out_copied", "o_ready", "feat_turned",
                 "feat_used", "order", "aorder")
        with phase(nc, *names) as (block, *sems):
            (gates, cscore, cshift, cexp, cweights, cturned, cturned_copied, cpv, cout, score, sf0, sf1, sf2,
             soft_in, logs, neg_ready, neg_masked, raw_weights, weights_masked, turned, turned_copied, pv,
             out_copied, o_ready, feat_turned, feat_used, order, aorder) = sems
            sfree = (sf0, sf1, sf2)
            cs = sc3[:, 0, 0:HEADS * NCMP].rearrange("p (h n) -> p h n", h=HEADS)
            ptc = pt3[:].rearrange("p a t -> p (a t)")

            def heads(h):
                return slice(64 * (h // 4), 64 * (h // 4) + 64), h % 4

            @block.tensor
            def _(pe):
                for tb in range(NT):
                    if tb:
                        pe.wait_ge(cshift, tb)
                    for h in range(HEADS):
                        r, b = heads(h)
                        ins = pe.matmul(ps[h // 4][:, (h % 4) * 32:(h % 4) * 32 + NCMP], q2[r, b, tb * P:(tb + 1) * P],
                                        kct[r, 0:NCMP], start=True, stop=True)
                    ins.then_inc(cscore, 1)
                    pe.wait_ge(cweights, tb + 1)
                    for h in range(HEADS):
                        ins = pe.transpose(ps[2 + h // 4][0:NCMP, (h % 4) * P:(h % 4 + 1) * P], cs[:, h, :], ident)
                    ins.then_inc(cturned, 1)
                    pe.wait_ge(cturned_copied, 2 * tb + 2)
                    if tb:
                        pe.wait_ge(cout, tb)
                    for h in range(HEADS):
                        ins = pe.matmul(ps[5][:, h * HD:(h + 1) * HD], ptc[0:NCMP, h * P:(h + 1) * P],
                                        vct[0:NCMP, 64 * (h // 4):64 * (h // 4) + 64], start=True, stop=True)
                    ins.then_inc(cpv, 1)
                pe.wait_ge(cout, NT)

                def scores(i):
                    kind, tb, h = items[i]
                    if i >= 3:
                        pe.wait_ge(sfree[i % 3], i // 3)
                    w_ = (tb + 1) * P
                    if kind == "sb":
                        r = slice(64 * (h % 2), 64 * (h % 2) + 64)
                        q_, k_ = sq2[r, h // 2, tb * P:(tb + 1) * P], sk2[r, h // 2, 0:w_]
                    else:
                        r, b = heads(h)
                        q_, k_ = q2[r, b, tb * P:(tb + 1) * P], (ksl if kind == "slc" else kwn)[r, 0:w_]
                    pe.matmul(ps[i % 3][:, 0:w_], q_, k_, start=True, stop=True).then_inc(score, 1)

                def turn(i):
                    kind, tb, h = items[i]
                    if kind == "sb":
                        pe.wait_ge(weights_masked, sb_no[i] + 1)
                    else:
                        pe.wait_ge(raw_weights, i + 1)
                    if i >= 2:
                        pe.wait_ge(turned_copied, i - 1)
                    for kb in range(tb + 1):
                        ins = pe.transpose(ps[3 + i % 2][:, kb * P:(kb + 1) * P],
                                           pr3[:, i % 3, kb * P:(kb + 1) * P], ident)
                    ins.then_inc(turned, 1)

                def values(i):
                    kind, tb, h = items[i]
                    pe.wait_ge(turned_copied, i + 1)
                    if h == 0 and kind == "slc" and tb:
                        pe.wait_ge(out_copied, 3 * tb)
                    for kb in range(tb + 1):
                        if kind == "sb":
                            v_ = sv2[:, kb, h * HD:(h + 1) * HD]
                        else:
                            v0 = (0 if kind == "slc" else P) + 64 * (h // 4)
                            v_ = vsw[:, kb, v0:v0 + HD]
                        ins = pe.matmul(ps[o_bank[kind]][:, h * HD:(h + 1) * HD],
                                        pt3[:, i % 2, kb * P:(kb + 1) * P], v_, start=(kb == 0), stop=(kb == tb))
                    ins.then_inc(pv, 1)
                for i in range(N + 4):
                    if i < N:
                        scores(i)
                    if 0 <= i - 3 < N:
                        turn(i - 3)
                    if 0 <= i - 4 < N:
                        values(i - 4)
                for g in range(2 * NT):
                    pe.wait_ge(o_ready, g % NT + 1)
                    if g >= 2:
                        pe.wait_ge(feat_used, g - 1)
                    src = (o_nsa if g < NT else o_sb)[:, g % NT, :]
                    for c in range(4):
                        ins = pe.transpose(ps[g % 2][:, c * P:(c + 1) * P], src[:, c * P:(c + 1) * P], ident)
                    ins.then_inc(feat_turned, 1)

            @block.scalar
            def _(act):
                step = Signal(act, aorder)
                act.activation(sm3[:, 192:288].rearrange("p (b c) -> p b c", b=NT), vsw[:, :, 256:280],
                               ACT.Sigmoid).then_inc(gates, 1)
                for tb in range(NT):
                    act.wait_ge(cshift, tb + 1)
                    act.activation(sc3[:, 0, 0:HEADS * NCMP], sc3[:, 0, 0:HEADS * NCMP], ACT.Exp, scale=SCALE)\
                       .then_inc(cexp, 1)
                    act.wait_ge(cturned, tb + 1)
                    if tb:
                        act.wait_ge(cpv, tb)
                    for half in range(2):
                        act.activation(ptc[0:NCMP, half * T:(half + 1) * T], ps[2 + half][0:NCMP, :], ACT.Copy)\
                           .then_inc(cturned_copied, 1)

                def log(i):
                    kind, tb, h = items[i]
                    w_ = (tb + 1) * P
                    act.wait_ge(score, i + 1)
                    if sb_no[i]:
                        act.wait_ge(neg_ready, sb_no[i])
                    step(act.activation(lg[:, 0:w_], ps[i % 3][:, 0:w_], ACT.Abs, scale=SCALE))
                    step(act.activation(lg[:, 0:w_], lg[:, 0:w_], ACT.Exp, scale=-1.0))
                    act.activation(lg[:, 0:w_], lg[:, 0:w_], ACT.Ln, bias=1.0).then_inc(logs, 1)

                def exps(i):
                    kind, tb, h = items[i]
                    w_ = (tb + 1) * P
                    if i >= 3:
                        act.wait_ge(turned, i - 2)
                    if kind == "sb":
                        act.wait_ge(sfree[i % 3], i // 3 + 1)
                        act.activation(pr3[:, i % 3, 0:w_], sc3[:, i % 3, 0:w_], ACT.Exp).then_inc(raw_weights, 1)
                    else:
                        n = soft_no[i]
                        act.wait_ge(soft_in, soft_rank[i] + 1)
                        act.activation(pr3[:, i % 3, 0:w_], sc3[:, i % 3, 0:w_], ACT.Exp, bias=nmx[:, n:n + 1],
                                       scale=SCALE, accum_out=den[:, n:n + 1]).then_inc(raw_weights, 1)

                def copy_turned(i):
                    w_ = (items[i][1] + 1) * P
                    act.wait_ge(turned, i + 1)
                    if i >= 2:
                        act.wait_ge(pv, i - 1)
                    act.activation(pt3[:, i % 2, 0:w_], ps[3 + i % 2][:, 0:w_], ACT.Copy).then_inc(turned_copied, 1)
                for i in range(N + 4):
                    if i < N and items[i][0] == "sb":
                        log(i)
                    if 0 <= i - 2 < N:
                        exps(i - 2)
                    if 0 <= i - 4 < N:
                        copy_turned(i - 4)

            @block.gpsimd
            def _(pool):
                sbs = [i for i, it in enumerate(items) if it[0] == "sb"]

                def strict(ap):
                    return pool.affine_select(out=ap, in_=ap, compare_op=ALU.is_gt, fill=0.0, base=0,
                                              pattern=[[-1, P]], channel_multiplier=1)
                for n, i in enumerate(sbs):
                    d = slice(items[i][1] * P, (items[i][1] + 1) * P)
                    pool.wait_ge(neg_ready, n + 1)
                    strict(ng[:, d]).then_inc(neg_masked, 1)
                    pool.wait_ge(raw_weights, i + 1)
                    strict(pr3[:, i % 3, d]).then_inc(weights_masked, 1)

            @block.vector
            def _(dve):
                step = Signal(dve, order)
                S = lambda sem: Signal(dve, sem)
                shift, cw, co, sin_, neg, ocop, oready, fused = (S(x) for x in (
                    cshift, cweights, cout, soft_in, neg_ready, out_copied, o_ready, feat_used))
                free = [S(x) for x in sfree]
                bc = lambda c, n_: c.unsqueeze(2).to_broadcast([P, HEADS, n_])
                cm = m.cst[:, C_CMP:C_CMP + 32 * NT].rearrange("p (b n) -> p b n", b=NT)
                step(dve.tensor_scalar(cneg, cm, 1.0, -NEG, ALU.subtract, ALU.mult))
                for tb in range(NT):
                    dve.wait_ge(cscore, tb + 1)
                    for half in range(2):
                        zs = ps[half][:, 0:P].rearrange("p (h n) -> p h n", h=4)[:, :, 0:NCMP]
                        step(dve.tensor_tensor(cs[:, 4 * half:4 * half + 4, :], zs,
                                               cneg[:, tb, 0:NCMP].unsqueeze(1).to_broadcast([P, 4, NCMP]),
                                               ALU.add))
                    step(dve.tensor_reduce(t8[:, 0:8], cs, AX_X, ALU.max))
                    shift(dve.tensor_tensor(cs, cs, bc(t8[:, 0:8], NCMP), ALU.subtract))
                    dve.wait_ge(cexp, tb + 1)
                    step(dve.tensor_reduce(t8[:, 8:16], cs, AX_X, ALU.add))
                    cw(dve.tensor_tensor(cs, cs, cm[:, tb, 0:NCMP].unsqueeze(1).to_broadcast([P, HEADS, NCMP]),
                                         ALU.mult))
                    step(dve.reciprocal(t8[:, 8:16], t8[:, 8:16]))
                    if tb == 0:
                        dve.wait_ge(gates, 1)
                    step(dve.tensor_tensor(t8[:, 8:16], t8[:, 8:16], gts[:, tb, :, 0], ALU.mult))
                    dve.wait_ge(cpv, tb + 1)
                    co(dve.tensor_tensor(o_nsa[:, tb, :].rearrange("p (h d) -> p h d", h=HEADS),
                                         ps[5][:].rearrange("p (h d) -> p h d", h=HEADS), bc(t8[:, 8:16], HD),
                                         ALU.mult))

                def first(i):
                    kind, tb, h = items[i]
                    w_ = (tb + 1) * P
                    bank = ps[i % 3][:, 0:w_]
                    if kind == "sb":
                        dve.wait_ge(logs, sb_no[i] + 1)
                        step(dve.tensor_scalar(ng[:, 0:w_], bank, SCALE, 0.0, ALU.mult, ALU.max))
                        neg(dve.scalar_tensor_tensor(ng[:, 0:w_], ng[:, 0:w_], -1.0, lg[:, 0:w_],
                                                     ALU.mult, ALU.subtract))
                    else:
                        n = soft_no[i]
                        if i >= 3:
                            dve.wait_ge(raw_weights, i - 2)
                        dve.wait_ge(score, i + 1)
                        free[i % 3](dve.tensor_tensor_reduce(sc3[:, i % 3, 0:w_], bank, causal(tb), 1.0, TAKEN,
                                                             ALU.add, ALU.max, mxs[:, n:n + 1]))
                        sin_(dve.tensor_scalar(nmx[:, n:n + 1], mxs[:, n:n + 1], -SCALE, None, ALU.mult))

                def second(i):
                    kind, tb, h = items[i]
                    w_ = (tb + 1) * P
                    if kind != "sb":
                        return
                    dve.wait_ge(neg_masked, sb_no[i] + 1)
                    if i >= 3:
                        dve.wait_ge(raw_weights, i - 2)
                    one = m.sq[:, 1, 0:w_]
                    rev = slice(w_ - 1, None, -1)
                    step(dve.tensor_tensor_scan(sc3[:, i % 3, 0:w_][:, ::-1], one, ng[:, 0:w_][:, ::-1], 0.0,
                                                ALU.mult, ALU.add))
                    free[i % 3](dve.scalar_tensor_tensor(sc3[:, i % 3, 0:w_], ps[i % 3][:, 0:w_], SCALE,
                                                         sc3[:, i % 3, 0:w_], ALU.mult, ALU.add))

                def finish(tb):
                    dve.wait_ge(pv, PER_TB * (tb + 1))
                    v3 = lambda a_: a_.rearrange("p (h d) -> p h d", h=HEADS)
                    for n, kind in enumerate(("slc", "win")):
                        col = t8[:, 16:24]
                        step(dve.reciprocal(col, den[:, 32 * n + 8 * tb:32 * n + 8 * tb + 8]))
                        step(dve.tensor_tensor(col, col, gts[:, tb, :, n + 1], ALU.mult))
                        ocop(dve.tensor_tensor(v3(m.tmp[:, 0, :]), v3(ps[o_bank[kind]][:]), bc(col, HD), ALU.mult))
                        step(dve.tensor_tensor(o_nsa[:, tb, :], o_nsa[:, tb, :], m.tmp[:, 0, :], ALU.add))
                    ocop(dve.tensor_copy(o_sb[:, tb, :], ps[7][:]))
                    dve.sem_inc(o_ready, 1)
                step(dve.memset(m.sq[:, 1, :], 1.0))
                for i in range(N + 4):
                    if i < N:
                        first(i)
                    if 0 <= i - 1 < N:
                        second(i - 1)
                    if i >= PER_TB and i % PER_TB == 3:
                        finish(i // PER_TB - 1)
                for g in range(2 * NT):
                    tb = g % NT
                    dve.wait_ge(feat_turned, g + 1)
                    src = ps[g % 2][:].rearrange("p (c t) -> p c t", c=4)
                    c0 = 0 if g < NT else 4
                    ts_ = slice(tb * P, (tb + 1) * P)
                    step(dve.tensor_copy(m.hh[:, c0:c0 + 4, ts_], src))
                    fused(dve.tensor_tensor(m.hl[:, c0:c0 + 4, ts_], src, m.hh[:, c0:c0 + 4, ts_].bitcast(F32),
                                            ALU.subtract))

    def merge2(s):
        with phase(nc, "bank_free", "order", "sum_ready", "head_written") as \
                (block, bank_free, order, sum_ready, head_written):

            @block.sync
            def _(sp):
                s.loads(sp, 0, PROJ + RING)

            @block.gpsimd
            def _(pool):
                s.rests(pool, 0, PROJ + 2)

            @block.tensor
            def _(pe):
                for t in range(PROJ):
                    s.ready(pe, t // RING, t % RING)
                    for half in range(2):
                        n = 2 * t + half
                        if n >= 4:
                            pe.wait_ge(bank_free, n - 3)
                        for k in range(4):
                            wc = slice(k * 256 + half * P, k * 256 + half * P + P)
                            xk = k + 4 * (t // 4)
                            last = three_pass(pe, ps[n % 4][:], m.wh[:, t % 2, wc], m.wl[:, t % 2, wc],
                                              m.hh[:, xk, :], m.hl[:, xk, :], start=(k == 0), stop=(k == 3))
                    last.then_inc(s.slot_done, 1)

            @block.scalar
            def _(act):
                s.heads(act, 0, PROJ + 2)
                act.wait_ge(s.slot_done, PROJ)
                for k in range(KD):
                    act.wait_ge(sum_ready, k + 1)
                    act.activation(m.hh[:, k, :], m.y[:, k, :], ACT.Copy).then_inc(head_written, 1)

            @block.vector
            def _(dve):
                step = Signal(dve, order)
                for n in range(2 * KD):
                    dve.wait_ge(s.slot_done, n // 2 + 1)
                    dst = m.y[:, n, :] if n < KD else m.tmp[:, 0, :]
                    dve.tensor_tensor(dst, ps[n % 4][:], gm[:, n, :], ALU.mult).then_inc(bank_free, 1)
                    if n >= KD:
                        dve.wait_ge(bank_free, n + 1)
                        dve.tensor_tensor(m.y[:, n - KD, :], m.y[:, n - KD, :], m.tmp[:, 0, :], ALU.add)\
                           .then_inc(sum_ready, 1)
                        dve.wait_ge(sum_ready, n - KD + 1)
                for k in range(KD):
                    dve.wait_ge(head_written, k + 1)
                    dve.tensor_tensor(m.hl[:, k, :], m.y[:, k, :], m.hh[:, k, :].bitcast(F32), ALU.subtract)


    return locals()


def program(nc, a, out):
    env = build(nc, a, out)
    m, junction = env["m"], env["junction"]

    def col(at):
        return m.pc[:, at:at + KD]

    def mod(i):
        return m.mod[:, KD * i:KD * (i + 1)]
    env["rope_tables"]("pos1")
    run, ff_run = env["run"], env["ff_run"]
    with nc.Fori(0, LAYERS) as l:
        w, at = a["w1"], l * SL1
        env["modulation"](a["wmod"], l * 48, a["pcA"][l])
        ins = run(w, at, IN1)
        junction("a", pre=(col(A_PRE), mod(1), mod(0)), ahead=ins)
        env["in_products1"](ins)
        env["mixer1"]()
        env["product_out"](run(w, at + IN1, OUT), 0, 1, KD, m.hh, m.hl, started=False)
        ff = ff_run(w, at + IN1 + OUT)
        junction("b", post=(col(A_POST), mod(2)), pre=(col(A_FPRE), mod(4), mod(3)), ahead=ff)
        env["feed_forward"]("a", ff, False)
        junction("c", post=(col(A_FPOST), mod(5)))
    env["rope_tables"]("pos2")
    with nc.Fori(0, LAYERS) as l:
        w, at = a["w2"], l * SL2
        env["params2"](a["pcB"][l])
        ins = run(w, at, IN2)
        junction("d", pre=(col(B_PRE), None, None), ahead=ins)
        env["in_products2"](ins)
        env["mixer2"]()
        outs = run(w, at + IN2, PROJ + OUT)
        env["merge2"](outs)
        env["product_out"](outs, PROJ, 1, KD, m.hh, m.hl)
        ff = ff_run(w, at + IN2 + PROJ + OUT)
        junction("e", post=(col(B_POST), None), pre=(col(B_FPRE), None, None), ahead=ff)
        env["feed_forward"]("d", ff, True)
        junction("f", post=(col(B_FPOST), None))
    with phase(nc, "stored") as (block, stored):
        @block.sync
        def _(sp):
            sp.dma_start(out, m.x[:]).then_inc(stored, 16)
            sp.wait_ge(stored, 16)


def _cols(v, n=None):
    return np.asarray(v).reshape(-1, P).T


def _feature(w, n0, n=P):
    k = w.shape[0] // P
    return w[:, n0:n0 + P].reshape(k, P, P).transpose(1, 0, 2).reshape(P, k * P)


def _token(w):
    return [w[256 * j:256 * j + 256].reshape(2, P, T).transpose(1, 0, 2).reshape(P, SLOT) for j in range(4)]


def _place(cols, at, width, dtype):
    out = np.zeros((cols[0].shape[0], width), dtype)
    for c, o in zip(cols, at):
        out[:, o:o + c.shape[1]] = c
    return out


def _down(w):
    out = []
    for nb in range(KD):
        for part in range(3):
            k0, k1 = 8 * part, min(8 * part + 8, KF)
            s = np.zeros((P, SLOT), w.dtype)
            s[:, :(k1 - k0) * P] = _feature(w[k0 * P:k1 * P], nb * P)
            out.append(s)
    return out


def _gate_up(w):
    out = []
    for mblk in range(KF):
        out += [_feature(w, mblk * P), _feature(w, FF + mblk * P)]
    return out


def _constants():
    c = np.zeros((P, C_COLS), np.float32)
    c[:, C_ID:C_ID + P] = np.eye(P)
    for p in range(P):
        if p % 64 < 32:
            c[p + 32, C_ROT + p] = -1.0
        else:
            c[p - 32, C_ROT + p] = 1.0
    q, k = np.arange(P)[:, None], np.arange(P)[None, :]
    c[:, C_CAUSAL + 3 * P:C_CAUSAL + T] = np.where(k > q, NEG, 0.0)
    c[:, C_ONES:C_ONES + P] = 1.0
    for h in range(MH):
        c[h, C_SEL + h * P:C_SEL + (h + 1) * P] = 1.0
    half = np.float32(10000.0) ** (-np.arange(32, dtype=np.float32) / np.float32(32))
    c[:, C_FREQ] = half[np.arange(P) % 32]
    for tb in range(NT):
        t = tb * P + np.arange(P)[:, None]
        n = np.arange(32)[None, :]
        c[:, C_CMP + 32 * tb:C_CMP + 32 * tb + 32] = (n * 16 + 31 <= t) & (n < NCMP)
    return c


def _layout(i):
    f = np.float32
    a = {"x": i["x"][0].T.reshape(KD, P, T).transpose(1, 0, 2), "cst": _constants(), "c": i["c"],
         "pos1": i["positions"], "pos2": i["positions_2"]}
    a["wmod"] = np.concatenate([i["w_mod"][l].T.reshape(48, P, D) for l in range(LAYERS)])
    w1, pa, w2, pb = [], [], [], []
    for l in range(LAYERS):
        w = i["w_in"][l]
        o = np.cumsum([0, 256, 512, 512, 64, 8, 512, 512, 512, 512, 4, 4])
        s = [_feature(w, 128 * c) for c in range(2)] + [_feature(w, o[1] + 128 * c) for c in range(4)]
        kid = w[:, o[3]:o[4]]
        s.append(_feature(np.concatenate([kid, kid], 1), 0))
        s.append(_feature(_place([w[:, o[4]:o[5]], w[:, o[9]:o[10]], w[:, o[10]:o[11]]], [0, 32, 64], P, f), 0))
        s += [_feature(w, o[5] + 128 * c) for c in range(8)]
        s += [_feature(w, o[8] + 128 * c) for c in range(4)]
        s += _token(w[:, o[2]:o[3]]) + _token(w[:, o[7]:o[8]])
        for up in (i["w_q_up"][l], i["w_qidx_up"][l]):
            s.append(up.reshape(2, P, T).transpose(1, 0, 2).reshape(P, SLOT))
        s += [_feature(i["w_out"][l], 128 * c) for c in range(KD)]
        s += _gate_up(i["w_gate_up"][l]) + _down(i["w_down"][l])
        assert len(s) == SL1
        w1 += s
        pc = np.zeros((P, A_COLS), f)
        for at, v in ((A_PRE, "mix_norm_pre"), (A_POST, "mix_norm_post"), (A_FPRE, "ffn_norm_pre"),
                      (A_FPOST, "ffn_norm_post"), (A_BMOD, "b_mod"), (A_QN, "q_latent_norm"), (A_CW, "conv_w"),
                      (A_CB, "conv_b"), (A_AN, "attn_out_norm"), (A_MN, "mlstm_out_norm")):
            v = _cols(i[v][l])
            pc[:, at:at + v.shape[1]] = v
        pc[:MH, A_BI], pc[:MH, A_BF] = i["b_igate"][l], i["b_fgate"][l]
        pa.append(pc)

        w = i["w_in_2"][l]
        o = np.cumsum([0, 512, 768, 24, 1536, 2048])
        heads = [w[:, 64 * h:64 * h + 64] for h in range(HEADS)]
        q = np.concatenate([heads[h] for pair in range(4) for h in (pair, 4 + pair)], 1)
        kv = [w[:, o[1] + 128 * c:o[1] + 128 * c + 128] for c in range(6)]
        s = [_feature(q, 128 * c) for c in range(4)]
        s += [_feature(kv[c], 0) for c in (0, 1, 2, 4)]
        s += _token(_place([kv[3], kv[5], w[:, o[2]:o[3]]], [0, 128, 256], T, f))
        s += [_feature(w, o[3] + 128 * c) for c in range(8)]
        s += _token(w[:, o[3] + 1024:o[4]])
        for w1_ in (i["ck_w1_2"][l], i["cv_w1_2"][l]):
            bd = np.zeros((P, CB, P), f)
            for h in range(2):
                bd[64 * h:64 * h + 64, :, 64 * h:64 * h + 64] = w1_.reshape(CB, HD, HD).transpose(1, 0, 2)
            s += [bd[:, 8 * j:8 * j + 8].reshape(P, SLOT) for j in range(4)]
        s += [_feature(w, o[4] + 128 * c) for c in range(16)]
        for wp in (i["w_proj_nsa_2"][l], i["w_proj_sb_2"][l]):
            s += [wp[:, 256 * j:256 * j + 256].reshape(4, P, 256).transpose(1, 0, 2).reshape(P, SLOT)
                  for j in range(4)]
        s += [_feature(i["w_out_2"][l], 128 * c) for c in range(KD)]
        s += _gate_up(i["w_up_2"][l]) + _down(i["w_down_2"][l])
        assert len(s) == SL2, (len(s), SL2)
        w2 += s
        pc = np.zeros((P, B_COLS), f)
        for at, v in ((B_PRE, "g_pre_mix_2"), (B_POST, "g_post_mix_2"), (B_FPRE, "g_pre_ffn_2"),
                      (B_FPOST, "g_post_ffn_2"), (B_CW, "conv_w_2"), (B_CB, "conv_b_2")):
            v = _cols(i[v][l])
            pc[:, at:at + v.shape[1]] = v
        for h in range(2):
            r = slice(64 * h, 64 * h + 64)
            pc[r, B_B1K], pc[r, B_B1V] = i["ck_b1_2"][l], i["cv_b1_2"][l]
            pc[r, B_PEK:B_PEK + CB], pc[r, B_PEV:B_PEV + CB] = i["ck_pe_2"][l].T, i["cv_pe_2"][l].T
            pc[r, B_W2K + 64 * h:B_W2K + 64 * h + 64] = i["ck_w2_2"][l]
            pc[r, B_W2V + 64 * h:B_W2V + 64 * h + 64] = i["cv_w2_2"][l]
        pb.append(pc)
    a["w1"], a["w2"], a["pcA"], a["pcB"] = np.stack(w1), np.stack(w2), np.stack(pa), np.stack(pb)
    return {k: np.ascontiguousarray(v) for k, v in a.items()}


def kernel(**inputs):
    import concourse.bacc as bacc
    from concourse.bass_utils import run_bass_kernel_spmd

    nc = bacc.Bacc("TRN2", target_bir_lowering=False, num_devices=1)
    arrays = _layout({k: np.asarray(v) for k, v in inputs.items()})
    a = {k: nc.dram_tensor(f"in_{k}", v.shape, mybir.dt.from_np(v.dtype), kind="ExternalInput").ap()
         for k, v in arrays.items()}
    out = nc.dram_tensor("out_xT", (P, KD, T), F32, kind="ExternalOutput").ap()
    program(nc, a, out)
    r = run_bass_kernel_spmd(nc, [{f"in_{k}": v for k, v in arrays.items()}], core_ids=[0])
    got = r.results[0]["out_xT"]
    return got.transpose(2, 1, 0).reshape(1, T, D)
```

```python
from contextlib import ExitStack, contextmanager

import concourse.bass as bass
import numpy as np
from concourse import mybir

F32 = mybir.dt.float32
F32R = mybir.dt.float32r
I32 = mybir.dt.int32
ALU = mybir.AluOpType
ACT = mybir.ActivationFunctionType
AX_X = mybir.AxisListType.X

P = 128
T = 512
D = 1024
KD = D // P
NT = T // P
LAYERS = 2
STREAM_SEM, FIRST_SEM = 193, 200
FF = 2816
KF = FF // P
SLOT = 1024
RING = 4
EPS = 1e-6
HEADS = 8
HD = 64
MH = 4
MD = 128
QR = 256
TOPK = T // 4
NCMP = (T - 32) // 16 + 1
CB = 32
NEG = -1e30
TAKEN = -3e38

IN1, GU, DN, OUT = 30, 2 * KF, 3 * KD, KD
IN2, PROJ = 48, 8
SL1 = IN1 + OUT + GU + DN
SL2 = IN2 + PROJ + OUT + GU + DN

C_ID, C_ROT, C_CAUSAL, C_ONES, C_SEL, C_FREQ, C_CMP = 0, 128, 256, 768, 896, 1408, 1409
C_COLS = 1409 + NT * 32

A_PRE, A_POST, A_FPRE, A_FPOST, A_BMOD, A_QN, A_CW, A_CB, A_AN, A_MN, A_BI, A_BF = (
    0, 8, 16, 24, 32, 80, 82, 114, 122, 126, 130, 131)
A_COLS = 132
B_PRE, B_POST, B_FPRE, B_FPOST, B_CW, B_CB, B_B1K, B_B1V, B_PEK, B_PEV, B_W2K, B_W2V = (
    0, 8, 16, 24, 32, 164, 208, 209, 210, 242, 274, 402)
B_COLS = 530


@contextmanager
def phase(nc, *names, run_ends=False):
    with ExitStack() as ctx:
        sems = [ctx.enter_context(nc.semaphore(n, num=FIRST_SEM + k)) for k, n in enumerate(names)]
        with nc.Block() as block:
            yield (block, *sems)
        first = STREAM_SEM if run_ends else FIRST_SEM
        nc.all_engine_barrier(sems_to_clear=range(first, FIRST_SEM + len(names)))


class Arena:

    def __init__(self, nc, base, size):
        self.nc, self.at, self.end = nc, base, base + size

    def __call__(self, name, shape, dt=F32):
        size = 4 * int(np.prod(shape[1:]))
        t = self.nc.alloc_sbuf_tensor_at(name, shape, dt, offset=self.at)
        self.at += -(-size // 32) * 32
        assert self.at <= self.end, (name, self.at, self.end)
        return t


class Signal:

    def __init__(self, eng, sem):
        self.eng, self.sem, self.n = eng, sem, 0

    def __call__(self, ins):
        self.n += 1
        ins.then_inc(self.sem, 1)
        self.eng.wait_ge(self.sem, self.n)


class Mem:
    pass


STREAM = ("w_in0", "w_in1", "w_in2", "w_in3", "head_ready", "rest_ready", "slot_done")


class Stream:

    def __init__(self, mem, w, base, total, sems, width=lambda t: SLOT):
        self.m, self.w, self.base, self.total, self.width = mem, w, base, total, width
        self.w_in, (self.head_ready, self.rest_ready, self.slot_done) = sems[:4], sems[4:7]

    def load(self, sp, i, j, width=SLOT):
        n = i * RING + j + self.base
        src = self.w[n if isinstance(n, int) else sp.snap(n)]
        if not (isinstance(i, int) and i == 0):
            sp.wait_ge(self.rest_ready, RING * i + j + 1 - RING)
        sp.dma_start(self.m.raw[:, j, 0:width], src[:, 0:width]).then_inc(self.w_in[j], 16)

    def head(self, act, i, j, width=SLOT):
        act.wait_ge(self.w_in[j], i * 16 + 16)
        if not (isinstance(i, int) and RING * i + j < 2):
            act.wait_ge(self.slot_done, RING * i + j - 1)
        act.activation(self.m.wh[:, j % 2, 0:width], self.m.raw[:, j, 0:width], ACT.Copy)\
           .then_inc(self.head_ready, 1)

    def rest(self, pool, i, j, width=SLOT):
        pool.wait_ge(self.head_ready, RING * i + j + 1)
        pool.tensor_tensor(self.m.wl[:, j % 2, 0:width], self.m.raw[:, j, 0:width],
                           self.m.wh[:, j % 2, 0:width].bitcast(F32), ALU.subtract)\
            .then_inc(self.rest_ready, 1)

    def ready(self, pe, i, j):
        pe.wait_ge(self.rest_ready, RING * i + j + 1)

    def loads(self, sp, t0, t1):
        for t in range(t0, min(t1, self.total)):
            self.load(sp, t // RING, t % RING, self.width(t))

    def heads(self, act, t0, t1):
        for t in range(t0, min(t1, self.total)):
            self.head(act, t // RING, t % RING, self.width(t))

    def rests(self, pool, t0, t1):
        for t in range(t0, min(t1, self.total)):
            self.rest(pool, t // RING, t % RING, self.width(t))


def three_pass(pe, out, wh, wl, xh, xl, start, stop):
    pe.matmul(out, wh, xh, start=start, stop=False)
    pe.matmul(out, wh, xl, start=False, stop=False)
    return pe.matmul(out, wl, xh, start=False, stop=stop)


def build(nc, a, out):
    m = Mem()
    base0 = -(-nc.sbuf_base // 32) * 32
    total = nc.sbuf_usable_end // 32 * 32 - base0
    MIX = KF * T * 4 * 2
    fixed = Arena(nc, base0, total - MIX)
    mix0 = base0 + total - MIX
    m.x = fixed("x", [P, KD, T])
    m.hh = fixed("hh", [P, KD, T], F32R)
    m.hl = fixed("hl", [P, KD, T], F32R)
    y_at = fixed.at
    m.y = fixed("y", [P, KD, T])
    ring_at = fixed.at
    m.raw = fixed("raw", [P, RING, SLOT])
    m.wh = fixed("wh", [P, 2, SLOT], F32R)
    m.wl = fixed("wl", [P, 2, SLOT], F32R)
    RING_BYTES = fixed.at - ring_at
    m.cst = fixed("cst", [P, C_COLS])
    m.pc = fixed("pc", [P, B_COLS])
    m.mod = fixed("mod", [P, 48])
    m.col = fixed("col", [P, 32])
    m.eps = fixed("eps", [P, 2])
    m.cos = fixed("cos", [P, T])
    m.sin = fixed("sin", [P, T])
    m.sq = fixed("sq", [P, 2, T])
    m.acc = fixed("acc", [P, T])
    m.tmp = fixed("tmp", [P, 2, T])

    ident = m.cst[:, C_ID:C_ID + P]
    rot = m.cst[:, C_ROT:C_ROT + P]
    ones = m.cst[:, C_ONES:C_ONES + P]
    freq = m.cst[:, C_FREQ:C_FREQ + 1]

    ps = [nc.alloc_psum_tensor(f"bank{i}", [P, T], F32) for i in range(8)]

    def causal(tb):
        return m.cst[:, C_CAUSAL + (NT - 1 - tb) * P:C_CAUSAL + T]

    with phase(nc, "loaded", "eps_set") as (block, loaded, eps_set):
        @block.sync
        def _(sp):
            sp.dma_start(m.x[:], a["x"]).then_inc(loaded, 16)
            sp.dma_start(m.cst[:], a["cst"]).then_inc(loaded, 16)
            sp.wait_ge(loaded, 32)

        @block.vector
        def _(dve):
            dve.memset(m.eps[:, 0:1], EPS).then_inc(eps_set, 1)
            dve.memset(m.eps[:, 1:2], 0.0).then_inc(eps_set, 1)

    def rope_tables(pos):
        TWO_PI = 2 * np.pi
        c1 = float(np.float32(np.round(TWO_PI * 512) / 512))
        c2 = float(np.float32(np.round((TWO_PI - c1) * 2 ** 22) / 2 ** 22))
        c3 = float(np.float32(TWO_PI - c1 - c2))
        MAGIC = 1.5 * 2.0 ** 23
        ar = Arena(nc, y_at, KD * T * 4)
        posi, ang = ar("posi" + pos, [P, T], I32), ar("ang" + pos, [P, T])
        k, r = ar("turns" + pos, [P, T]), ar("rest" + pos, [P, T])
        with phase(nc, "loaded", "reduced", "order") as (block, loaded, reduced, order):
            @block.sync
            def _(sp):
                sp.dma_start(posi[:], a[pos].partition_broadcast(P)).then_inc(loaded, 16)

            @block.vector
            def _(dve):
                step, done = Signal(dve, order), Signal(dve, reduced)
                dve.wait_ge(loaded, 16)
                step(dve.tensor_copy(ang[:], posi[:]))
                step(dve.tensor_scalar(ang[:], ang[:], freq, None, ALU.mult))
                for quarter, dst in ((0.0, m.sin), (0.25, m.cos)):
                    step(dve.tensor_scalar(k[:], ang[:], 1 / TWO_PI, quarter, ALU.mult, ALU.add))
                    step(dve.tensor_scalar(k[:], k[:], MAGIC, None, ALU.add))
                    step(dve.tensor_scalar(k[:], k[:], -MAGIC, None, ALU.add))
                    step(dve.scalar_tensor_tensor(r[:], k[:], -c1, ang[:], ALU.mult, ALU.add))
                    step(dve.scalar_tensor_tensor(r[:], k[:], -c2, r[:], ALU.mult, ALU.add))
                    step(dve.scalar_tensor_tensor(r[:], k[:], -c3, r[:], ALU.mult, ALU.add))
                    step(dve.tensor_scalar(r[:], r[:], quarter * TWO_PI, 3.1415925, ALU.add, ALU.min))
                    done(dve.tensor_scalar(dst[:], r[:], -3.1415925, None, ALU.max))

            @block.scalar
            def _(act):
                act.wait_ge(reduced, 2)
                act.activation(m.sin[:], m.sin[:], ACT.Sin)
                act.activation(m.cos[:], m.cos[:], ACT.Sin)

    def junction(tag, post=None, pre=None, ahead=None):
        names = ("sum_ready", "root_ready", "x_ready", "square_ready", "square_used", "xsum_ready",
                 "xroot_ready", "scaled_ready", "h_head_ready", "order", "act_order")
        with phase(nc, *names) as (block, sum_ready, root_ready, x_ready, square_ready, square_used,
                                   xsum_ready, xroot_ready, scaled_ready, head_ready, order, act_order):
            A = m.col[:, 0:8]
            G = m.col[:, 8:16]

            @block.sync
            def _(sp):
                if ahead:
                    ahead.loads(sp, 0, RING)

            @block.gpsimd
            def _(pool):
                if ahead:
                    ahead.rests(pool, 0, 2)

            @block.tensor
            def _(pe):
                if post:
                    pe.matmul(ps[0][:], ones, m.acc[:], start=True, stop=True).then_inc(sum_ready, 1)
                if pre:
                    for k in range(KD):
                        pe.wait_ge(square_ready, k + 1)
                        pe.matmul(ps[1][:], ones, m.sq[:, k % 2, :], start=(k == 0), stop=(k == KD - 1))\
                          .then_inc(square_used, 1)

            @block.scalar
            def _(act):
                if ahead:
                    ahead.heads(act, 0, 2)
                if post:
                    act.wait_ge(sum_ready, 1)
                    act.activation(m.acc[:], ps[0][:], ACT.Sqrt, bias=m.eps[:, 0:1], scale=1.0 / D)\
                       .then_inc(root_ready, 1)
                if pre:
                    for k in range(KD):
                        if post:
                            act.wait_ge(x_ready, k + 1)
                        if k >= 2:
                            act.wait_ge(square_used, k - 1)
                        act.activation(m.sq[:, k % 2, :], m.x[:, k, :], ACT.Square).then_inc(square_ready, 1)
                    act.wait_ge(square_used, KD)
                    act.activation(m.acc[:], ps[1][:], ACT.Sqrt, bias=m.eps[:, 0:1], scale=1.0 / D)\
                       .then_inc(xroot_ready, 1)
                    for k in range(KD):
                        act.wait_ge(scaled_ready, k + 1)
                        shift = pre[2][:, k:k + 1] if pre[2] is not None else 0.0
                        act.activation(m.hh[:, k, :], m.tmp[:, k % 2, :], ACT.Identity, bias=shift)\
                           .then_inc(head_ready, 1)

            @block.vector
            def _(dve):
                step, x_done, scaled = Signal(dve, order), Signal(dve, x_ready), Signal(dve, scaled_ready)
                if post:
                    if post[1] is not None:
                        step(dve.tensor_tensor(G, post[0], post[1], ALU.mult))
                        gain = G
                    else:
                        gain = post[0]
                if pre:
                    if pre[1] is not None:
                        step(dve.scalar_tensor_tensor(A, pre[1], 1.0, pre[0], ALU.add, ALU.mult))
                        scale = A
                    else:
                        scale = pre[0]
                if post:
                    dve.wait_ge(root_ready, 1)
                    step(dve.reciprocal(m.acc[:], m.acc[:]))
                    for k in range(KD):
                        step(dve.scalar_tensor_tensor(m.tmp[:, k % 2, :], m.y[:, k, :], gain[:, k:k + 1],
                                                      m.acc[:], ALU.mult, ALU.mult))
                        x_done(dve.tensor_tensor(m.x[:, k, :], m.x[:, k, :], m.tmp[:, k % 2, :], ALU.add))
                if pre:
                    dve.wait_ge(xroot_ready, 1)
                    step(dve.reciprocal(m.acc[:], m.acc[:]))
                    for k in range(KD + 1):
                        if k < KD:
                            if k >= 2:
                                dve.wait_ge(head_ready, k - 1)
                            scaled(dve.scalar_tensor_tensor(m.tmp[:, k % 2, :], m.x[:, k, :], scale[:, k:k + 1],
                                                            m.acc[:], ALU.mult, ALU.mult))
                        if k >= 1:
                            dve.wait_ge(head_ready, k)
                            shift = pre[2][:, k - 1:k] if pre[2] is not None else 0.0
                            step(dve.scalar_tensor_tensor(m.hl[:, k - 1, :], m.tmp[:, (k - 1) % 2, :], shift,
                                                          m.hh[:, k - 1, :].bitcast(F32), ALU.add, ALU.subtract))

    def product_out(s, t0, per, chunks, xh, xl, started=True):
        n = t0 + KD * per
        with phase(nc, "square_ready", "square_used", "y_order", run_ends=(n == s.total)) as \
                (block, square_ready, square_used, y_order):
            @block.sync
            def _(sp):
                s.loads(sp, t0 + RING if started else t0, n + RING)

            @block.gpsimd
            def _(pool):
                s.rests(pool, t0 + 2 if started else t0, n + 2)

            @block.tensor
            def _(pe):
                for t in range(t0, n):
                    nb, part = (t - t0) // per, (t - t0) % per
                    s.ready(pe, t // RING, t % RING)
                    if part == 0 and nb >= 2:
                        pe.wait_ge(square_ready, nb - 1)
                    c0 = 8 * part
                    for c in range(s.width(t) // P):
                        wc = slice(c * P, (c + 1) * P)
                        last = three_pass(pe, ps[nb % 2][:], m.wh[:, t % 2, wc], m.wl[:, t % 2, wc],
                                          xh[:, c0 + c, :], xl[:, c0 + c, :],
                                          start=(c0 + c == 0), stop=(c0 + c == chunks - 1))
                    last.then_inc(s.slot_done, 1)

            @block.scalar
            def _(act):
                if not started:
                    s.heads(act, t0, t0 + 2)
                for t in range(t0, n):
                    s.heads(act, t + 2, t + 3)
                    nb = (t - t0) // per
                    if (t - t0) % per == per - 1:
                        act.wait_ge(s.slot_done, t + 1)
                        act.activation(m.y[:, nb, :], ps[nb % 2][:], ACT.Copy).then_inc(y_order, 1)
                        if nb >= 2:
                            act.wait_ge(square_used, nb - 1)
                        act.activation(m.sq[:, nb % 2, :], ps[nb % 2][:], ACT.Square).then_inc(square_ready, 1)

            @block.vector
            def _(dve):
                for nb in range(KD):
                    dve.wait_ge(square_ready, nb + 1)
                    if nb == 0:
                        dve.tensor_copy(m.acc[:], m.sq[:, 0, :]).then_inc(square_used, 1)
                    else:
                        dve.wait_ge(square_used, nb)
                        dve.tensor_tensor(m.acc[:], m.acc[:], m.sq[:, nb % 2, :], ALU.add)\
                           .then_inc(square_used, 1)

    hid = Arena(nc, mix0, MIX)
    hidh, hidl = hid("hidh", [P, KF, T], F32R), hid("hidl", [P, KF, T], F32R)

    hidh2 = hidh[:].rearrange("p k t -> p (k t)")
    hidl2 = hidl[:].rearrange("p k t -> p (k t)")

    def gate_up(tag, s, conv):
        n = KF // 2
        ar = Arena(nc, y_at, KD * T * 4)
        gs, us = ar("gate" + tag, [P, 2, T]), ar("up" + tag, [P, 2, T])
        hs = ar("hidden" + tag, [P, 2, T])
        with phase(nc, "gate_base", "up_base", "gate_conv", "gate_act", "hid_ready", "pair_free",
                   "order") as (block, *sems):
            gate_base, up_base, gate_conv, gate_act, hid_ready, pair_free, order = sems

            @block.sync
            def _(sp):
                with sp.Fori(1, n) as i:
                    for j in range(RING):
                        s.load(sp, i, j)
                s.loads(sp, GU, GU + RING)

            @block.gpsimd
            def _(pool):
                s.rests(pool, 2, RING)
                with pool.Fori(1, n) as i:
                    for j in range(RING):
                        s.rest(pool, i, j)
                s.rests(pool, GU, GU + 2)

            @block.tensor
            def _(pe):
                def body(i, first=False):
                    for j in range(RING):
                        s.ready(pe, i, j)
                        if not first and j % 2 == 0:
                            pe.wait_ge(pair_free, i * 2 + (j // 2 - 1))
                        for c in range(KD):
                            wc = slice(c * P, (c + 1) * P)
                            last = three_pass(pe, ps[j][:], m.wh[:, j % 2, wc], m.wl[:, j % 2, wc],
                                              m.hh[:, c, :], m.hl[:, c, :], start=(c == 0), stop=(c == KD - 1))
                        last.then_inc(s.slot_done, 1)
                body(0, True)
                with pe.Fori(1, n) as i:
                    body(i)

            @block.scalar
            def _(act):
                def body(i, first=False):
                    for j in range(RING):
                        s.head(act, i + j // 2, (j + 2) % RING)
                        pair = j // 2
                        if conv:
                            act.wait_ge(s.slot_done, i * RING + (j + 1))
                            if not first:
                                act.wait_ge(pair_free, i * 2 + (pair - 1))
                            dst, cb, ready = (gs, 0, gate_base) if j % 2 == 0 else (us, KF, up_base)
                            act.activation(dst[:, pair, :], ps[j][:], ACT.Identity,
                                           bias=m.pc[:, bass.ds(i * 2 + (B_CB + cb + pair), 1)],
                                           scale=m.pc[:, bass.ds(i * 2 + (B_CW + 88 + cb + pair), 1)])\
                               .then_inc(ready, 1)
                            if j % 2 == 1:
                                act.wait_ge(gate_conv, i * 2 + (pair + 1))
                                act.activation(gs[:, pair, :], gs[:, pair, :], ACT.Gelu_apprx_tanh)\
                                   .then_inc(gate_act, 1)
                        elif j % 2 == 0:
                            act.wait_ge(s.slot_done, i * RING + (j + 1))
                            if not first:
                                act.wait_ge(pair_free, i * 2 + (pair - 1))
                            act.activation(gs[:, pair, :], ps[j][:], ACT.Silu).then_inc(gate_act, 1)
                body(0, first=True)
                with act.Fori(1, n) as i:
                    body(i)

            @block.vector
            def _(dve):
                STEPS = 5 if conv else 2

                def body(i):
                    for pair in range(2):
                        cnt = [0]

                        def step(ins):
                            cnt[0] += 1
                            ins.then_inc(order, 1)
                            dve.wait_ge(order, i * (2 * STEPS) + (pair * STEPS + cnt[0]))

                        def tap(buf, bank, block, shift, ready):
                            w_col = B_CW + 44 * (2 - shift) + block
                            return dve.scalar_tensor_tensor(
                                buf[:, pair, shift:T], bank[:, 0:T - shift],
                                m.pc[:, bass.ds(i * 2 + (w_col + pair), 1)], buf[:, pair, shift:T],
                                ALU.mult, ALU.add)
                        if conv:
                            dve.wait_ge(gate_base, i * 2 + (pair + 1))
                            step(tap(gs, ps[2 * pair], 0, 1, gate_base))
                            tap(gs, ps[2 * pair], 0, 2, None).then_inc(gate_conv, 1)
                            dve.wait_ge(up_base, i * 2 + (pair + 1))
                            step(tap(us, ps[2 * pair + 1], KF, 1, up_base))
                            step(tap(us, ps[2 * pair + 1], KF, 2, None))
                            up = us[:, pair, :]
                        else:
                            dve.wait_ge(s.slot_done, i * RING + (2 * pair + 2))
                            up = ps[2 * pair + 1][:]
                        dve.wait_ge(gate_act, i * 2 + (pair + 1))
                        dve.tensor_tensor(hs[:, pair, :], gs[:, pair, :], up, ALU.mult).then_inc(pair_free, 1)
                        dve.wait_ge(pair_free, i * 2 + (pair + 1))
                        step(dve.tensor_copy(hidh2[:, bass.ds(i * (2 * T) + pair * T, T)], hs[:, pair, :]))
                        step(dve.tensor_tensor(hidl2[:, bass.ds(i * (2 * T) + pair * T, T)], hs[:, pair, :],
                                               hidh2[:, bass.ds(i * (2 * T) + pair * T, T)].bitcast(F32), ALU.subtract))
                with dve.Fori(0, n) as i:
                    body(i)

    def feed_forward(tag, s, conv):
        gate_up(tag, s, conv)
        product_out(s, GU, 3, KF, hidh, hidl)

    stream_sems = [nc.semaphore(n, num=STREAM_SEM + k).__enter__() for k, n in enumerate(STREAM)]

    def run(w, base, total, width=lambda t: SLOT):
        return Stream(m, w, base, total, stream_sems, width)

    def ff_run(w, base):
        return run(w, base, GU + DN, lambda t: SLOT if t < GU or (t - GU) % 3 < 2 else (KF - 16) * P)

    mx = Arena(nc, mix0, MIX)
    qT, kT, qi = mx("qT", [P, 4, T]), mx("kT", [P, 4, T]), mx("qi", [P, 4, T])
    ki, va = mx("ki", [P, T]), mx("va", [P, NT, T])
    qk = mx("qk", [P, 8, T])
    og = mx("og", [P, MH, T])
    vm = mx("vm", [P, NT, MH, MD + 1])
    wi, ir, fr = mx("wi", [8, T]), mx("ir", [MH, T]), mx("fr", [MH, T])
    work1 = mx.at
    rawb = mx("rawb", [P, 2, T])
    yar = Arena(nc, y_at, KD * T * 4)
    cqf, cqh, cql = yar("cqf", [P, 2, T]), yar("cqh", [P, 2, T], F32R), yar("cql", [P, 2, T], F32R)
    cbc = mx("cbc", [P, D])
    mod_raw = mx("mod_raw0", [P, D]), yar("mod_raw1", [P, D])

    cst4 = Arena(nc, mix0, MIX)("mod4", [P, 4])
    MOD_FIRST = 2 * KD

    def modulation(w, base, pcols):
        n = MOD_FIRST // RING
        with phase(nc, "cols_in0", "cols_in1", "cols_in2", "cols_in3", "c_in", "c_act", "used", "moved",
                   "p_in") as \
                (block, w0, w1, w2, w3, c_in, c_act, used, moved, p_in):
            w_in = (w0, w1, w2, w3)

            @block.sync
            def _(sp):
                sp.dma_start(cbc[:], a["c"].partition_broadcast(P)).then_inc(c_in, 16)
                sp.dma_start(m.pc[:, 0:A_COLS], pcols).then_inc(p_in, 16)
                for j in range(RING):
                    sp.dma_start(m.raw[:, j, :], w[sp.snap(base + j)]).then_inc(w_in[j], 16)
                with sp.Fori(1, n) as i:
                    for j in range(RING):
                        src = w[sp.snap(base + i * RING + j)]
                        sp.wait_ge(used, i * RING + (j + 1 - RING))
                        sp.dma_start(m.raw[:, j, :], src).then_inc(w_in[j], 16)

            @block.scalar
            def _(act):
                act.wait_ge(c_in, 16)
                act.activation(cbc[:], cbc[:], ACT.Silu).then_inc(c_act, 1)

            @block.vector
            def _(dve):
                dve.wait_ge(c_act, 1)

                def body(i, first=False):
                    for j in range(RING):
                        dve.wait_ge(w_in[j], i * 16 + 16)
                        if j == 0 and not first:
                            dve.wait_ge(moved, i)
                        if not (first and j == 0):
                            dve.wait_ge(used, i * RING + j)
                        dve.tensor_tensor_reduce(mod_raw[0][:], m.raw[:, j, :], cbc[:], 1.0, 0.0, ALU.mult, ALU.add,
                                                 cst4[:, j:j + 1]).then_inc(used, 1)
                    dve.wait_ge(used, i * RING + RING)
                    dve.tensor_copy(m.mod[:, bass.ds(i * RING, RING)], cst4[:]).then_inc(moved, 1)
                body(0, True)
                with dve.Fori(1, n) as i:
                    body(i)
                dve.wait_ge(moved, n)
                dve.wait_ge(p_in, 16)
                dve.tensor_tensor(m.mod[:, 0:MOD_FIRST], m.mod[:, 0:MOD_FIRST],
                                  m.pc[:, A_BMOD:A_BMOD + MOD_FIRST], ALU.add)


    def in_products1(s, wmod, mod_base):
        MOD_REST = 48 - MOD_FIRST
        kinds = ([("latent", c) for c in range(2)] + [("key", c) for c in range(4)] + [("ikey", 0), ("rows", 0)]
                 + [("conv", c) for c in range(8)] + [("ogate", c) for c in range(4)]
                 + [("value", c) for c in range(4)] + [("mvalue", c) for c in range(4)]
                 + [("query", 0), ("iquery", 0)])
        assert len(kinds) == IN1
        mods = [range(min(MOD_REST, t * MOD_REST // (IN1 - 2)), min(MOD_REST, (t + 1) * MOD_REST // (IN1 - 2)))
                for t in range(IN1)]
        ropes = []
        for t, (kind, c) in enumerate(kinds):
            if kind == "key":
                ropes.append((t, t % 4, kT[:, c, :]))
            if kind == "ikey":
                ropes.append((t, t % 4, ki[:]))
            if kind in ("query", "iquery"):
                dst = qT if kind == "query" else qi
                ropes += [(t, (4 if kind == "query" else 0) + b, dst[:, b, :]) for b in range(4)]
        rope_of = {}
        for r, (t, _, _) in enumerate(ropes):
            rope_of.setdefault(t, []).append(r)
        uses = [0] * 8
        before = {}
        for t, (kind, c) in enumerate(kinds):
            if t < 20:
                before[t] = {t % 4: uses[t % 4]}
                uses[t % 4] += 1
            elif kind in ("value", "mvalue", "query", "iquery") and c == 0:
                banks = range(4, 8) if kind in ("value", "query") else range(4)
                before[t] = {b: uses[b] for b in banks}
                for b in banks:
                    uses[b] += 1
            if t == 1:
                uses[4] += 1
        free_names = [f"bank_free{b}" for b in range(8)]
        with phase(nc, *free_names, "latent_sq", "latent_sum", "latent_root", "latent_ready",
                   "unrotated_ready", "rotated_ready", "rope_done", "conv_base", "conv_done", "order",
                   "act_order", "ones_set", "mod_in0", "mod_in1", "mod_used", run_ends=True) as (block, *sems):
            bank_free = sems[0:8]
            (latent_sq, latent_sum, latent_root, latent_ready, unrotated_ready, rotated_ready, rope_done,
             conv_base, conv_done, order, act_order, ones_set, *mod_in, mod_used) = sems[8:]

            @block.sync
            def _(sp):
                for t in range(IN1):
                    for n in mods[t]:
                        src = wmod[sp.snap(mod_base + MOD_FIRST + n)]
                        if n >= 2:
                            sp.wait_ge(mod_used, n - 1)
                        sp.dma_start(mod_raw[n % 2][:], src).then_inc(mod_in[n % 2], 16)
                    s.loads(sp, RING + t, RING + t + 1)

            @block.gpsimd
            def _(pool):
                pool.memset(vm[:, :, :, MD:MD + 1], 1.0).then_inc(ones_set, 1)
                s.rests(pool, 2, IN1)

            @block.tensor
            def _(pe):
                def rotate(t):
                    for r in rope_of.get(t, ()):
                        pe.wait_ge(unrotated_ready, r + 1)
                        pe.matmul(ps[ropes[r][1]][:], rot, rawb[:, r % 2, :], start=True, stop=True)\
                          .then_inc(rotated_ready, 1)

                for t, (kind, c) in enumerate(kinds):
                    s.ready(pe, t // RING, t % RING)
                    for b, n in before.get(t, {}).items():
                        if n:
                            pe.wait_ge(bank_free[b], n)
                    if kind in ("value", "mvalue"):
                        b0 = 4 if kind == "value" else 0
                        for kk in range(2):
                            k = 2 * c + kk
                            wc = slice(kk * T, (kk + 1) * T)
                            for tb in range(NT):
                                tc = slice(tb * P, (tb + 1) * P)
                                o = ps[b0 + tb][:]
                                pe.matmul(o, m.hh[:, k, tc], m.wh[:, t % 2, wc], start=(k == 0), stop=False)
                                pe.matmul(o, m.hh[:, k, tc], m.wl[:, t % 2, wc], start=False, stop=False)
                                last = pe.matmul(o, m.hl[:, k, tc], m.wh[:, t % 2, wc], start=False,
                                                 stop=(k == KD - 1))
                    elif kind in ("query", "iquery"):
                        if kind == "query":
                            pe.wait_ge(latent_ready, 1)
                        b0 = 4 if kind == "query" else 0
                        for nb in range(4):
                            for k in range(2):
                                wc = slice(k * T + nb * P, k * T + (nb + 1) * P)
                                last = three_pass(pe, ps[b0 + nb][:], m.wh[:, t % 2, wc], m.wl[:, t % 2, wc],
                                                  cqh[:, k, :], cql[:, k, :], start=(k == 0), stop=(k == 1))
                    else:
                        for k in range(KD):
                            wc = slice(k * P, (k + 1) * P)
                            last = three_pass(pe, ps[t % 4][:], m.wh[:, t % 2, wc], m.wl[:, t % 2, wc],
                                              m.hh[:, k, :], m.hl[:, k, :], start=(k == 0), stop=(k == KD - 1))
                    last.then_inc(s.slot_done, 1)
                    if t == 3:
                        pe.wait_ge(latent_sq, 2)
                        pe.matmul(ps[4][:], ones, m.sq[:, 0, :], start=True, stop=False)
                        pe.matmul(ps[4][:], ones, m.sq[:, 1, :], start=False, stop=True).then_inc(latent_sum, 1)
                    if t >= 1:
                        rotate(t - 1)
                rotate(IN1 - 1)

            @block.scalar
            def _(act):
                step = Signal(act, act_order)

                def silu(c):
                    act.wait_ge(conv_done, c + 1)
                    step(act.activation(qk[:, c, :], qk[:, c, :], ACT.Silu))

                for t, (kind, c) in enumerate(kinds):
                    s.heads(act, t + 2, t + 3)
                    act.wait_ge(s.slot_done, t + 1)
                    bank = ps[t % 4]
                    if kind == "latent":
                        step(act.activation(cqf[:, c, :], bank[:], ACT.Copy))
                        act.activation(m.sq[:, c, :], bank[:], ACT.Square).then_inc(bank_free[t % 4], 1)
                        act.wait_ge(bank_free[t % 4], 1)
                        act.sem_inc(latent_sq, 1)
                    if t == 4:
                        act.wait_ge(latent_sum, 1)
                        act.activation(m.acc[:], ps[4][:], ACT.Sqrt, bias=m.eps[:, 0:1], scale=1.0 / QR)\
                           .then_inc(latent_root, 1)
                    for r in rope_of.get(t, ()):
                        if r >= 2:
                            act.wait_ge(rope_done, r - 1)
                        act.activation(rawb[:, r % 2, :], ps[ropes[r][1]][:], ACT.Copy).then_inc(unrotated_ready, 1)
                    if kind == "rows":
                        step(act.activation(wi[:], bank[0:8, :], ACT.Copy, scale=float((8 * 64) ** -0.5)))
                        step(act.activation(ir[:], bank[32:32 + MH, :], ACT.Identity, bias=m.pc[0:MH, A_BI:A_BI + 1]))
                        act.activation(fr[:], bank[64:64 + MH, :], ACT.Identity, bias=m.pc[0:MH, A_BF:A_BF + 1])\
                           .then_inc(bank_free[t % 4], 1)
                    if kind == "conv":
                        act.activation(qk[:, c, :], bank[:], ACT.Identity, bias=m.pc[:, A_CB + c:A_CB + c + 1],
                                       scale=m.pc[:, A_CW + 24 + c:A_CW + 25 + c]).then_inc(conv_base, 1)
                        if c:
                            silu(c - 1)
                    if kind == "ogate":
                        if c == 0:
                            silu(7)
                        act.activation(og[:, c, :], bank[:], ACT.Sigmoid).then_inc(bank_free[t % 4], 1)
                    if kind == "mvalue" and c == 3:
                        act.wait_ge(ones_set, 1)
                        for tb in range(NT):
                            act.activation(vm[:, tb, :, 0:MD], ps[tb][:].rearrange("p (h d) -> p h d", h=MH),
                                           ACT.Copy).then_inc(bank_free[tb], 1)

            @block.vector
            def _(dve):
                step = Signal(dve, order)

                def rope(r):
                    _, bank, dst = ropes[r]
                    dve.wait_ge(unrotated_ready, r + 1)
                    step(dve.tensor_tensor(m.tmp[:, 0, :], rawb[:, r % 2, :], m.cos[:], ALU.mult))
                    dve.wait_ge(rotated_ready, r + 1)
                    dve.tensor_tensor(m.tmp[:, 1, :], ps[bank][:], m.sin[:], ALU.mult).then_inc(bank_free[bank], 1)
                    freed[bank] += 1
                    dve.wait_ge(bank_free[bank], freed[bank])
                    dve.tensor_tensor(dst, m.tmp[:, 0, :], m.tmp[:, 1, :], ALU.add).then_inc(rope_done, 1)
                    dve.wait_ge(rope_done, r + 1)

                def modulate(n):
                    dve.wait_ge(mod_in[n % 2], 16 * (n // 2 + 1))
                    raw_ = mod_raw[n % 2][:]
                    dve.tensor_tensor_reduce(raw_, raw_, cbc[:], 1.0, 0.0, ALU.mult, ALU.add,
                                             m.mod[:, MOD_FIRST + n:MOD_FIRST + n + 1]).then_inc(mod_used, 1)

                freed = [0] * 8
                for t, (kind, c) in enumerate(kinds):
                    for n in mods[t]:
                        modulate(n)
                    if t == 5:
                        dve.wait_ge(latent_root, 1)
                        dve.reciprocal(m.acc[:], m.acc[:]).then_inc(bank_free[4], 1)
                        freed[4] += 1
                        dve.wait_ge(bank_free[4], 1)
                        for k in range(2):
                            step(dve.scalar_tensor_tensor(cqf[:, k, :], cqf[:, k, :],
                                                          m.pc[:, A_QN + k:A_QN + k + 1], m.acc[:],
                                                          ALU.mult, ALU.mult))
                            step(dve.tensor_copy(cqh[:, k, :], cqf[:, k, :]))
                            step(dve.tensor_tensor(cql[:, k, :], cqf[:, k, :], cqh[:, k, :].bitcast(F32),
                                                   ALU.subtract))
                        dve.sem_inc(latent_ready, 1)
                    for r in rope_of.get(t, ()):
                        rope(r)
                    bank = ps[t % 4]
                    if kind == "conv":
                        dve.wait_ge(conv_base, c + 1)
                        for shift in (1, 2, 3):
                            w_col = A_CW + 8 * (3 - shift) + c
                            ins = dve.scalar_tensor_tensor(qk[:, c, shift:T], bank[:, 0:T - shift],
                                                           m.pc[:, w_col:w_col + 1], qk[:, c, shift:T],
                                                           ALU.mult, ALU.add)
                            if shift < 3:
                                step(ins)
                        ins.then_inc(conv_done, 1)
                        dve.wait_ge(conv_done, c + 1)
                        dve.sem_inc(bank_free[t % 4], 1)
                    if kind == "value" and c == 3:
                        dve.wait_ge(s.slot_done, t + 1)
                        for tb in range(NT):
                            dve.tensor_copy(va[:, tb, :], ps[4 + tb][:]).then_inc(bank_free[4 + tb], 1)
                            freed[4 + tb] += 1

                    for b, n in before.get(t, {}).items():
                        if t < 20:
                            freed[b] = n + 1
                        elif kind == "mvalue":
                            freed[b] = n + 1
                dve.wait_ge(mod_used, MOD_REST)
                dve.tensor_tensor(m.mod[:, MOD_FIRST:48], m.mod[:, MOD_FIRST:48],
                                  m.pc[:, A_BMOD + MOD_FIRST:A_BMOD + 48], ALU.add)



    wk = Arena(nc, ring_at, RING_BYTES)
    sc, pr, pt = wk("sc", [P, 2, T]), wk("pr", [P, 3, T]), wk("pt", [P, 2, T])
    sel_at = wk.at
    sel = wk("sel", [P, NT, T])
    on = wk("on", [P, T])
    small = wk("small", [P, 256])
    yk = Arena(nc, y_at, KD * T * 4)
    wt = yk("wt", [P, 2, 1280])
    arg = yk("arg", [P, 2, T])
    att_n = Arena(nc, y_at, NT * T * 4)("att_n", [P, NT, T])
    wk2 = Arena(nc, work1, mix0 + MIX - work1)
    num = wk2("num", [P, NT, MH, MD + 1])
    b_row = wk2("b_row", [MH, T])
    rw = Arena(nc, sel_at, NT * T * 4)
    f_row, lf_row, m_row, one_row = (rw(n, [MH, T]) for n in ("f_row", "lf_row", "m_row", "one_row"))
    WT_AT = [0, 512, 896, 1152]

    def mixer1():
        names = ("gate_abs", "gate_log", "gate_sums", "m_exp", "rows_turned", "cols_ready",
                 "peak_row", "peak_used", "mscore", "arg_ready", "decay", "weight_ready", "masked",
                 "mout", "mout_copied", "iscore", "irelu", "irelu_used", "sel_ready",
                 "score", "soft_in", "weights", "turned", "turned_copied", "pv", "out_copied",
                 "root_in", "root", "norm_ready", "feat_turned", "feat_used", "order", "aorder", "porder")
        with phase(nc, *names) as (block, *sems):
            (gate_abs, gate_log, gate_sums, m_exp, rows_turned, cols_ready, peak_row, peak_used, mscore,
             arg_ready, decay, weight_ready, masked, mout, mout_copied, iscore, irelu, irelu_used, sel_ready,
             score, soft_in, weights, turned, turned_copied, pv, out_copied, root_in, root, norm_ready,
             feat_turned, feat_used, order, aorder, porder) = sems
            wi_col = small[:, 0:32]
            bm_col = small[:, 32:64]
            mxs, nmx = small[:, 64:96], small[:, 96:128]
            den, root_c = small[:, 128:160], small[:, 160:192]
            peak = small[:, 192:200]
            mden = small[:, 200:216]
            mitems = [(h, sb) for h in range(MH) for sb in range(NT)]
            iitems = [(tb, h) for tb in range(1, NT) for h in range(HEADS)]
            items = [(tb, h) for tb in range(NT) for h in range(HEADS)]

            def attend(pe):
                def scores(i):
                    tb, h = items[i]
                    if i >= 3:
                        pe.wait_ge(soft_in, i - 2)
                    r = slice(64 * (h % 2), 64 * (h % 2) + 64)
                    w_ = (tb + 1) * P
                    pe.matmul(ps[i % 3][:, 0:w_], qT[r, h // 2, tb * P:(tb + 1) * P], kT[r, h // 2, 0:w_],
                              start=True, stop=True).then_inc(score, 1)

                def turn(i):
                    tb, h = items[i]
                    pe.wait_ge(weights, i + 1)
                    if i >= 2:
                        pe.wait_ge(turned_copied, i - 1)
                    for kb in range(tb + 1):
                        ins = pe.transpose(ps[3 + i % 2][:, kb * P:(kb + 1) * P],
                                           pr[:, i % 3, kb * P:(kb + 1) * P], ident)
                    ins.then_inc(turned, 1)

                def values(i):
                    tb, h = items[i]
                    pe.wait_ge(turned_copied, i + 1)
                    if h == 0 and tb >= 2:
                        pe.wait_ge(out_copied, tb - 1)
                    for kb in range(tb + 1):
                        ins = pe.matmul(ps[5 + tb % 2][:, h * HD:(h + 1) * HD], pt[:, i % 2, kb * P:(kb + 1) * P],
                                        va[:, kb, h * HD:(h + 1) * HD], start=(kb == 0), stop=(kb == tb))
                    ins.then_inc(pv, 1)
                N = len(items)
                for i in range(N + 3):
                    if i < N:
                        scores(i)
                    if 0 <= i - 2 < N:
                        turn(i - 2)
                    if 0 <= i - 3 < N:
                        values(i - 3)

            def square_root(act, g):
                act.wait_ge(root_in, g + 1)
                n_ = MH if g < NT else HEADS
                act.activation(root_c[:, 0:n_], root_c[:, 0:n_], ACT.Sqrt, bias=m.eps[:, 0:1],
                               scale=1.0 / (MD if g < NT else HD)).then_inc(root, 1)

            def mcopy(act, h):
                act.wait_ge(mout, h + 1)
                for half in range(2):
                    act.activation(num[:, 2 * half:2 * half + 2, h, :],
                                   ps[4 + half][:, 0:258].rearrange("p (b d) -> p b d", b=2), ACT.Copy)\
                       .then_inc(mout_copied, 1)

            def mweight(dve, n, wready):
                h, sb = mitems[n]
                w_ = T - sb * P
                dve.wait_ge(mscore, n + 1)
                dve.wait_ge(decay, n + 1)
                if h >= 2 and sb == 0:
                    dve.wait_ge(mout, h - 1)
                wready(dve.scalar_tensor_tensor(wt[:, h % 2, WT_AT[sb]:WT_AT[sb] + w_], ps[n % 2][:, 0:w_],
                                                MD ** -0.5, arg[:, n % 2, 0:w_], ALU.mult, ALU.mult))

            def rescale(dve, step, rin, nready, g, src, dst, col, n_, d_, r2):
                bc = lambda c: c.unsqueeze(2).to_broadcast([P, n_, d_])
                step(dve.tensor_tensor(dst, src, bc(col), ALU.mult))
                sq_ = m.sq[:, 0, :].rearrange("p (h d) -> p h d", h=n_)
                step(dve.tensor_tensor(sq_, dst, dst, ALU.mult))
                rin(dve.tensor_reduce(root_c[:, 0:n_], sq_, AX_X, ALU.add))
                dve.wait_ge(root, g + 1)
                step(dve.reciprocal(r2, root_c[:, 0:n_]))
                nready(dve.tensor_tensor(dst, dst, bc(r2), ALU.mult))

            def finish(dve, step, ocop, rin, nready, tb):
                dve.wait_ge(pv, HEADS * (tb + 1))
                r_ = small[:, 216:224]
                step(dve.reciprocal(r_, den[:, HEADS * tb:HEADS * (tb + 1)]))
                src = ps[5 + tb % 2][:].rearrange("p (h d) -> p h d", h=HEADS)
                dst = att_n[:, tb, :].rearrange("p (h d) -> p h d", h=HEADS)
                ocop(dve.tensor_tensor(dst, src, r_.unsqueeze(2).to_broadcast([P, HEADS, HD]), ALU.mult))
                sq_ = m.sq[:, 0, :].rearrange("p (h d) -> p h d", h=HEADS)
                step(dve.tensor_tensor(sq_, dst, dst, ALU.mult))
                rin(dve.tensor_reduce(root_c[:, 0:HEADS], sq_, AX_X, ALU.add))
                dve.wait_ge(root, NT + tb + 1)
                step(dve.reciprocal(small[:, 224:232], root_c[:, 0:HEADS]))
                nready(dve.tensor_tensor(dst, dst, small[:, 224:232].unsqueeze(2).to_broadcast([P, HEADS, HD]),
                                         ALU.mult))

            @block.tensor
            def _(pe):
                for tb in range(NT):
                    ins = pe.transpose(ps[7][:, 8 * tb:8 * tb + 8], wi[0:8, tb * P:(tb + 1) * P], ident[0:8, 0:8])
                ins.then_inc(rows_turned, 1)
                def index(n):
                    tb, h = iitems[n]
                    if n >= 3:
                        pe.wait_ge(irelu, n - 2)
                    r = slice(64 * (h % 2), 64 * (h % 2) + 64)
                    w_ = (tb + 1) * P
                    pe.matmul(ps[n % 3][:, 0:w_], qi[r, h // 2, tb * P:(tb + 1) * P], ki[r, 0:w_],
                              start=True, stop=True).then_inc(iscore, 1)
                pe.wait_ge(m_exp, 1)
                pe.wait_ge(gate_sums, 2)
                for tb in range(NT):
                    pe.transpose(ps[7][:, 32 + 8 * tb:36 + 8 * tb], b_row[:, tb * P:(tb + 1) * P], ident[0:4, 0:4])
                    ins = pe.transpose(ps[7][:, 36 + 8 * tb:40 + 8 * tb], f_row[:, tb * P:(tb + 1) * P],
                                       ident[0:4, 0:4])
                ins.then_inc(rows_turned, 1)
                for h in range(MH):
                    if h:
                        pe.wait_ge(arg_ready, NT * h)
                    pe.matmul(ps[6][:], m.cst[0:MH, C_SEL + h * P:C_SEL + (h + 1) * P], m_row[:],
                              start=True, stop=True).then_inc(peak_row, 1)
                    for sb in range(NT):
                        n = NT * h + sb
                        if n >= 2:
                            pe.wait_ge(weight_ready, n - 1)
                        pe.matmul(ps[n % 2][:, 0:T - sb * P], qk[:, 4 + h, sb * P:(sb + 1) * P],
                                  qk[:, h, sb * P:T], start=True, stop=True).then_inc(mscore, 1)
                    if h:
                        pe.wait_ge(mout_copied, 2 * h)
                    pe.wait_ge(masked, NT * (h + 1))
                    for tb in range(NT):
                        for sb in range(tb + 1):
                            c0 = WT_AT[sb] + (tb - sb) * P
                            ins = pe.matmul(ps[4 + tb // 2][:, (tb % 2) * 129:(tb % 2) * 129 + 129],
                                            wt[:, h % 2, c0:c0 + P], vm[:, sb, h, :],
                                            start=(sb == 0), stop=(sb == tb))
                    ins.then_inc(mout, 1)
                for n in range(len(iitems)):
                    if n == 0:
                        pe.wait_ge(weight_ready, 16)
                    index(n)
                pe.wait_ge(irelu, len(iitems))
                pe.wait_ge(mout_copied, 8)
                attend(pe)
                for g in range(2 * NT):
                    pe.wait_ge(norm_ready, g + 1)
                    if g:
                        pe.wait_ge(feat_used, g)
                    for c in range(4):
                        s_ = num[:, g, c, 0:MD] if g < NT else att_n[:, g - NT, c * P:(c + 1) * P]
                        ins = pe.transpose(ps[7][:, c * P:(c + 1) * P], s_, ident)
                    ins.then_inc(feat_turned, 1)

            @block.scalar
            def _(act):
                step = Signal(act, aorder)
                step(act.activation(lf_row[:], fr[:], ACT.Abs))
                step(act.activation(lf_row[:], lf_row[:], ACT.Exp, scale=-1.0))
                act.activation(lf_row[:], lf_row[:], ACT.Ln, bias=1.0).then_inc(gate_log, 1)
                act.wait_ge(gate_sums, 1)
                act.activation(f_row[:], f_row[:], ACT.Exp, scale=-1.0).then_inc(m_exp, 1)
                for n, (h, sb) in enumerate(mitems):
                    act.wait_ge(arg_ready, n + 1)
                    act.activation(arg[:, n % 2, 0:T - sb * P], arg[:, n % 2, 0:T - sb * P], ACT.Exp)\
                       .then_inc(decay, 1)
                    if sb == NT - 1 and h >= 1:
                        mcopy(act, h - 1)
                mcopy(act, MH - 1)
                for n, (tb, h) in enumerate(iitems):
                    act.wait_ge(iscore, n + 1)
                    if n >= 2:
                        act.wait_ge(irelu_used, n - 1)
                    act.activation(sc[:, n % 2, 0:(tb + 1) * P], ps[n % 3][:, 0:(tb + 1) * P], ACT.Relu)\
                       .then_inc(irelu, 1)

                def soften(i):
                    tb, h = items[i]
                    act.wait_ge(soft_in, i + 1)
                    if i >= 3:
                        act.wait_ge(turned, i - 2)
                    w_ = (tb + 1) * P
                    act.activation(pr[:, i % 3, 0:w_], sc[:, i % 2, 0:w_], ACT.Exp, bias=nmx[:, i:i + 1],
                                   scale=HD ** -0.5, accum_out=den[:, i:i + 1]).then_inc(weights, 1)

                def copy_turned(i):
                    tb, h = items[i]
                    act.wait_ge(turned, i + 1)
                    if i >= 2:
                        act.wait_ge(pv, i - 1)
                    w_ = (tb + 1) * P
                    act.activation(pt[:, i % 2, 0:w_], ps[3 + i % 2][:, 0:w_], ACT.Copy).then_inc(turned_copied, 1)
                N = len(items)
                for g in range(NT):
                    square_root(act, g)
                for i in range(N + 1):
                    if i < N:
                        soften(i)
                    if i >= 1:
                        copy_turned(i - 1)
                    if i > HEADS and i % HEADS == 3:
                        square_root(act, NT + i // HEADS - 1)
                square_root(act, 2 * NT - 1)

            @block.gpsimd
            def _(pool):
                for n, (h, sb) in enumerate(mitems):
                    pool.wait_ge(weight_ready, n + 1)
                    w_ = wt[:, h % 2, WT_AT[sb]:WT_AT[sb] + P]
                    pool.affine_select(out=w_, in_=w_, compare_op=ALU.is_ge, fill=0.0, base=0,
                                       pattern=[[1, P]], channel_multiplier=-1).then_inc(masked, 1)

            @block.vector
            def _(dve):
                step = Signal(dve, order)
                S = lambda sem: Signal(dve, sem)
                sums, cols, args, wready, iused, sready = (S(x) for x in (
                    gate_sums, cols_ready, arg_ready, weight_ready, irelu_used, sel_ready))
                sin_, ocop, rin, nready, fused = (S(x) for x in (soft_in, out_copied, root_in, norm_ready,
                                                                 feat_used))
                step(dve.memset(one_row[:], 1.0))
                dve.wait_ge(rows_turned, 1)
                step(dve.tensor_copy(wi_col, ps[7][:, 0:32]))
                dve.wait_ge(gate_log, 1)
                step(dve.scalar_tensor_tensor(lf_row[:], fr[:], 0.0, lf_row[:], ALU.min, ALU.subtract))
                step(dve.tensor_tensor_scan(f_row[:], one_row[:], lf_row[:], 0.0, ALU.mult, ALU.add))
                step(dve.tensor_tensor(b_row[:], ir[:], f_row[:], ALU.subtract))
                step(dve.tensor_tensor_scan(m_row[:], b_row[:], b_row[:], 0.0, ALU.max, ALU.max))
                sums(dve.tensor_tensor(f_row[:], f_row[:], m_row[:], ALU.add))
                sums(dve.tensor_scalar(m_row[:], m_row[:], -1.0, None, ALU.mult))
                dve.wait_ge(rows_turned, 2)
                cols(dve.tensor_copy(bm_col, ps[7][:, 32:64]))
                for n, (h, sb) in enumerate(mitems):
                    w_ = T - sb * P
                    if sb == 0 and n:
                        mweight(dve, n - 1, wready)
                    dve.wait_ge(peak_row, h + 1)
                    if n >= 2:
                        dve.wait_ge(weight_ready, n - 1)
                    args(dve.tensor_scalar(arg[:, n % 2, 0:w_], ps[6][:, sb * P:T],
                                           bm_col[:, 8 * sb + h:8 * sb + h + 1], 0.0, ALU.add, ALU.min))
                    if sb:
                        mweight(dve, n - 1, wready)
                mweight(dve, 15, wready)
                for n, (tb, h) in enumerate(iitems):
                    w_ = (tb + 1) * P
                    acc_ = sel[:, tb, 0:w_]
                    dve.wait_ge(irelu, n + 1)
                    wcol = wi_col[:, 8 * tb + h:8 * tb + h + 1]
                    if h == 0:
                        iused(dve.scalar_tensor_tensor(acc_, sc[:, n % 2, 0:w_], wcol, causal(tb),
                                                       ALU.mult, ALU.add))
                    else:
                        iused(dve.scalar_tensor_tensor(acc_, sc[:, n % 2, 0:w_], wcol, acc_, ALU.mult, ALU.add))
                    if h == HEADS - 1:
                        for _ in range(TOPK // 8):
                            step(dve.max(peak, acc_))
                            step(dve.match_replace(acc_, peak, acc_, TAKEN))
                        sready(dve.tensor_scalar(acc_, acc_, TAKEN, NEG, ALU.not_equal, ALU.mult))
                dve.wait_ge(mout_copied, 8)
                for tb in range(NT):
                    step(dve.scalar_tensor_tensor(mden[:, 0:4], num[:, tb, :, MD], -1.0, num[:, tb, :, MD],
                                                  ALU.mult, ALU.max))
                    step(dve.tensor_tensor(mden[:, 0:4], mden[:, 0:4], bm_col[:, 8 * tb + 4:8 * tb + 8], ALU.max))
                    step(dve.reciprocal(mden[:, 0:4], mden[:, 0:4]))
                    rescale(dve, step, rin, nready, tb, num[:, tb, :, 0:MD], num[:, tb, :, 0:MD],
                            mden[:, 0:4], MH, MD, mden[:, 4:8])
                for i, (tb, h) in enumerate(items):
                    w_ = (tb + 1) * P
                    dve.wait_ge(score, i + 1)
                    if i >= 2:
                        dve.wait_ge(weights, i - 1)
                    mask = causal(tb) if tb == 0 else sel[:, tb, 0:w_]
                    step(dve.tensor_tensor_reduce(sc[:, i % 2, 0:w_], ps[i % 3][:, 0:w_], mask, 1.0, TAKEN,
                                                  ALU.add, ALU.max, mxs[:, i:i + 1]))
                    sin_(dve.tensor_scalar(nmx[:, i:i + 1], mxs[:, i:i + 1], -(HD ** -0.5), None, ALU.mult))
                    if h == 3 and tb:
                        finish(dve, step, ocop, rin, nready, tb - 1)
                finish(dve, step, ocop, rin, nready, NT - 1)
                for g in range(2 * NT):
                    tb = g % NT
                    dve.wait_ge(feat_turned, g + 1)
                    c0 = 4 if g < NT else 0
                    for c in range(4):
                        ts_ = slice(tb * P, (tb + 1) * P)
                        dst = on[:, c * P:(c + 1) * P]
                        if g < NT:
                            ins = dve.scalar_tensor_tensor(dst, ps[7][:, c * P:(c + 1) * P],
                                                           m.pc[:, A_MN + c:A_MN + c + 1], og[:, c, ts_],
                                                           ALU.mult, ALU.mult)
                        else:
                            ins = dve.tensor_scalar(dst, ps[7][:, c * P:(c + 1) * P],
                                                    m.pc[:, A_AN + c:A_AN + c + 1], None, ALU.mult)
                        if c < 3:
                            step(ins)
                        else:
                            fused(ins)
                    o3 = on[:].rearrange("p (c t) -> p c t", c=4)
                    step(dve.tensor_copy(m.hh[:, c0:c0 + 4, tb * P:(tb + 1) * P], o3))
                    step(dve.tensor_tensor(m.hl[:, c0:c0 + 4, tb * P:(tb + 1) * P], o3,
                                           m.hh[:, c0:c0 + 4, tb * P:(tb + 1) * P].bitcast(F32), ALU.subtract))


    mz = Arena(nc, mix0, MIX)
    q2 = mz("q2", [P, 4, T])
    kc, vc, ksl, kwn = (mz(n, [P, T]) for n in ("kc", "vc", "ksl", "kwn"))
    VSW = 280
    vsw = mz("vsw", [P, NT, VSW])
    sq2, sk2, sv2 = mz("sq2", [P, 4, T]), mz("sk2", [P, 4, T]), mz("sv2", [P, NT, T])
    gm = mz("gm", [P, 2 * KD, T])
    kct, vct = mz("kct", [P, 32]), mz("vct", [P, P])
    rawb2 = mz("rawb2", [P, T])
    y2 = Arena(nc, y_at, KD * T * 4)
    peh = [y2(f"peh{i}", [P, CB, 32], F32R) for i in range(2)]
    pel = [y2(f"pel{i}", [P, CB, 32], F32R) for i in range(2)]

    def params2(pcols):
        with phase(nc, "loaded") as (block, loaded):
            @block.sync
            def _(sp):
                sp.dma_start(m.pc[:], pcols).then_inc(loaded, 16)
                sp.wait_ge(loaded, 16)

    def in_products2(s):
        kinds = ([("rope", q2[:, c, :]) for c in range(4)] + [("rope", kc[:]), ("plain", vc[:]), ("rope", ksl[:]),
                 ("rope", kwn[:])] + [("value", c) for c in range(4)]
                 + [("plain", sq2[:, c, :]) for c in range(4)] + [("plain", sk2[:, c, :]) for c in range(4)]
                 + [("svalue", c) for c in range(4)] + [("compress", c) for c in range(8)]
                 + [("merge", c) for c in range(16)])
        assert len(kinds) == IN2
        ropes = [(t, t % 4, dst) for t, (kind, dst) in enumerate(kinds) if kind == "rope"]
        rope_of = {t: r for r, (t, _, _) in enumerate(ropes)}
        uses, before = [0] * 8, {}
        for t, (kind, c) in enumerate(kinds):
            if kind in ("value", "svalue"):
                banks = range(4, 8) if c == 0 else ()
            elif kind == "compress":
                banks = (4 + c // 4,) if c % 4 == 0 else ()
            else:
                banks = (t % 4,)
            before[t] = {b: uses[b] for b in banks}
            for b in banks:
                uses[b] += 1
        free_names = [f"bank_free{b}" for b in range(8)]
        with phase(nc, *free_names, "unrotated_ready", "rotated_ready", "rope_done", "plain_done",
                   "windows_ready", "hidden_ready", "second_done", "order", "aorder", run_ends=True) as (block, *sems):
            bank_free = sems[0:8]
            (unrotated_ready, rotated_ready, rope_done, plain_done, windows_ready, hidden_ready, second_done,
             order, aorder) = sems[8:]
            hc = [m.sq[:, 0, 0:32], m.sq[:, 0, 32:64]]

            @block.sync
            def _(sp):
                s.loads(sp, RING, IN2)

            @block.gpsimd
            def _(pool):
                s.rests(pool, 2, IN2)

            @block.tensor
            def _(pe):
                def rotate(t):
                    if t in rope_of:
                        r = rope_of[t]
                        pe.wait_ge(unrotated_ready, r + 1)
                        pe.matmul(ps[t % 4][:], rot, rawb2[:], start=True, stop=True).then_inc(rotated_ready, 1)

                for t, (kind, c) in enumerate(kinds):
                    s.ready(pe, t // RING, t % RING)
                    for b, n in before[t].items():
                        if n:
                            pe.wait_ge(bank_free[b], n)
                    if kind in ("value", "svalue"):
                        nw = VSW if kind == "value" else T
                        for kk in range(2):
                            k = 2 * c + kk
                            wc = slice(kk * T, kk * T + nw)
                            for tb in range(NT):
                                tc = slice(tb * P, (tb + 1) * P)
                                o = ps[4 + tb][:, 0:nw]
                                pe.matmul(o, m.hh[:, k, tc], m.wh[:, t % 2, wc], start=(k == 0), stop=False)
                                pe.matmul(o, m.hh[:, k, tc], m.wl[:, t % 2, wc], start=False, stop=False)
                                last = pe.matmul(o, m.hl[:, k, tc], m.wh[:, t % 2, wc], start=False,
                                                 stop=(k == KD - 1))
                    elif kind == "compress":
                        kv, q_ = c // 4, c % 4
                        pe.wait_ge(windows_ready, kv + 1)
                        for j in range(8):
                            wc = slice(j * P, (j + 1) * P)
                            jj = 8 * q_ + j
                            last = three_pass(pe, ps[4 + kv][:, 0:32], m.wh[:, t % 2, wc], m.wl[:, t % 2, wc],
                                              peh[kv][:, jj, :], pel[kv][:, jj, :], start=(jj == 0),
                                              stop=(jj == CB - 1))
                    else:
                        for k in range(KD):
                            wc = slice(k * P, (k + 1) * P)
                            last = three_pass(pe, ps[t % 4][:], m.wh[:, t % 2, wc], m.wl[:, t % 2, wc],
                                              m.hh[:, k, :], m.hl[:, k, :], start=(k == 0), stop=(k == KD - 1))
                    last.then_inc(s.slot_done, 1)
                    if t >= 1:
                        rotate(t - 1)
                    if kind == "merge" and c == 1:
                        pe.wait_ge(hidden_ready, 2)
                        pe.wait_ge(bank_free[6], uses[6])
                        pe.wait_ge(bank_free[7], uses[7])
                        pe.matmul(ps[6][:, 0:NCMP], m.pc[:, B_W2K:B_W2K + P], hc[0][:, 0:NCMP],
                                  start=True, stop=True)
                        pe.matmul(ps[7][0:NCMP, 0:P], hc[1][:, 0:NCMP], m.pc[:, B_W2V:B_W2V + P],
                                  start=True, stop=True).then_inc(second_done, 1)

            @block.scalar
            def _(act):
                for t, (kind, c) in enumerate(kinds):
                    s.heads(act, t + 2, t + 3)
                    act.wait_ge(s.slot_done, t + 1)
                    bank = ps[t % 4]
                    if kind == "rope":
                        r = rope_of[t]
                        if r:
                            act.wait_ge(rope_done, r)
                        act.activation(rawb2[:], bank[:], ACT.Copy).then_inc(unrotated_ready, 1)
                    if kind == "plain":
                        act.activation(c, bank[:], ACT.Copy).then_inc(bank_free[t % 4], 1)
                    if kind == "merge":
                        act.activation(gm[:, c, :], bank[:], ACT.Sigmoid).then_inc(bank_free[t % 4], 1)
                    if kind == "compress" and c % 4 == 3:
                        kv = c // 4
                        act.activation(hc[kv], ps[4 + kv][:, 0:32], ACT.Gelu_apprx_tanh,
                                       bias=m.pc[:, B_B1K + kv:B_B1K + kv + 1]).then_inc(hidden_ready, 1)

            @block.vector
            def _(dve):
                step = Signal(dve, order)
                for t, (kind, c) in enumerate(kinds):
                    if kind == "rope":
                        r = rope_of[t]
                        dve.wait_ge(unrotated_ready, r + 1)
                        step(dve.tensor_tensor(m.tmp[:, 0, :], rawb2[:], m.cos[:], ALU.mult))
                        dve.wait_ge(rotated_ready, r + 1)
                        step(dve.tensor_tensor(m.tmp[:, 1, :], ps[t % 4][:], m.sin[:], ALU.mult))
                        dve.sem_inc(bank_free[t % 4], 1)
                        dve.tensor_tensor(c, m.tmp[:, 0, :], m.tmp[:, 1, :], ALU.add).then_inc(rope_done, 1)
                        dve.wait_ge(rope_done, r + 1)
                    if kind in ("value", "svalue") and c == 3:
                        dve.wait_ge(s.slot_done, t + 1)
                        for tb in range(NT):
                            dst = vsw[:, tb, :] if kind == "value" else sv2[:, tb, :]
                            nw = VSW if kind == "value" else T
                            dve.tensor_copy(dst, ps[4 + tb][:, 0:nw]).then_inc(bank_free[4 + tb], 1)
                        dve.wait_ge(bank_free[4 + NT - 1], 1 if kind == "value" else 2)
                    if t == 9:
                        dve.wait_ge(bank_free[1], 2)
                        win = m.tmp[:].rearrange("p a (j n) -> p (a j) n", n=32)
                        for kv, src in enumerate((kc, vc)):
                            pe_col = m.pc[:, B_PEK + CB * kv:B_PEK + CB * (kv + 1)]
                            step(dve.memset(m.tmp[:], 0.0))
                            for half in range(2):
                                j0 = 16 * half
                                view = src[:, j0:j0 + 16 * NCMP].rearrange("p (n j) -> p j n", j=16)
                                step(dve.tensor_tensor(
                                    win[:, j0:j0 + 16, 0:NCMP], view,
                                    pe_col[:, j0:j0 + 16].unsqueeze(2).to_broadcast([P, 16, NCMP]), ALU.add))
                            step(dve.tensor_copy(peh[kv][:], win))
                            step(dve.tensor_tensor(pel[kv][:], win, peh[kv][:].bitcast(F32), ALU.subtract))
                            dve.sem_inc(windows_ready, 1)
                dve.wait_ge(second_done, 1)
                dve.tensor_copy(kct[:, 0:NCMP], ps[6][:, 0:NCMP])
                dve.tensor_copy(vct[0:NCMP, :], ps[7][0:NCMP, 0:P])

    w3 = Arena(nc, ring_at, RING_BYTES)
    sc3, pr3, pt3 = w3("sc3", [P, 4, T]), w3("pr3", [P, 4, T]), w3("pt3", [P, 2, T])
    lg, keep = w3("lg", [P, 3, T]), w3("keep", [P, 2, T + 1])
    sm3 = w3("sm3", [P, 448])
    y3 = Arena(nc, y_at, KD * T * 4)
    o_nsa, o_sb = y3("o_nsa", [P, NT, T]), y3("o_sb", [P, NT, T])
    SCALE = HD ** -0.5

    def mixer2():
        items = [(kind, tb, h) for tb in range(NT) for kind in ("slc", "win") for h in (0, 4, 1, 5, 2, 6, 3, 7)]
        SOFT = len(items)
        items += [("sb", tb, h) for tb in range(NT) for h in range(HEADS)]
        N, PAIRS, GROUPS = len(items), len(items) // 2, len(items) // HEADS
        soft_col = [i // HEADS * HEADS + h for i, (_, _, h) in enumerate(items[:SOFT])]
        turn_step = [p + (1 if 2 * p < SOFT else 2) for p in range(PAIRS)]
        turned_at = {s: p for p, s in enumerate(turn_step)}
        values_at = {s + 1: p for p, s in enumerate(turn_step)}
        STEPS = turn_step[-1] + 2
        mxs, nmx, den = sm3[:, 0:64], sm3[:, 64:128], sm3[:, 128:192]
        gts = sm3[:, 192:288].rearrange("p (b h c) -> p b h c", b=NT, c=3)
        cneg = sm3[:, 288:288 + 32 * NT].rearrange("p (b n) -> p b n", b=NT)
        t32 = sm3[:, 416:448]
        names = ("gates", "cscore", "cshift", "cexp", "cweights", "cturned", "cturned_copied", "cpv", "cout",
                 "score", "soft_read", "soft_in", "soft_weights", "keeps", "betas", "keeps_masked", "suffixes",
                 "products", "weights_masked", "turned", "turned_copied", "pv", "out_copied", "o_ready",
                 "feat_turned", "feat_used", "order")
        with phase(nc, *names) as (block, *sems):
            (gates, cscore, cshift, cexp, cweights, cturned, cturned_copied, cpv, cout, score, soft_read,
             soft_in, soft_weights, keeps, betas, keeps_masked, suffixes, products, weights_masked, turned,
             turned_copied, pv, out_copied, o_ready, feat_turned, feat_used, order) = sems
            cs_flat = sc3[:, 0:2, :].rearrange("p a t -> p (a t)")[:, 0:NT * HEADS * NCMP]
            cs = cs_flat.rearrange("p (b h n) -> p b h n", b=NT, h=HEADS)
            cs3 = cs_flat.rearrange("p (g n) -> p g n", n=NCMP)
            ptc = (pt3[:], pr3[:, 0:2, :], pr3[:, 2:4, :], sc3[:, 2:4, :])
            turn_banks = ((2, 3), (4, 5), (6, 7), (0, 1))

            def heads(h):
                return slice(64 * (h // 4), 64 * (h // 4) + 64), h % 4

            @block.tensor
            def _(pe):
                for tb in range(NT):
                    for h in (0, 4, 1, 5, 2, 6, 3, 7):
                        r, b = heads(h)
                        at = tb * P + b * 32
                        ins = pe.matmul(ps[h // 4][:, at:at + NCMP], q2[r, b, tb * P:(tb + 1) * P],
                                        kct[r, 0:NCMP], start=True, stop=True)
                ins.then_inc(cscore, 1)
                pe.wait_ge(cweights, 1)
                for tb in range(NT):
                    for h in range(HEADS):
                        ins = pe.transpose(ps[turn_banks[tb][h // 4]][0:NCMP, (h % 4) * P:(h % 4 + 1) * P],
                                           cs[:, tb, h, :], ident)
                    ins.then_inc(cturned, 1)
                for tb in range(NT):
                    pe.wait_ge(cturned_copied, 2 * tb + 2)
                    for h in range(HEADS):
                        ins = pe.matmul(ps[turn_banks[tb][0]][:, h * HD:(h + 1) * HD],
                                        ptc[tb][0:NCMP, h // 4, (h % 4) * P:(h % 4 + 1) * P],
                                        vct[0:NCMP, 64 * (h // 4):64 * (h // 4) + 64], start=True, stop=True)
                    ins.then_inc(cpv, 1)
                pe.wait_ge(cout, NT)

                def scores(i):
                    kind, tb, h = items[i]
                    j = i - 4
                    if 0 <= j < SOFT:
                        pe.wait_ge(soft_read, j + 1)
                    elif j >= SOFT:
                        pe.wait_ge(betas, j - SOFT + 1)
                    w_ = (tb + 1) * P
                    if kind == "sb":
                        r = slice(64 * (h % 2), 64 * (h % 2) + 64)
                        q_, k_ = sq2[r, h // 2, tb * P:(tb + 1) * P], sk2[r, h // 2, 0:w_]
                    else:
                        r, b = heads(h)
                        q_, k_ = q2[r, b, tb * P:(tb + 1) * P], (ksl if kind == "slc" else kwn)[r, 0:w_]
                    pe.matmul(ps[i % 4][:, 0:w_], q_, k_, start=True, stop=True).then_inc(score, 1)

                def turn(i):
                    kind, tb, h = items[i]
                    if kind == "sb":
                        pe.wait_ge(weights_masked, i - SOFT + 1)
                    else:
                        pe.wait_ge(soft_weights, i + 1)
                    if i >= 2:
                        pe.wait_ge(turned_copied, i - 1)
                    for kb in range(tb + 1):
                        ins = pe.transpose(ps[4 + i % 2][:, kb * P:(kb + 1) * P],
                                           pr3[:, i % 4, kb * P:(kb + 1) * P], ident)
                    ins.then_inc(turned, 1)

                def values(i):
                    kind, tb, h = items[i]
                    g = i // HEADS
                    pe.wait_ge(turned_copied, i + 1)
                    if i % HEADS == 0 and g >= 2:
                        pe.wait_ge(out_copied, g - 1)
                    for kb in range(tb + 1):
                        if kind == "sb":
                            v_ = sv2[:, kb, h * HD:(h + 1) * HD]
                        else:
                            v0 = (0 if kind == "slc" else P) + 64 * (h // 4)
                            v_ = vsw[:, kb, v0:v0 + HD]
                        ins = pe.matmul(ps[6 + g % 2][:, h * HD:(h + 1) * HD],
                                        pt3[:, i % 2, kb * P:(kb + 1) * P], v_, start=(kb == 0), stop=(kb == tb))
                    ins.then_inc(pv, 1)
                for s in range(STEPS):
                    if s < PAIRS:
                        scores(2 * s)
                        scores(2 * s + 1)
                    for one in range(2):
                        if s in turned_at:
                            turn(2 * turned_at[s] + one)
                        if s in values_at:
                            values(2 * values_at[s] + one)
                for g in range(2 * NT):
                    pe.wait_ge(o_ready, g + 1)
                    if g >= 2:
                        pe.wait_ge(feat_used, g - 1)
                    src = (o_nsa if g < NT else o_sb)[:, g % NT, :]
                    for c in range(4):
                        ins = pe.transpose(ps[g % 2][:, c * P:(c + 1) * P], src[:, c * P:(c + 1) * P], ident)
                    ins.then_inc(feat_turned, 1)

            @block.scalar
            def _(act):
                act.activation(sm3[:, 192:288].rearrange("p (b c) -> p b c", b=NT), vsw[:, :, 256:280],
                               ACT.Sigmoid).then_inc(gates, 1)
                act.wait_ge(cshift, 1)
                act.activation(cs_flat, cs_flat, ACT.Exp, scale=SCALE).then_inc(cexp, 1)
                for tb in range(NT):
                    act.wait_ge(cturned, tb + 1)
                    for half in range(2):
                        act.activation(ptc[tb][0:NCMP, half, :], ps[turn_banks[tb][half]][0:NCMP, :], ACT.Copy)\
                           .then_inc(cturned_copied, 1)

                def exps(i):
                    n, w_ = soft_col[i], (items[i][1] + 1) * P
                    if i >= 4:
                        act.wait_ge(turned, i - 3)
                    else:
                        act.wait_ge(cpv, NT)
                    act.wait_ge(soft_in, i // 2 + 1)
                    act.activation(pr3[:, i % 4, 0:w_], sc3[:, i % 4, 0:w_], ACT.Exp, bias=nmx[:, n:n + 1],
                                   scale=SCALE, accum_out=den[:, n:n + 1]).then_inc(soft_weights, 1)

                def sigmoids(i):
                    n, w_ = i - SOFT, (items[i][1] + 1) * P
                    act.wait_ge(score, i + 1)
                    if n >= 3:
                        act.wait_ge(suffixes, n - 2)
                    act.activation(lg[:, n % 3, 0:w_], ps[i % 4][:, 0:w_], ACT.Sigmoid, scale=-SCALE)\
                       .then_inc(keeps, 1)
                    if n >= 4:
                        act.wait_ge(products, n - 3)
                    else:
                        act.wait_ge(soft_weights, i - 3)
                    act.activation(sc3[:, i % 4, 0:w_], ps[i % 4][:, 0:w_], ACT.Sigmoid, scale=SCALE)\
                       .then_inc(betas, 1)

                def copy_turned(i):
                    w_ = (items[i][1] + 1) * P
                    act.wait_ge(turned, i + 1)
                    if i >= 2:
                        act.wait_ge(pv, i - 1)
                    act.activation(pt3[:, i % 2, 0:w_], ps[4 + i % 2][:, 0:w_], ACT.Copy).then_inc(turned_copied, 1)
                for s in range(STEPS):
                    if s < PAIRS:
                        for one in range(2):
                            (exps if 2 * s < SOFT else sigmoids)(2 * s + one)
                    if s in turned_at:
                        for one in range(2):
                            copy_turned(2 * turned_at[s] + one)

            @block.gpsimd
            def _(pool):
                def strict(ap, fill):
                    return pool.affine_select(out=ap, in_=ap, compare_op=ALU.is_gt, fill=fill, base=0,
                                              pattern=[[-1, P]], channel_multiplier=1)
                for n in range(N - SOFT + 1):
                    if n < N - SOFT:
                        tb = items[SOFT + n][1]
                        pool.wait_ge(keeps, n + 1)
                        strict(lg[:, n % 3, tb * P:(tb + 1) * P], 1.0).then_inc(keeps_masked, 1)
                    if n:
                        i = SOFT + n - 1
                        tb = items[i][1]
                        pool.wait_ge(products, n)
                        strict(pr3[:, i % 4, tb * P:(tb + 1) * P], 0.0).then_inc(weights_masked, 1)

            @block.vector
            def _(dve):
                step = Signal(dve, order)
                S = lambda sem: Signal(dve, sem)
                cw, ocop, fused = (S(x) for x in (cweights, out_copied, feat_used))
                cm = m.cst[:, C_CMP:C_CMP + 32 * NT].rearrange("p (b n) -> p b n", b=NT)
                by_group = lambda c: c.unsqueeze(2).to_broadcast([P, NT * HEADS, NCMP])
                by_block = lambda c: c[:, :, 0:NCMP].unsqueeze(2).to_broadcast([P, NT, 4, NCMP])
                step(dve.tensor_scalar(cneg, cm, 1.0, -NEG, ALU.subtract, ALU.mult))
                step(dve.memset(m.sq[:, 1, :], 0.0))
                step(dve.memset(keep[:, :, T:T + 1], 1.0))
                dve.wait_ge(cscore, 1)
                for half in range(2):
                    zs = ps[half][:].rearrange("p (b h n) -> p b h n", b=NT, h=4)[:, :, :, 0:NCMP]
                    step(dve.tensor_tensor(cs[:, :, 4 * half:4 * half + 4, :], zs, by_block(cneg), ALU.add))
                step(dve.tensor_reduce(t32, cs3, AX_X, ALU.max))
                dve.tensor_tensor(cs3, cs3, by_group(t32), ALU.subtract).then_inc(cshift, 1)
                dve.wait_ge(cexp, 1)
                step(dve.tensor_reduce(t32, cs3, AX_X, ALU.add))
                for half in range(2):
                    c_ = cs[:, :, 4 * half:4 * half + 4, :]
                    (cw if half else step)(dve.tensor_tensor(c_, c_, by_block(cm), ALU.mult))
                step(dve.reciprocal(t32, t32))
                dve.wait_ge(gates, 1)
                t_ = t32.rearrange("p (b h) -> p b h", b=NT)
                step(dve.tensor_tensor(t_, t_, gts[:, :, :, 0], ALU.mult))
                heads_of = lambda a_: a_.rearrange("p (h d) -> p h d", h=HEADS)
                by_head = lambda c: c.unsqueeze(2).to_broadcast([P, HEADS, HD])
                for tb in range(NT):
                    dve.wait_ge(cpv, tb + 1)
                    dve.tensor_tensor(heads_of(o_nsa[:, tb, :]), heads_of(ps[turn_banks[tb][0]][:]),
                                      by_head(t_[:, tb, :]), ALU.mult).then_inc(cout, 1)
                dve.wait_ge(cout, NT)

                def maxima(p):
                    for i in (2 * p, 2 * p + 1):
                        w_ = (items[i][1] + 1) * P
                        if i >= 4:
                            dve.wait_ge(soft_weights, i - 3)
                        dve.wait_ge(score, i + 1)
                        n = soft_col[i]
                        dve.tensor_tensor_reduce(sc3[:, i % 4, 0:w_], ps[i % 4][:, 0:w_], causal(items[i][1]),
                                                 1.0, TAKEN, ALU.add, ALU.max, mxs[:, n:n + 1])\
                           .then_inc(soft_read, 1)
                    dve.wait_ge(soft_read, 2 * p + 2)
                    n = soft_col[2 * p]
                    dve.tensor_scalar(nmx[:, n:n + 5:4], mxs[:, n:n + 5:4], -SCALE, None, ALU.mult)\
                       .then_inc(soft_in, 1)

                def products_of(p):
                    for i in (2 * p, 2 * p + 1):
                        n, w_ = i - SOFT, (items[i][1] + 1) * P
                        dve.wait_ge(keeps_masked, n + 1)
                        if n >= 2:
                            dve.wait_ge(products, n - 1)
                        dve.tensor_tensor_scan(keep[:, n % 2, T - w_:T][:, ::-1], lg[:, n % 3, 0:w_][:, ::-1],
                                               m.sq[:, 1, 0:w_], 1.0, ALU.mult, ALU.add).then_inc(suffixes, 1)
                    for i in (2 * p, 2 * p + 1):
                        n, w_ = i - SOFT, (items[i][1] + 1) * P
                        dve.wait_ge(suffixes, n + 1)
                        dve.wait_ge(betas, n + 1)
                        dve.wait_ge(turned, i - 3)
                        dve.tensor_tensor(pr3[:, i % 4, 0:w_], sc3[:, i % 4, 0:w_],
                                          keep[:, n % 2, T - w_ + 1:T + 1], ALU.mult).then_inc(products, 1)

                def finish(g):
                    kind, tb, _ = items[g * HEADS]
                    dve.wait_ge(pv, HEADS * (g + 1))
                    if kind == "sb":
                        ocop(dve.tensor_copy(o_sb[:, tb, :], ps[6 + g % 2][:]))
                    else:
                        col = t32[:, 0:8]
                        step(dve.reciprocal(col, den[:, HEADS * g:HEADS * (g + 1)]))
                        step(dve.tensor_tensor(col, col, gts[:, tb, :, 1 + g % 2], ALU.mult))
                        ocop(dve.tensor_tensor(heads_of(m.tmp[:, 0, :]), heads_of(ps[6 + g % 2][:]), by_head(col),
                                               ALU.mult))
                        step(dve.tensor_tensor(o_nsa[:, tb, :], o_nsa[:, tb, :], m.tmp[:, 0, :], ALU.add))
                    if kind != "slc":
                        dve.sem_inc(o_ready, 1)
                finish_at = {min(turn_step[4 * g + 3] + 2, STEPS - 1): g for g in range(GROUPS)}
                for s in range(STEPS):
                    if s < PAIRS:
                        (maxima if 2 * s < SOFT else products_of)(s)
                    if s in finish_at:
                        finish(finish_at[s])
                for g in range(2 * NT):
                    tb = g % NT
                    dve.wait_ge(feat_turned, g + 1)
                    src = ps[g % 2][:].rearrange("p (c t) -> p c t", c=4)
                    c0 = 0 if g < NT else 4
                    ts_ = slice(tb * P, (tb + 1) * P)
                    step(dve.tensor_copy(m.hh[:, c0:c0 + 4, ts_], src))
                    fused(dve.tensor_tensor(m.hl[:, c0:c0 + 4, ts_], src, m.hh[:, c0:c0 + 4, ts_].bitcast(F32),
                                            ALU.subtract))

    def merge2(s):
        with phase(nc, "bank_free", "order", "sum_ready", "head_written") as \
                (block, bank_free, order, sum_ready, head_written):

            @block.sync
            def _(sp):
                s.loads(sp, 0, PROJ + RING)

            @block.gpsimd
            def _(pool):
                s.rests(pool, 0, PROJ + 2)

            @block.tensor
            def _(pe):
                for t in range(PROJ):
                    s.ready(pe, t // RING, t % RING)
                    for half in range(2):
                        n = 2 * t + half
                        if n >= 4:
                            pe.wait_ge(bank_free, n - 3)
                        for k in range(4):
                            wc = slice(k * 256 + half * P, k * 256 + half * P + P)
                            xk = k + 4 * (t // 4)
                            last = three_pass(pe, ps[n % 4][:], m.wh[:, t % 2, wc], m.wl[:, t % 2, wc],
                                              m.hh[:, xk, :], m.hl[:, xk, :], start=(k == 0), stop=(k == 3))
                    last.then_inc(s.slot_done, 1)

            @block.scalar
            def _(act):
                s.heads(act, 0, PROJ + 2)
                act.wait_ge(s.slot_done, PROJ)
                for k in range(KD):
                    act.wait_ge(sum_ready, k + 1)
                    act.activation(m.hh[:, k, :], m.y[:, k, :], ACT.Copy).then_inc(head_written, 1)

            @block.vector
            def _(dve):
                step = Signal(dve, order)
                for n in range(2 * KD):
                    dve.wait_ge(s.slot_done, n // 2 + 1)
                    dst = m.y[:, n, :] if n < KD else m.tmp[:, 0, :]
                    dve.tensor_tensor(dst, ps[n % 4][:], gm[:, n, :], ALU.mult).then_inc(bank_free, 1)
                    if n >= KD:
                        dve.wait_ge(bank_free, n + 1)
                        dve.tensor_tensor(m.y[:, n - KD, :], m.y[:, n - KD, :], m.tmp[:, 0, :], ALU.add)\
                           .then_inc(sum_ready, 1)
                        dve.wait_ge(sum_ready, n - KD + 1)
                for k in range(KD):
                    dve.wait_ge(head_written, k + 1)
                    dve.tensor_tensor(m.hl[:, k, :], m.y[:, k, :], m.hh[:, k, :].bitcast(F32), ALU.subtract)


    return locals()


def program(nc, a, out):
    env = build(nc, a, out)
    m, junction = env["m"], env["junction"]

    def col(at):
        return m.pc[:, at:at + KD]

    def mod(i):
        return m.mod[:, KD * i:KD * (i + 1)]
    env["rope_tables"]("pos1")
    run, ff_run = env["run"], env["ff_run"]
    with nc.Fori(0, LAYERS) as l:
        w, at = a["w1"], l * SL1
        env["modulation"](a["wmod"], l * 48, a["pcA"][l])
        ins = run(w, at, IN1)
        junction("a", pre=(col(A_PRE), mod(1), mod(0)), ahead=ins)
        env["in_products1"](ins, a["wmod"], l * 48)
        env["mixer1"]()
        env["product_out"](run(w, at + IN1, OUT), 0, 1, KD, m.hh, m.hl, started=False)
        ff = ff_run(w, at + IN1 + OUT)
        junction("b", post=(col(A_POST), mod(2)), pre=(col(A_FPRE), mod(4), mod(3)), ahead=ff)
        env["feed_forward"]("a", ff, False)
        junction("c", post=(col(A_FPOST), mod(5)))
    env["rope_tables"]("pos2")
    with nc.Fori(0, LAYERS) as l:
        w, at = a["w2"], l * SL2
        env["params2"](a["pcB"][l])
        ins = run(w, at, IN2)
        junction("d", pre=(col(B_PRE), None, None), ahead=ins)
        env["in_products2"](ins)
        env["mixer2"]()
        outs = run(w, at + IN2, PROJ + OUT)
        env["merge2"](outs)
        env["product_out"](outs, PROJ, 1, KD, m.hh, m.hl)
        ff = ff_run(w, at + IN2 + PROJ + OUT)
        junction("e", post=(col(B_POST), None), pre=(col(B_FPRE), None, None), ahead=ff)
        env["feed_forward"]("d", ff, True)
        junction("f", post=(col(B_FPOST), None))
    with phase(nc, "stored") as (block, stored):
        @block.sync
        def _(sp):
            sp.dma_start(out, m.x[:]).then_inc(stored, 16)
            sp.wait_ge(stored, 16)


def _cols(v, n=None):
    return np.asarray(v).reshape(-1, P).T


def _feature(w, n0, n=P):
    k = w.shape[0] // P
    return w[:, n0:n0 + P].reshape(k, P, P).transpose(1, 0, 2).reshape(P, k * P)


def _token(w):
    return [w[256 * j:256 * j + 256].reshape(2, P, T).transpose(1, 0, 2).reshape(P, SLOT) for j in range(4)]


def _place(cols, at, width, dtype):
    out = np.zeros((cols[0].shape[0], width), dtype)
    for c, o in zip(cols, at):
        out[:, o:o + c.shape[1]] = c
    return out


def _down(w):
    out = []
    for nb in range(KD):
        for part in range(3):
            k0, k1 = 8 * part, min(8 * part + 8, KF)
            s = np.zeros((P, SLOT), w.dtype)
            s[:, :(k1 - k0) * P] = _feature(w[k0 * P:k1 * P], nb * P)
            out.append(s)
    return out


def _gate_up(w):
    out = []
    for mblk in range(KF):
        out += [_feature(w, mblk * P), _feature(w, FF + mblk * P)]
    return out


def _constants():
    c = np.zeros((P, C_COLS), np.float32)
    c[:, C_ID:C_ID + P] = np.eye(P)
    for p in range(P):
        if p % 64 < 32:
            c[p + 32, C_ROT + p] = -1.0
        else:
            c[p - 32, C_ROT + p] = 1.0
    q, k = np.arange(P)[:, None], np.arange(P)[None, :]
    c[:, C_CAUSAL + 3 * P:C_CAUSAL + T] = np.where(k > q, NEG, 0.0)
    c[:, C_ONES:C_ONES + P] = 1.0
    for h in range(MH):
        c[h, C_SEL + h * P:C_SEL + (h + 1) * P] = 1.0
    half = np.float32(10000.0) ** (-np.arange(32, dtype=np.float32) / np.float32(32))
    c[:, C_FREQ] = half[np.arange(P) % 32]
    for tb in range(NT):
        t = tb * P + np.arange(P)[:, None]
        n = np.arange(32)[None, :]
        c[:, C_CMP + 32 * tb:C_CMP + 32 * tb + 32] = (n * 16 + 31 <= t) & (n < NCMP)
    return c


def _layout(i):
    f = np.float32
    a = {"x": i["x"][0].T.reshape(KD, P, T).transpose(1, 0, 2), "cst": _constants(), "c": i["c"],
         "pos1": i["positions"], "pos2": i["positions_2"]}
    a["wmod"] = np.concatenate([i["w_mod"][l].T.reshape(48, P, D) for l in range(LAYERS)])
    w1, pa, w2, pb = [], [], [], []
    for l in range(LAYERS):
        w = i["w_in"][l]
        o = np.cumsum([0, 256, 512, 512, 64, 8, 512, 512, 512, 512, 4, 4])
        s = [_feature(w, 128 * c) for c in range(2)] + [_feature(w, o[1] + 128 * c) for c in range(4)]
        kid = w[:, o[3]:o[4]]
        s.append(_feature(np.concatenate([kid, kid], 1), 0))
        s.append(_feature(_place([w[:, o[4]:o[5]], w[:, o[9]:o[10]], w[:, o[10]:o[11]]], [0, 32, 64], P, f), 0))
        s += [_feature(w, o[5] + 128 * c) for c in range(8)]
        s += [_feature(w, o[8] + 128 * c) for c in range(4)]
        s += _token(w[:, o[2]:o[3]]) + _token(w[:, o[7]:o[8]])
        for up in (i["w_q_up"][l], i["w_qidx_up"][l]):
            s.append(up.reshape(2, P, T).transpose(1, 0, 2).reshape(P, SLOT))
        s += [_feature(i["w_out"][l], 128 * c) for c in range(KD)]
        s += _gate_up(i["w_gate_up"][l]) + _down(i["w_down"][l])
        assert len(s) == SL1
        w1 += s
        pc = np.zeros((P, A_COLS), f)
        for at, v in ((A_PRE, "mix_norm_pre"), (A_POST, "mix_norm_post"), (A_FPRE, "ffn_norm_pre"),
                      (A_FPOST, "ffn_norm_post"), (A_BMOD, "b_mod"), (A_QN, "q_latent_norm"), (A_CW, "conv_w"),
                      (A_CB, "conv_b"), (A_AN, "attn_out_norm"), (A_MN, "mlstm_out_norm")):
            v = _cols(i[v][l])
            pc[:, at:at + v.shape[1]] = v
        pc[:MH, A_BI], pc[:MH, A_BF] = i["b_igate"][l], i["b_fgate"][l]
        pa.append(pc)

        w = i["w_in_2"][l]
        o = np.cumsum([0, 512, 768, 24, 1536, 2048])
        heads = [w[:, 64 * h:64 * h + 64] for h in range(HEADS)]
        q = np.concatenate([heads[h] for pair in range(4) for h in (pair, 4 + pair)], 1)
        kv = [w[:, o[1] + 128 * c:o[1] + 128 * c + 128] for c in range(6)]
        s = [_feature(q, 128 * c) for c in range(4)]
        s += [_feature(kv[c], 0) for c in (0, 1, 2, 4)]
        s += _token(_place([kv[3], kv[5], w[:, o[2]:o[3]]], [0, 128, 256], T, f))
        s += [_feature(w, o[3] + 128 * c) for c in range(8)]
        s += _token(w[:, o[3] + 1024:o[4]])
        for w1_ in (i["ck_w1_2"][l], i["cv_w1_2"][l]):
            bd = np.zeros((P, CB, P), f)
            for h in range(2):
                bd[64 * h:64 * h + 64, :, 64 * h:64 * h + 64] = w1_.reshape(CB, HD, HD).transpose(1, 0, 2)
            s += [bd[:, 8 * j:8 * j + 8].reshape(P, SLOT) for j in range(4)]
        s += [_feature(w, o[4] + 128 * c) for c in range(16)]
        for wp in (i["w_proj_nsa_2"][l], i["w_proj_sb_2"][l]):
            s += [wp[:, 256 * j:256 * j + 256].reshape(4, P, 256).transpose(1, 0, 2).reshape(P, SLOT)
                  for j in range(4)]
        s += [_feature(i["w_out_2"][l], 128 * c) for c in range(KD)]
        s += _gate_up(i["w_up_2"][l]) + _down(i["w_down_2"][l])
        assert len(s) == SL2, (len(s), SL2)
        w2 += s
        pc = np.zeros((P, B_COLS), f)
        for at, v in ((B_PRE, "g_pre_mix_2"), (B_POST, "g_post_mix_2"), (B_FPRE, "g_pre_ffn_2"),
                      (B_FPOST, "g_post_ffn_2"), (B_CW, "conv_w_2"), (B_CB, "conv_b_2")):
            v = _cols(i[v][l])
            pc[:, at:at + v.shape[1]] = v
        for h in range(2):
            r = slice(64 * h, 64 * h + 64)
            pc[r, B_B1K], pc[r, B_B1V] = i["ck_b1_2"][l], i["cv_b1_2"][l]
            pc[r, B_PEK:B_PEK + CB], pc[r, B_PEV:B_PEV + CB] = i["ck_pe_2"][l].T, i["cv_pe_2"][l].T
            pc[r, B_W2K + 64 * h:B_W2K + 64 * h + 64] = i["ck_w2_2"][l]
            pc[r, B_W2V + 64 * h:B_W2V + 64 * h + 64] = i["cv_w2_2"][l]
        pb.append(pc)
    a["w1"], a["w2"], a["pcA"], a["pcB"] = np.stack(w1), np.stack(w2), np.stack(pa), np.stack(pb)
    return {k: np.ascontiguousarray(v) for k, v in a.items()}


def kernel(**inputs):
    import concourse.bacc as bacc
    from concourse.bass_utils import run_bass_kernel_spmd

    nc = bacc.Bacc("TRN2", target_bir_lowering=False, num_devices=1)
    arrays = _layout({k: np.asarray(v) for k, v in inputs.items()})
    a = {k: nc.dram_tensor(f"in_{k}", v.shape, mybir.dt.from_np(v.dtype), kind="ExternalInput").ap()
         for k, v in arrays.items()}
    out = nc.dram_tensor("out_xT", (P, KD, T), F32, kind="ExternalOutput").ap()
    program(nc, a, out)
    r = run_bass_kernel_spmd(nc, [{f"in_{k}": v for k, v in arrays.items()}], core_ids=[0])
    got = r.results[0]["out_xT"]
    return got.transpose(2, 1, 0).reshape(1, T, D)
```
